# Optimizing a Trainium2 kernel written in Bass

```python
import jax
import jax.numpy as jnp
from jax import lax
import numpy as np

D_MODEL = 1024
BATCH = 1
SEQ = 256
DEPTH = 2

ATTN_HEADS = 8
HEAD_DIM = 64
ATTN_WIDTH = ATTN_HEADS * HEAD_DIM
IDX_HEADS = 8
IDX_DIM = 64
INDEX_TOPK = 256
Q_BLOCK = 128
ROPE_THETA = 10000.0
CONV_WIDTH = D_MODEL - ATTN_WIDTH
CONV_K = 3
HYB_SIZES = (ATTN_WIDTH, HEAD_DIM, HEAD_DIM, IDX_HEADS * IDX_DIM, IDX_DIM, IDX_HEADS, CONV_WIDTH, CONV_WIDTH, CONV_WIDTH)
HYB_IN = sum(HYB_SIZES)

ML_HEADS = 8
ML_QK_DIM = D_MODEL // (2 * ML_HEADS)
ML_V_DIM = D_MODEL // ML_HEADS
ML_CHUNK = 64
ML_SIZES = (ML_HEADS * ML_QK_DIM, ML_HEADS * ML_QK_DIM, ML_HEADS * ML_V_DIM, ML_HEADS, ML_HEADS, ML_HEADS * ML_V_DIM)
ML_IN = sum(ML_SIZES)

N_GROUPS = 4
EXPERTS_PER_GROUP = 8
N_EXPERTS = N_GROUPS * EXPERTS_PER_GROUP
TOP_K = 2
D_EXPERT = 512
MOE_BLOCK = 256
NORM_EPS = 1e-6

kernel_name = 'hybrid_dsa_conv_mlstm_hmoe'

def _split(a, sizes):
    return jnp.split(a, [int(i) for i in np.cumsum(sizes)[:-1]], axis=-1)

def rms_norm(x, g):
    xf = x.astype(jnp.float32)
    y = xf * lax.rsqrt(jnp.mean(xf * xf, axis=-1, keepdims=True) + NORM_EPS)
    return (y * g.astype(jnp.float32)).astype(x.dtype)

def rope_tables(seq, dim):
    inv = 1.0 / (ROPE_THETA ** (jnp.arange(0, dim, 2, dtype=jnp.float32) / dim))
    ang = jnp.arange(seq, dtype=jnp.float32)[:, None] * inv[None, :]
    return jnp.cos(ang), jnp.sin(ang)

def apply_rope(x, cos, sin):
    half = x.shape[-1] // 2
    xf = x.astype(jnp.float32)
    x1, x2 = xf[..., :half], xf[..., half:]
    c = cos[None, :, None, :]
    s = sin[None, :, None, :]
    return jnp.concatenate([x1 * c - x2 * s, x2 * c + x1 * s], axis=-1).astype(x.dtype)

def dsa_attention(q, k, v, iq, ik, iw):
    B, S, H, d = q.shape
    nb = S // Q_BLOCK
    k_sel = min(INDEX_TOPK, S // 4)
    pos = jnp.arange(S, dtype=jnp.int32)
    ikf = ik.astype(jnp.float32)
    gather = jax.vmap(lambda a, i: a[i])

    def to_blocks(a):
        return jnp.moveaxis(a.reshape((B, nb, Q_BLOCK) + a.shape[2:]), 1, 0)

    def block(args):
        qb, iqb, iwb, pb = args
        s = jnp.einsum('bqhd,bsd->bqhs', iqb.astype(jnp.float32), ikf) * (IDX_DIM ** -0.5)
        score = jnp.einsum('bqhs,bqh->bqs', jax.nn.relu(s), iwb.astype(jnp.float32) * (IDX_HEADS ** -0.5))
        score = jnp.where((pos[None, :] <= pb[:, None])[None], score, -jnp.inf)
        top_val, top_idx = lax.top_k(score, k_sel)
        valid = jnp.isfinite(top_val)
        kg = gather(k, top_idx)
        vg = gather(v, top_idx)
        logits = jnp.einsum('bqhd,bqkd->bqhk', qb, kg).astype(jnp.float32) * (d ** -0.5)
        logits = jnp.where(valid[:, :, None, :], logits, -jnp.inf)
        p = jax.nn.softmax(logits, axis=-1).astype(vg.dtype)
        return jnp.einsum('bqhk,bqkd->bqhd', p, vg)

    out = lax.map(block, (to_blocks(q), to_blocks(iq), to_blocks(iw), pos.reshape(nb, Q_BLOCK)))
    return jnp.moveaxis(out, 0, 1).reshape(B, S, H * d)

def short_gated_conv(bg, cg, u, conv_w):
    S = u.shape[1]
    z = cg * u
    zp = jnp.pad(z, ((0, 0), (CONV_K - 1, 0), (0, 0)))
    y = zp[:, 0:S] * conv_w[0]
    for j in range(1, CONV_K):
        y = y + zp[:, j:j + S] * conv_w[j]
    return bg * y

def hybrid_mixer(h, w_in, q_norm, k_norm, conv_w, w_out, cos, sin):
    B, S, _ = h.shape
    q, k, v, iq, ik, iw, bg, cg, u = _split(h @ w_in, HYB_SIZES)
    q = apply_rope(rms_norm(q.reshape(B, S, ATTN_HEADS, HEAD_DIM), q_norm), cos, sin)
    k = apply_rope(rms_norm(k.reshape(B, S, 1, HEAD_DIM), k_norm), cos, sin)[:, :, 0]
    iq = apply_rope(iq.reshape(B, S, IDX_HEADS, IDX_DIM), cos, sin)
    ik = apply_rope(ik.reshape(B, S, 1, IDX_DIM), cos, sin)[:, :, 0]
    y_attn = dsa_attention(q, k, v, iq, ik, iw)
    y_conv = short_gated_conv(bg, cg, u, conv_w)
    return jnp.concatenate([y_attn, y_conv], axis=-1) @ w_out

def mlstm_chunkwise(q, k, v, i_pre, f_pre):
    B, H, S, dk = q.shape
    dv = v.shape[-1]
    nc = S // ML_CHUNK
    log_f = jax.nn.log_sigmoid(f_pre)
    tril = jnp.tril(jnp.ones((ML_CHUNK, ML_CHUNK), dtype=bool))

    def chunks(a):
        return jnp.moveaxis(a.reshape(a.shape[:2] + (nc, ML_CHUNK) + a.shape[3:]), 2, 0)

    def step(carry, inp):
        C, n, m = carry
        qc, kc, vc, ic, lfc = inp
        b = jnp.cumsum(lfc, axis=-1)
        dmat = b[..., :, None] - b[..., None, :] + ic[..., None, :]
        dmat = jnp.where(tril, dmat, -jnp.inf)
        inter = b + m[..., None]
        m_t = jnp.maximum(inter, jnp.max(dmat, axis=-1))
        w_intra = jnp.exp(dmat - m_t[..., None])
        w_inter = jnp.exp(inter - m_t)
        intra = w_intra * jnp.einsum('bhtd,bhsd->bhts', qc, kc)
        num = w_inter[..., None] * jnp.einsum('bhvd,bhtd->bhtv', C, qc) + jnp.einsum('bhts,bhsv->bhtv', intra, vc)
        den = w_inter * jnp.einsum('bhd,bhtd->bht', n, qc) + jnp.sum(intra, axis=-1)
        hc = num / jnp.maximum(jnp.abs(den), jnp.exp(-m_t))[..., None]
        b_last = b[..., -1]
        g = b_last[..., None] - b + ic
        m_new = jnp.maximum(b_last + m, jnp.max(g, axis=-1))
        decay = jnp.exp(b_last + m - m_new)
        ws = jnp.exp(g - m_new[..., None])
        C_new = decay[..., None, None] * C + jnp.einsum('bhsv,bhsd->bhvd', vc * ws[..., None], kc)
        n_new = decay[..., None] * n + jnp.einsum('bhs,bhsd->bhd', ws, kc)
        return (C_new, n_new, m_new), hc

    init = (jnp.zeros((B, H, dv, dk), jnp.float32), jnp.zeros((B, H, dk), jnp.float32), jnp.zeros((B, H), jnp.float32))
    _, hs = lax.scan(step, init, (chunks(q), chunks(k), chunks(v), chunks(i_pre), chunks(log_f)))
    return jnp.moveaxis(hs, 0, 2).reshape(B, H, S, dv)

def mlstm_mixer(h, w_in, b_gates, out_norm, w_out):
    B, S, _ = h.shape
    q, k, v, ig, fg, og = _split(h @ w_in, ML_SIZES)

    def heads(a, d):
        return jnp.transpose(a.reshape(B, S, ML_HEADS, d), (0, 2, 1, 3)).astype(jnp.float32)

    qh = heads(q, ML_QK_DIM) * (ML_QK_DIM ** -0.5)
    kh = heads(k, ML_QK_DIM)
    vh = heads(v, ML_V_DIM)
    i_pre = jnp.transpose((ig + b_gates[:ML_HEADS]).astype(jnp.float32), (0, 2, 1))
    f_pre = jnp.transpose((fg + b_gates[ML_HEADS:]).astype(jnp.float32), (0, 2, 1))
    hh = jnp.transpose(mlstm_chunkwise(qh, kh, vh, i_pre, f_pre), (0, 2, 1, 3))
    hh = rms_norm(hh, out_norm.reshape(ML_HEADS, ML_V_DIM)).astype(h.dtype).reshape(B, S, ML_HEADS * ML_V_DIM)
    return (jax.nn.sigmoid(og) * hh) @ w_out

def hier_moe(h, w_group, b_group, w_expert, b_expert, w_gate, w_up, w_down):
    B, S, D = h.shape
    T = B * S
    xt = h.reshape(T, D)
    p_group = jax.nn.softmax((xt @ w_group + b_group).astype(jnp.float32), axis=-1)
    g_sel = jnp.argmax(p_group, axis=-1)
    pg = jnp.take_along_axis(p_group, g_sel[:, None], axis=-1)
    e_logits = (xt @ w_expert + b_expert).astype(jnp.float32).reshape(T, N_GROUPS, EXPERTS_PER_GROUP)
    in_group = jnp.take_along_axis(e_logits, g_sel[:, None, None], axis=1)[:, 0]
    top_val, top_idx = lax.top_k(in_group, TOP_K)
    weight = pg * jax.nn.softmax(top_val, axis=-1)
    expert_id = g_sel[:, None].astype(jnp.int32) * EXPERTS_PER_GROUP + top_idx.astype(jnp.int32)
    A = T * TOP_K
    flat_e = expert_id.reshape(A)
    flat_tok = jnp.repeat(jnp.arange(T, dtype=jnp.int32), TOP_K)
    flat_w = weight.reshape(A)
    order = jnp.argsort(flat_e)
    sorted_e = flat_e[order]
    counts = jnp.bincount(flat_e, length=N_EXPERTS)
    blocks_per = (counts + MOE_BLOCK - 1) // MOE_BLOCK
    block_end = jnp.cumsum(blocks_per)
    block_start = block_end - blocks_per
    seg_start = jnp.cumsum(counts) - counts
    rank = jnp.arange(A, dtype=jnp.int32) - seg_start[sorted_e]
    dest = block_start[sorted_e] * MOE_BLOCK + rank
    n_blk = -(-A // MOE_BLOCK) + N_EXPERTS
    R = n_blk * MOE_BLOCK
    row_tok = jnp.zeros((R,), jnp.int32).at[dest].set(flat_tok[order])
    row_w = jnp.zeros((R,), h.dtype).at[dest].set(flat_w[order].astype(h.dtype))
    blk_e = jnp.clip(jnp.searchsorted(block_end, jnp.arange(n_blk), side='right'), 0, N_EXPERTS - 1)
    xs = xt[row_tok].reshape(n_blk, MOE_BLOCK, D)

    def run(args):
        xb, e = args
        return (jax.nn.silu(xb @ w_gate[e]) * (xb @ w_up[e])) @ w_down[e]

    ys = lax.map(run, (xs, blk_e)).reshape(R, D) * row_w[:, None]
    out = jnp.zeros((T, D), h.dtype).at[row_tok].add(ys)
    return out.reshape(B, S, D)

def setup_inputs(seed: int = 0) -> dict:
    key = jax.random.key(seed)
    ks = jax.random.split(key, 24)
    n_even = (DEPTH + 1) // 2
    n_odd = DEPTH // 2
    D = D_MODEL

    def nrm(k, shape, scale):
        return jax.random.normal(k, shape, jnp.float32) * scale

    f_bias = jnp.linspace(3.0, 6.0, ML_HEADS, dtype=jnp.float32)[None, :] + nrm(ks[12], (n_odd, ML_HEADS), 0.1)
    return {
        'x': nrm(ks[0], (BATCH, SEQ, D), 1.0),
        'c': nrm(ks[1], (BATCH, D), 1.0),
        'ada_w': nrm(ks[2], (DEPTH, D, 6 * D), 0.5 * D ** -0.5),
        'ada_b': nrm(ks[3], (DEPTH, 6 * D), 0.02),
        'norm_mix': 1.0 + nrm(ks[4], (DEPTH, D), 0.05),
        'norm_ffn': 1.0 + nrm(ks[5], (DEPTH, D), 0.05),
        'hy_w_in': nrm(ks[6], (n_even, D, HYB_IN), D ** -0.5),
        'hy_q_norm': 1.0 + nrm(ks[7], (n_even, HEAD_DIM), 0.05),
        'hy_k_norm': 1.0 + nrm(ks[8], (n_even, HEAD_DIM), 0.05),
        'hy_conv_w': nrm(ks[9], (n_even, CONV_K, CONV_WIDTH), CONV_K ** -0.5),
        'hy_w_out': nrm(ks[10], (n_even, D, D), D ** -0.5),
        'ml_w_in': nrm(ks[11], (n_odd, D, ML_IN), D ** -0.5),
        'ml_b_gates': jnp.concatenate([nrm(ks[13], (n_odd, ML_HEADS), 0.1), f_bias], axis=-1),
        'ml_out_norm': 1.0 + nrm(ks[14], (n_odd, ML_HEADS * ML_V_DIM), 0.05),
        'ml_w_out': nrm(ks[15], (n_odd, ML_HEADS * ML_V_DIM, D), (ML_HEADS * ML_V_DIM) ** -0.5),
        'moe_w_group': nrm(ks[16], (DEPTH, D, N_GROUPS), D ** -0.5),
        'moe_b_group': nrm(ks[17], (DEPTH, N_GROUPS), 0.01),
        'moe_w_expert': nrm(ks[18], (DEPTH, D, N_EXPERTS), D ** -0.5),
        'moe_b_expert': nrm(ks[19], (DEPTH, N_EXPERTS), 0.01),
        'moe_w_gate': nrm(ks[20], (DEPTH, N_EXPERTS, D, D_EXPERT), D ** -0.5),
        'moe_w_up': nrm(ks[21], (DEPTH, N_EXPERTS, D, D_EXPERT), D ** -0.5),
        'moe_w_down': nrm(ks[22], (DEPTH, N_EXPERTS, D_EXPERT, D), D_EXPERT ** -0.5),
    }

def reference(x, c, ada_w, ada_b, norm_mix, norm_ffn, hy_w_in, hy_q_norm, hy_k_norm, hy_conv_w, hy_w_out,
              ml_w_in, ml_b_gates, ml_out_norm, ml_w_out, moe_w_group, moe_b_group, moe_w_expert, moe_b_expert,
              moe_w_gate, moe_w_up, moe_w_down):
    S = x.shape[1]
    cos, sin = rope_tables(S, HEAD_DIM)
    c_act = jax.nn.silu(c)
    for l in range(DEPTH):
        mod = c_act @ ada_w[l] + ada_b[l]
        sh1, sc1, g1, sh2, sc2, g2 = [m[:, None, :] for m in jnp.split(mod, 6, axis=-1)]
        h = rms_norm(x, norm_mix[l]) * (1 + sc1) + sh1
        j = l // 2
        if l % 2 == 0:
            y = hybrid_mixer(h, hy_w_in[j], hy_q_norm[j], hy_k_norm[j], hy_conv_w[j], hy_w_out[j], cos, sin)
        else:
            y = mlstm_mixer(h, ml_w_in[j], ml_b_gates[j], ml_out_norm[j], ml_w_out[j])
        x = x + g1 * y
        h = rms_norm(x, norm_ffn[l]) * (1 + sc2) + sh2
        x = x + g2 * hier_moe(h, moe_w_group[l], moe_b_group[l], moe_w_expert[l], moe_b_expert[l],
                              moe_w_gate[l], moe_w_up[l], moe_w_down[l])
    return x


_drawn_inputs = setup_inputs


def setup_inputs(seed=0):
    import zlib

    import numpy as np

    out = dict(_drawn_inputs(seed))
    spreads = {}
    factors = {'hy_q_norm': 8.0,
     'hy_k_norm': 8.0,
     'ml_out_norm': 5.214,
     'moe_b_group': 30.845,
     'moe_b_expert': 18.554}
    for name, (base, spread) in spreads.items():
        noise = np.random.default_rng([zlib.crc32(name.encode()), seed]).standard_normal(out[name].shape)
        drawn = base * np.exp(spread * noise) if base else spread * noise
        out[name] = jnp.asarray(drawn.astype(out[name].dtype))
    for name, factor in factors.items():
        out[name] = (out[name] * factor).astype(out[name].dtype)
    return out
```

```python
from contextlib import ExitStack

import concourse.bass as bass
from concourse import mybir

F32 = mybir.dt.float32
I32 = mybir.dt.int32
ALU = mybir.AluOpType
ACT = mybir.ActivationFunctionType
AX = mybir.AxisListType.X

P = 128
SEQ = 256
NT = SEQ // P
D = 1024
KC = D // P
DEPTH = 2
HEADS = 8
HD = 64
TOPK = SEQ // 4
CONV = 512
VD = D // HEADS
NG, NE = 4, 32
EG = NE // NG
DE = 512
FC = DE // P
BLK = 32
EPS = 1e-6
MASKED = -1.0e30
TAKEN = -3.0e38
SLOT = 4096
NS = 6
UNROLL = 2

C_IDENT, C_ONES, C_MEAN32, C_FOLD, C_LE, C_LT = 0, 128, 256, 384, 416, 544
C_CAUSAL, C_MASKT, C_IOTA, C_IDXM, C_THR, C_PMOD, C_ROPE = 672, 800, 928, 960, 992, 1000, 1002
NCONST = C_ROPE + NT * 2 * (HD // 2)


def constant_table():
    import numpy as np
    t = np.zeros((P, NCONST), np.float32)
    p = np.arange(P)[:, None]
    f = np.arange(P)[None, :]
    t[:, C_IDENT:C_IDENT + P] = p == f
    t[:, C_ONES:C_ONES + P] = 1.0
    t[:, C_MEAN32:C_MEAN32 + P] = 1.0 / BLK
    t[:, C_FOLD:C_FOLD + BLK] = (p % BLK) == np.arange(BLK)[None, :]
    t[:, C_LE:C_LE + P] = p <= f
    t[:, C_LT:C_LT + P] = p < f
    t[:, C_CAUSAL:C_CAUSAL + P] = np.where(f <= p, 0.0, MASKED)
    t[:, C_MASKT:C_MASKT + P] = np.where(p <= f, 0.0, MASKED)
    t[:, C_IOTA:C_IOTA + BLK] = np.arange(BLK)[None, :]
    t[:, C_IDXM:C_IDXM + NE] = np.arange(NE)[None, :] - 99.0
    t[:, C_THR:C_THR + 8] = BLK * np.arange(1, 9)[None, :]
    t[:, C_PMOD] = (np.arange(P) % BLK)
    t[:, C_PMOD + 1] = EPS
    inv = (np.float32(1.0) / np.power(np.float32(10000.0), np.arange(0, HD, 2, dtype=np.float32) / np.float32(HD))).astype(np.float32)
    ang = (np.arange(SEQ, dtype=np.float32)[:, None] * inv[None, :]).astype(np.float32)
    rope = np.stack([np.cos(ang), np.sin(ang)], 1).astype(np.float32)
    t[:, C_ROPE:] = rope.reshape(NT, P, 2 * (HD // 2)).transpose(1, 0, 2).reshape(P, -1)
    return t


def weight_stream():
    ada = [[("ada", l, n, 0) for n in range(12)] for l in range(DEPTH)]
    hy_cols = [(0, 512), (512, 512), (1024, 200), (1224, 512), (1736, 512), (2248, 512)]
    ml_cols = [(0, 512), (512, 512), (1024, 512), (1536, 512), (2048, 16), (2064, 512), (2576, 512)]
    out = [[("out", l, n, 0) for n in range(2)] for l in range(DEPTH)]
    s = ada[0][:6] + [("in", 0, a, n) for a, n in hy_cols] + ada[0][6:] + ada[1][:6] + out[0]
    s += [("experts", 0, 0, 0)]
    s += [("in", 1, a, n) for a, n in ml_cols] + ada[1][6:] + out[1]
    s += [("experts", 1, 0, 0)]
    return s


def decoder_kernel(nc, x, c, ada_w, ada_b, norm_mix, norm_ffn, hy_w_in, hy_q_norm, hy_k_norm, hy_conv_w,
                   hy_w_out, ml_w_in, ml_b_gates, ml_out_norm, ml_w_out, moe_w_group, moe_b_group,
                   moe_w_expert, moe_b_expert, moe_w_gate, moe_w_up, moe_w_down, consts, out):
    stream = weight_stream()
    at, n = {}, 0
    for piece in stream:
        at[piece] = n
        n += 3 * NE if piece[0] == "experts" else 1

    with ExitStack() as ctx:
        def sb(name, shape, dt=F32):
            return ctx.enter_context(nc.sbuf_tensor(name, shape, dt))

        def sem(name):
            return ctx.enter_context(nc.semaphore(name))

        bank = [ctx.enter_context(nc.psum_tensor(f"bank{i}", [P, 512], F32)) for i in range(8)]

        ring = [sb(f"ring{i}", [P, SLOT]) for i in range(NS)]
        xs = sb("xs", [P, NT, D])
        hbuf = sb("hbuf", [P, NT, D])
        hTb = sb("hTb", [P, KC * SEQ])
        mod = sb("mod", [P, 9, D])
        gam = sb("gam", [P, D])
        cst = sb("cst", [P, NCONST])
        RA = sb("RA", [P, 2560])
        RB = sb("RB", [P, 2560])
        RC = sb("RC", [P, 2048])
        RD = sb("RD", [P, 3072])
        modp = RD[:, 0:512]
        small = sb("small", [P, 256])
        rw = sb("rw", [P, KC, NG + NE])
        tab = sb("tab", [P, NE + 1], I32)

        hT = hTb[:, :].rearrange("p (k t) -> p k t", k=KC)
        h = hbuf[:, :, :].rearrange("q t (k p) -> q t k p", k=KC)
        ident = cst[:, C_IDENT:C_IDENT + P]
        ones = cst[:, C_ONES:C_ONES + P]
        mean32 = cst[:, C_MEAN32:C_MEAN32 + P]
        fold = cst[:, C_FOLD:C_FOLD + BLK]
        tri_le = cst[:, C_LE:C_LE + P]
        tri_lt = cst[:, C_LT:C_LT + P]
        causal = cst[:, C_CAUSAL:C_CAUSAL + P]
        maskT = cst[:, C_MASKT:C_MASKT + P]
        iota32 = cst[:, C_IOTA:C_IOTA + BLK]
        idxm = cst[:, C_IDXM:C_IDXM + NE]
        eps = cst[:, C_PMOD + 1:C_PMOD + 2]
        rope = cst[:, C_ROPE:NCONST].rearrange("p (t c j) -> p t c j", t=NT, c=2)

        cact = small[:, 0:8]
        ssq = small[:, 8:10]
        rstd = small[:, 10:12]
        brow = sb("brow", [24, 512])
        gam9 = sb("gam9", [P, 9, HD])
        cwT = small[:, 12:24]
        cwr = sb("cwr", [12, P])
        bgate = small[:, 24:40]
        rb = small[:, 40:76]

        slot_full = [sem(f"slot_full{i}") for i in range(NS)]
        slot_used = [sem(f"slot_used{i}") for i in range(NS)]
        x_in = sem("x_in")
        const_in = sem("const_in")
        param_in = sem("param_in")
        gam_in = sem("gam_in")
        gam_free = sem("gam_free")
        rparam_in = sem("rparam_in")
        rparam_free = sem("rparam_free")
        out_done = sem("out_done")
        cact_ready = sem("cact_ready")
        part_done = sem("part_done")
        part_copied = sem("part_copied")
        sum_done = sem("sum_done")
        mod_ready = sem("mod_ready")
        ssq_done = sem("ssq_done")
        std_done = sem("std_done")
        gsc_ready = sem("gsc_ready")
        h_ready = sem("h_ready")
        ht_done = sem("ht_done")
        ht_act = sem("ht_act")
        ht_dve = sem("ht_dve")
        V = sem("dve_step")
        A = sem("act_step")
        proj_done = sem("proj_done")
        proj_act = sem("proj_act")
        proj_dve = sem("proj_dve")
        bg_act = sem("bg_act")
        vone_ready = sem("vone_ready")
        sq_ready = sem("sq_ready")
        qss_ready = sem("qss_ready")
        qstd_ready = sem("qstd_ready")
        q2_ready = sem("q2_ready")
        cwt_done = sem("cwt_done")
        qt_done = sem("qt_done")
        qt_act = sem("qt_act")
        qt_dve = sem("qt_dve")
        score_done = sem("score_done")
        relu_done = sem("relu_done")
        relu_used = sem("relu_used")
        yconv_ready = sem("yconv_ready")
        logit_done = sem("logit_done")
        logit_read = sem("logit_read")
        max_ready = sem("max_ready")
        exp_done = sem("exp_done")
        probs_ready = sem("probs_ready")
        pt_done = sem("pt_done")
        pt_act = sem("pt_act")
        pt_dve = sem("pt_dve")
        pv_done = sem("pv_done")
        yt_act = sem("yt_act")
        yt_dve = sem("yt_dve")
        outp_done = sem("outp_done")
        x_ready = sem("x_ready")
        gates_ready = sem("gates_ready")
        absexp_done = sem("absexp_done")
        logf_ready = sem("logf_ready")
        cumf_done = sem("cumf_done")
        a_ready = sem("a_ready")
        at_done = sem("at_done")
        m_ready = sem("m_ready")
        mb_done = sem("mb_done")
        mbc_dve = sem("mbc_dve")
        mbc_act = sem("mbc_act")
        em_in = sem("em_in")
        em_ready = sem("em_ready")
        w_done = sem("w_done")
        st_done = sem("st_done")
        pw_ready = sem("pw_ready")
        num_done = sem("num_done")
        hn_ready = sem("hn_ready")
        hsq_done = sem("hsq_done")
        hss_ready = sem("hss_ready")
        hstd_done = sem("hstd_done")
        y_ready = sem("y_ready")
        yb_done = sem("yb_done")
        rlog_done = sem("rlog_done")
        gexp_in = sem("gexp_in")
        gexp_done = sem("gexp_done")
        wexp_in = sem("wexp_in")
        wexp_done = sem("wexp_done")
        onehot_ready = sem("onehot_ready")
        rank_done = sem("rank_done")
        table_ready = sem("table_ready")
        diag_ready = sem("diag_ready")
        rows_done = sem("rows_done")
        rows_copied = sem("rows_copied")
        zero_ready = sem("zero_ready")
        acc_done = sem("acc_done")

        def per_layer(name):
            return [sem(f"{name}_{l}") for l in range(DEPTH)]
        sel_ready = per_layer("sel_ready")
        gather_done = per_layer("gather_done")
        xt_ready = per_layer("xt_ready")
        gate_done = per_layer("gate_done")
        up_done = per_layer("up_done")
        hg_ready = per_layer("hg_ready")
        hu_ready = per_layer("hu_ready")
        turn_done = per_layer("turn_done")
        silu_ready = per_layer("silu_ready")
        hid_ready = per_layer("hid_ready")
        down_done = per_layer("down_done")
        y_act = per_layer("y_act")
        y_dve = per_layer("y_dve")
        scat_ready = per_layer("scat_ready")
        selstep = per_layer("selstep")

        def modvec(layer, j):
            k = j if layer == 0 else (6 + j if j < 3 else j - 3)
            return mod[:, k, :]

        patt = RA[:, 0:NT * 1224].rearrange("p (t n) -> p t n", t=NT)
        QT = RA[:, :].rearrange("p (c t) -> p c t", c=10)
        Q2 = RB[:, :].rearrange("p (t g d) -> p t g d", t=NT, g=20)
        qsq = RB[:, 0:NT * 576].rearrange("p (t g d) -> p t g d", t=NT, g=9)
        yT = RC[:, :].rearrange("p (c t) -> p c t", c=8)
        vv = RD[:, 512:512 + NT * 72].rearrange("p (t n) -> p t n", t=NT)
        relu = [RD[:, 768 + 512 * i:1280 + 512 * i] for i in range(2)]
        score = RD[:, 1792:2048]
        work = RD[:, 2048:2304]
        selb = RD[:, 2304:2816].rearrange("p (t s) -> p t s", t=NT)
        cgs = hbuf[:, 0, :].rearrange("p (c t) -> p c t", c=4)
        ctmp = hbuf[:, 1, :].rearrange("p (c t) -> p c t", c=4)
        logits = hTb[:, :].rearrange("p (h s) -> p h s", h=HEADS)
        PT = hbuf[:, :, :].rearrange("p k (h q) -> p k h q", h=HEADS)
        amax = small[:, 76:84]
        asum = small[:, 84:92]
        rsum = small[:, 92:100]
        qss = small[:, 100:118]
        qrs = small[:, 118:136]
        top8 = small[:, 136:144]
        wsc = small[:, 144:160].rearrange("p (t n) -> p t n", t=NT)
        otmp = RD[:, 2560:3072]

        qkT = RA[:, 0:2048].rearrange("p (c t) -> p c t", c=8)
        vx = RB[:, 0:NT * HEADS * (VD + 1)].rearrange("p (t h v) -> p t h v", t=NT, h=HEADS)
        ogs = hbuf
        MB0 = RD[:, 0:2048].rearrange("p (h t) -> p h t", h=HEADS)
        MB1 = RD[:, 2048:3072].rearrange("p (h t) -> p h t", h=HEADS)
        HN = hTb[:, :].rearrange("p (t h v) -> p t h v", t=NT, h=HEADS)
        hsq = RA[:, 0:2048].rearrange("p (t h v) -> p t h v", t=NT, h=HEADS)
        gts = small[:, 76:108].rearrange("p (t n) -> p t n", t=NT)
        g3 = small[:, 108:124].rearrange("p (t n) -> p t n", t=NT)
        lf = small[:, 124:140].rearrange("p (t n) -> p t n", t=NT)
        cumf = small[:, 140:156].rearrange("p (t n) -> p t n", t=NT)
        asb = small[:, 156:172].rearrange("p (t n) -> p t n", t=NT)
        mrow = sb("mrow", [HEADS, 2, SEQ])
        em = small[:, 172:188].rearrange("p (t n) -> p t n", t=NT)
        den = small[:, 188:204].rearrange("p (t n) -> p t n", t=NT)
        hss = small[:, 204:220].rearrange("p (t n) -> p t n", t=NT)

        XT = RA[:, 0:KC * BLK].rearrange("p (k s) -> p k s", k=KC)
        HG = RA[:, 256:768]
        HU = RA[:, 768:1280]
        SIL = RA[:, 1280:1408].rearrange("p (f s) -> p f s", f=FC)
        HID = RA[:, 1408:1536].rearrange("p (f s) -> p f s", f=FC)
        SC = RA[:, 1536:1792]
        SCT = RA[:, 1792:2048]
        SEL = RA[:, 2048:2112].rearrange("p (t s) -> p t s", t=NT)
        SELQ = RA[:, 2112:2240].rearrange("p (c s) -> p c s", c=4)
        Y = RB[:, 0:1024]
        posrow = RB[:, 1024:1536].rearrange("p (c t) -> p c t", c=2)
        wrow = RB[:, 1536:2048].rearrange("p (c t) -> p c t", c=2)
        DG = RC[:, 0:1024].rearrange("p (r t) -> p r t", r=8)
        LG = RD[:, 0:72].rearrange("p (t n) -> p t n", t=NT)
        R1 = RD[:, 72:136].rearrange("p (t n) -> p t n", t=NT)
        R2 = RD[:, 136:200].rearrange("p (t n) -> p t n", t=NT)
        O1 = RD[:, 200:264].rearrange("p (t n) -> p t n", t=NT)
        O2 = RD[:, 264:328].rearrange("p (t n) -> p t n", t=NT)
        OS = RD[:, 328:392].rearrange("p (t n) -> p t n", t=NT)
        CMP = RD[:, 392:392 + NE * 7].rearrange("p (e b) -> p e b", b=7)
        NBL = RD[:, 616:648]
        BBF = RD[:, 648:681]
        POSM = RD[:, 684:748].rearrange("p (t n) -> p t n", t=NT)
        zero = RD[:, 768:1280]
        s1 = small[:, 204:206]
        vals = small[:, 208:216]
        PR = small[:, 216:220]
        VP = small[:, 220:221]
        gmx, gsm, pg, v1, v2, ex = [small[:, 222 + 2 * i:224 + 2 * i] for i in range(6)]
        mnx = small[:, 234:236]

        def bc(ap, n):
            return ap.unsqueeze(2).to_broadcast([ap.shape[0], ap.shape[1], n])

        def mid(ap, n):
            return ap.unsqueeze(1).to_broadcast([ap.shape[0], n, ap.shape[1]])

        block = ctx.enter_context(nc.Block())

        @block.sync
        def _(sp):
            def load(n, turn, per_turn, src, cols, rows=KC):
                s = n % NS
                k = n // NS
                if turn is not None or k > 0:
                    sp.wait_ge(slot_used[s], k + turn * per_turn if turn is not None else k)
                dst = ring[s][:, 0:rows * cols].rearrange("p (k n) -> p k n", k=rows)
                sp.dma_start(dst, src).then_inc(slot_full[s], 16)

            for piece in stream:
                kind, l, a, w = piece
                n = at[piece]
                if kind == "ada":
                    load(n, None, 0, ada_w[l].rearrange("(p k) n -> p k n", k=KC)[:, :, 512 * a:512 * a + 512], 512)
                elif kind == "in":
                    src = hy_w_in[0] if l == 0 else ml_w_in[0]
                    load(n, None, 0, src.rearrange("(p k) n -> p k n", k=KC)[:, :, a:a + w], w)
                elif kind == "out":
                    src = hy_w_out[0] if l == 0 else ml_w_out[0]
                    load(n, None, 0, src.rearrange("(k p) n -> p k n", k=KC)[:, :, 512 * a:512 * a + 512], 512)
                else:
                    with sp.Fori(0, NE // UNROLL) as turn:
                        for u in range(UNROLL):
                            e = turn * UNROLL + u
                            for j, m in enumerate((moe_w_gate, moe_w_up, moe_w_down)):
                                rows = FC if j == 2 else KC
                                src = m[l, bass.ds(e, 1)].rearrange("a (p k) n -> p (a k) n", k=rows)
                                load(n + 3 * u + j, turn, 3 * UNROLL // NS, src, m.shape[-1], rows)
            sp.wait_ge(x_ready, 2 * DEPTH)
            sp.dma_start(out[0].rearrange("(t p) d -> p t d", p=P), xs[:, :, :]).then_inc(out_done, 16)
            sp.wait_ge(out_done, 16)

        @block.gpsimd
        def _(pool):
            for t in range(NT):
                pool.dma_start(xs[:, t, :], x[0, t * P:(t + 1) * P, :]).then_inc(x_in, 16)
            pool.dma_start(cact, c[0].rearrange("(p k) -> p k", k=KC)).then_inc(x_in, 16)
            pool.dma_start(cst[:, :], consts).then_inc(const_in, 16)
            pool.dma_start(brow[:, :], ada_b.rearrange("l (r n) -> (l r) n", n=512)).then_inc(param_in, 16)
            pool.dma_start(gam9[:, 0:8, :], hy_q_norm.unsqueeze(1).to_broadcast([P, 8, HD])).then_inc(param_in, 16)
            pool.dma_start(gam9[:, 8, :], hy_k_norm.to_broadcast([P, HD])).then_inc(param_in, 16)
            pool.dma_start(cwr[:, :], hy_conv_w[0].rearrange("j (c p) -> (j c) p", p=P)).then_inc(param_in, 16)
            pool.dma_start(bgate, ml_b_gates.to_broadcast([P, 2 * HEADS])).then_inc(param_in, 16)
            gi = 0
            for l in range(DEPTH):
                for w in range(2):
                    if gi:
                        pool.wait_ge(gam_free, gi)
                    src = (norm_mix if w == 0 else norm_ffn)[l:l + 1, :]
                    pool.dma_start(gam[:, :], src.to_broadcast([P, D])).then_inc(gam_in, 16)
                    gi += 1
                    if l == 1 and w == 0:
                        pool.wait_ge(gam_free, gi)
                        pool.dma_start(gam[:, :], ml_out_norm.to_broadcast([P, D])).then_inc(gam_in, 16)
                        gi += 1
                if l:
                    pool.wait_ge(rparam_free, l)
                pool.dma_start(rw[:, :, 0:NG], moe_w_group[l].rearrange("(p k) n -> p k n", k=KC)).then_inc(rparam_in, 16)
                pool.dma_start(rw[:, :, NG:], moe_w_expert[l].rearrange("(p k) n -> p k n", k=KC)).then_inc(rparam_in, 16)
                pool.dma_start(rb[:, 0:NG], moe_b_group[l:l + 1, :].to_broadcast([P, NG])).then_inc(rparam_in, 16)
                pool.dma_start(rb[:, NG:], moe_b_expert[l:l + 1, :].to_broadcast([P, NE])).then_inc(rparam_in, 16)

        @block.tensor
        def _(pe):
            mm = nc.tensor.matmul
            state = {"mod": 0, "outp": 0}

            def landed(piece):
                n = at[piece]
                pe.wait_ge(slot_full[n % NS], 16 * (n // NS + 1))
                cols = piece[3] or 512
                return ring[n % NS][:, 0:KC * cols].rearrange("p (k n) -> p k n", k=KC), slot_used[n % NS]

            def mod_sum(i, used):
                pe.wait_ge(part_copied, i + 1)
                if i:
                    pe.wait_ge(mod_ready, i)
                mm(bank[1][:, :], mean32, modp, start=True, stop=False).then_inc(used, 1)
                mm(bank[1][:, :], ident[0:24, i:i + 1].to_broadcast([24, P]), brow[:, :], start=False, stop=True).then_inc(sum_done, 1)

            def mod_pieces(pieces):
                for piece in pieces:
                    i = state["mod"]
                    w, used = landed(piece)
                    if i:
                        pe.wait_ge(part_copied, i)
                    for k in range(KC):
                        g = k % 4
                        last = mm(bank[0][32 * g:32 * g + 32, :], cact[:, k:k + 1].to_broadcast([P, 32]), w[:, k, :],
                                  start=(k < 4), stop=(k >= 4))
                    last.then_inc(part_done, 1)
                    mod_sum(i, used)
                    state["mod"] += 1

            def transpose_h(q):
                for t in range(NT):
                    pe.wait_ge(h_ready, NT * q + t + 1)
                    for g in range(2):
                        b = bank[2 + 2 * t + g]
                        for j in range(4):
                            last = nc.tensor.transpose(b[:, P * j:P * j + P], h[:, t, 4 * g + j, :], ident)
                        last.then_inc(ht_done, 1)

            def out_proj(l):
                for n in range(2):
                    w, used = landed(("out", l, n, 0))
                    for t in range(NT):
                        if t == 0 and n == 0:
                            pe.wait_ge(yt_act, 2 * (l + 1))
                            if l == 0:
                                pe.wait_ge(yconv_ready, 1)
                            else:
                                pe.wait_ge(yt_dve, 2)
                        for k in range(KC):
                            last = mm(bank[4 + 2 * n + t][:, :], yT[:, k, t * P:(t + 1) * P], w[:, k, :],
                                      start=(k == 0), stop=(k == KC - 1))
                        last.then_inc(outp_done, 1)
                    mark_used(used)

            def mark_used(used):
                mm(bank[0][0:32, 0:1], ident[:, 0:32], ident[:, 0:1], start=True, stop=True).then_inc(used, 1)

            def hybrid():
                l = 0
                pe.wait_ge(ht_act, 2)
                pe.wait_ge(ht_dve, 2)
                cols = [(0, 512), (512, 512), (1024, 200)]
                for i, (a, n) in enumerate(cols):
                    w, used = landed(("in", 0, a, n))
                    for t in range(NT):
                        for k in range(KC):
                            last = mm(bank[2 + 2 * i + t][:, 0:n], hT[:, k, t * P:(t + 1) * P], w[:, k, :],
                                      start=(k == 0), stop=(k == KC - 1))
                        last.then_inc(proj_done, 1)
                    mark_used(used)
                for i, a in enumerate((1224, 1736, 2248)):
                    w, used = landed(("in", 0, a, 512))
                    pe.wait_ge(proj_act, i + 1)
                    pe.wait_ge(proj_dve, i + 1)
                    for f in range(4):
                        for k in range(KC):
                            last = mm(bank[2 + 2 * i + f // 2][:, 256 * (f % 2):256 * (f % 2) + 256],
                                      w[:, k, P * f:P * f + P], hT[:, k, :], start=(k == 0), stop=(k == KC - 1))
                        if f % 2:
                            last.then_inc(proj_done, 1)
                    mark_used(used)
                mod_pieces([("ada", 0, i, 0) for i in range(6, 12)])
                pe.wait_ge(param_in, 5 * 16)
                pe.wait_ge(mod_ready, 12)
                nc.tensor.transpose(bank[1][:, 16:28], cwr[:, :], ident[0:12, 0:12]).then_inc(cwt_done, 1)
                pe.wait_ge(proj_act, 6)
                pe.wait_ge(proj_dve, 4)
                pe.wait_ge(bg_act, 2)
                pe.wait_ge(q2_ready, 2)
                for t in range(NT):
                    for g in range(3):
                        b = bank[2 + 3 * t + g]
                        for j in range(4 if g < 2 else 2):
                            ch = 4 * g + j
                            last = nc.tensor.transpose(b[:, P * j:P * j + P], Q2[:, t, 2 * ch:2 * ch + 2, :], ident)
                        last.then_inc(qt_done, 1)
                pe.wait_ge(qt_act, 3)
                pe.wait_ge(qt_dve, 3)
                def head_products(t, first, key, signal):
                    nk = P * (t + 1)
                    for g in range(2):
                        for i in range(2):
                            for par in range(2):
                                hd = 4 * g + 2 * i + par
                                r = slice(64 * par, 64 * par + 64)
                                last = mm(bank[2 + 2 * g + par][:, 256 * i:256 * i + nk],
                                          QT[r, first + hd // 2, t * P:(t + 1) * P], QT[r, key, 0:nk],
                                          start=True, stop=True)
                                if i == 1:
                                    last.then_inc(signal, 1)
                for t in range(NT):
                    if t:
                        pe.wait_ge(relu_done, 4 * t)
                    head_products(t, 5, 9, score_done)
                mod_pieces([("ada", 1, i, 0) for i in range(6)])
                pe.wait_ge(relu_done, 8)
                for t in range(NT):
                    if t:
                        pe.wait_ge(logit_read, 4 * t)
                    head_products(t, 0, 4, logit_done)
                ptn = 0
                for t in range(NT):
                    pe.wait_ge(probs_ready, t + 1)
                    for kt in range(t + 1):
                        for g in range(2):
                            if ptn >= 2:
                                pe.wait_ge((pt_act, pt_dve)[g], ptn // 2)
                            for j in range(4):
                                last = nc.tensor.transpose(bank[6 + g][:, P * j:P * j + P],
                                                           logits[:, 4 * g + j, kt * P:(kt + 1) * P], ident)
                            last.then_inc(pt_done, 1)
                            ptn += 1
                    pe.wait_ge(pt_act, ptn // 2)
                    pe.wait_ge(pt_dve, ptn // 2)
                    if t == 0:
                        pe.wait_ge(logit_read, 8)
                    for par in range(2):
                        for kt in range(t + 1):
                            last = mm(bank[2 + t][64 * par:64 * par + 64, :], vv[:, kt, 0:HD],
                                      PT[:, kt, par:HEADS:2, :], start=(kt == 0), stop=(kt == t))
                    last.then_inc(pv_done, 1)
                out_proj(l)

            def mlstm():
                l = 1
                pe.wait_ge(ht_act, 2 + 2 * 2)
                pe.wait_ge(ht_dve, 2 + 2 * 2)
                b0 = 12
                for i, a in enumerate((0, 512)):
                    w, used = landed(("in", 1, a, 512))
                    for f in range(4):
                        for k in range(KC):
                            last = mm(bank[2 + 2 * i + f // 2][:, 256 * (f % 2):256 * (f % 2) + 256],
                                      w[:, k, P * f:P * f + P], hT[:, k, :], start=(k == 0), stop=(k == KC - 1))
                        if f % 2:
                            last.then_inc(proj_done, 1)
                    mark_used(used)
                banks = [(6, 7), (2, 3), (4, 5), (6, 7), (2, 3)]
                for i, (a, n) in enumerate(((1024, 512), (1536, 512), (2048, 16), (2064, 512), (2576, 512))):
                    w, used = landed(("in", 1, a, n))
                    if i:
                        pe.wait_ge(proj_act, (7, 7, 8, 9)[i - 1])
                    if i > 2:
                        pe.wait_ge(proj_dve, i + 2)
                    for t in range(NT):
                        for k in range(KC):
                            last = mm(bank[banks[i][t]][:, 0:n], hT[:, k, t * P:(t + 1) * P], w[:, k, :],
                                      start=(k == 0), stop=(k == KC - 1))
                        last.then_inc(proj_done, 1)
                    mark_used(used)
                pe.wait_ge(logf_ready, 1)
                mm(bank[4][:, 0:8], tri_le, lf[:, 0, :], start=True, stop=True)
                mm(bank[4][:, 8:16], ones, lf[:, 0, :], start=True, stop=False)
                mm(bank[4][:, 8:16], tri_le, lf[:, 1, :], start=False, stop=True).then_inc(cumf_done, 1)
                mod_pieces([("ada", 1, i, 0) for i in range(6, 12)])
                pe.wait_ge(a_ready, 1)
                for t in range(NT):
                    last = nc.tensor.transpose(bank[5][0:8, t * P:(t + 1) * P], asb[:, t, :], ident)
                last.then_inc(at_done, 1)
                pe.wait_ge(m_ready, 1)
                for t in range(NT):
                    last = nc.tensor.transpose(bank[5][:, 256 + 8 * t:264 + 8 * t], mrow[:, 1, t * P:(t + 1) * P], ident[0:8, 0:8])
                last.then_inc(at_done, 1)
                pe.wait_ge(proj_act, 11)
                mb = (2, 3, 6, 7)
                for hd in range(HEADS):
                    last = mm(bank[mb[hd // 2]][:, 256 * (hd % 2):256 * (hd % 2) + 256],
                              ident[0:8, hd:hd + 1].to_broadcast([8, P]), mrow[:, 1, :], start=True, stop=True)
                    if hd % 2:
                        last.then_inc(mb_done, 1)
                sbk = (4, 5, 2, 3, 6, 7, 4, 5)
                pe.wait_ge(em_in, 1)
                for hd in range(HEADS):
                    if 2 <= hd < 6:
                        pe.wait_ge(mbc_dve, 4 * (hd // 2))
                        pe.wait_ge(mbc_act, 2 * (hd // 2))
                    if hd >= 6:
                        pe.wait_ge(pw_ready, 2 * (hd - 5))
                    r = slice(64 * (hd % 2), 64 * (hd % 2) + 64)
                    b = bank[sbk[hd]]
                    mm(b[:, 0:256], qkT[r, 4 + hd // 2, 0:P], qkT[r, hd // 2, :], start=True, stop=True)
                    mm(b[:, 256:384], qkT[r, 4 + hd // 2, P:], qkT[r, hd // 2, P:], start=True, stop=True).then_inc(st_done, 1)
                pe.wait_ge(pw_ready, 16)
                pe.wait_ge(vone_ready, 1)
                nb = ((0, 1, 2), (3, 6, 7))
                for t in range(NT):
                    if t == 0:
                        pe.wait_ge(mod_ready, 24)
                    for hd in range(HEADS):
                        b = bank[nb[t][hd // 3]]
                        o = b[:, 129 * (hd % 3):129 * (hd % 3) + 129]
                        if t == 0:
                            last = mm(o, MB0[:, hd, 0:P], vx[:, 0, hd, :], start=True, stop=True)
                        else:
                            mm(o, MB0[:, hd, P:], vx[:, 0, hd, :], start=True, stop=False)
                            last = mm(o, MB1[:, hd, :], vx[:, 1, hd, :], start=False, stop=True)
                        if hd in (2, 5, 7):
                            last.then_inc(num_done, 1)
                for t in range(NT):
                    pe.wait_ge(y_ready, t + 1)
                    for g in range(2):
                        for j in range(4):
                            last = nc.tensor.transpose(bank[4 + g if t == 0 else 2 * g][:, P * j:P * j + P], HN[:, t, 4 * g + j, :], ident)
                        last.then_inc(yb_done, 1)
                out_proj(l)

            def ffn(l):
                pe.wait_ge(ht_act, 2 * (2 * l + 2))
                pe.wait_ge(ht_dve, 2 * (2 * l + 2))
                pe.wait_ge(rparam_in, 64 * (l + 1))
                for t in range(NT):
                    for k in range(KC):
                        last = mm(bank[6][:, 36 * t:36 * t + 36], hT[:, k, t * P:(t + 1) * P], rw[:, k, :],
                                  start=(k == 0), stop=(k == KC - 1))
                last.then_inc(rlog_done, 1)
                pe.wait_ge(onehot_ready, l + 1)
                mm(bank[7][:, 0:32], tri_lt, OS[:, 0, :], start=True, stop=True)
                mm(bank[7][:, 32:64], ones, OS[:, 0, :], start=True, stop=False)
                mm(bank[7][:, 32:64], tri_lt, OS[:, 1, :], start=False, stop=True)
                mm(bank[7][:, 64:96], ones, OS[:, 0, :], start=True, stop=False)
                mm(bank[7][:, 64:96], ones, OS[:, 1, :], start=False, stop=True).then_inc(rank_done, 1)
                pe.wait_ge(zero_ready, l + 1)
                for b in range(4):
                    mm(bank[b][:, :], zero[:, 0:P], zero, start=True, stop=True)
                pe.wait_ge(diag_ready, l + 1)
                for g in range(2):
                    last = mm(bank[5 + g][:, :], ones, DG[:, 4 * g:4 * g + 4, :], start=True, stop=True)
                last.then_inc(rows_done, 1)

                def gather(v):
                    pe.wait_ge(sel_ready[l], v + 1)
                    for k in range(KC):
                        for t in range(NT):
                            last = mm(bank[4][:, BLK * k:BLK * k + BLK], h[:, t, k, :], SEL[:, t, :],
                                      start=(t == 0), stop=(t == NT - 1))
                    last.then_inc(gather_done[l], 1)

                def scatter(t):
                    for n in range(2):
                        last = mm(bank[2 * t + n][:, :], SC[:, t * P:(t + 1) * P], Y[:, 512 * n:512 * n + 512],
                                  start=False, stop=False, skip_group_check=True)
                    return last

                def expert_block(v, weights, landed_expert):
                    pe.wait_ge(xt_ready[l], v + 1)
                    pe.wait_ge(y_act[l], v + 1)
                    pe.wait_ge(y_dve[l], v + 1)
                    for j, (b, done) in enumerate(((5, gate_done[l]), (6, up_done[l]))):
                        w = weights[j]
                        landed_expert(j)
                        for k in range(KC):
                            g = k % 4
                            last = mm(bank[b][32 * g:32 * g + 32, :], XT[:, k, :], w[:, k, :], start=(k < 4), stop=(k >= 4))
                        last.then_inc(done, 1)
                    pe.wait_ge(scat_ready[l], v + 1)
                    scatter(0)
                    pe.wait_ge(hg_ready[l], v + 1)
                    for f in range(FC):
                        mm(bank[7][:, BLK * f:BLK * f + BLK], HG[:, f:DE:FC], fold, start=True, stop=True)
                    pe.wait_ge(hu_ready[l], v + 1)
                    for f in range(FC):
                        last = mm(bank[7][:, P + BLK * f:P + BLK * f + BLK], HU[:, f:DE:FC], fold, start=True, stop=True)
                    last.then_inc(turn_done[l], 1)
                    scatter(1)
                    landed_expert(2)
                    pe.wait_ge(hid_ready[l], v + 1)
                    for n in range(2):
                        for f in range(FC):
                            last = mm(bank[5 + n][32 * f:32 * f + 32, :], HID[:, f, :], weights[2][:, f, 512 * n:512 * n + 512],
                                      start=True, stop=True)
                        last.then_inc(down_done[l], 1)
                    gather(v + 1)

                gather(0)
                pe.wait_ge(table_ready, l + 1)
                n0 = at[("experts", l, 0, 0)]
                with pe.Fori(0, NE // UNROLL) as turn:
                    for u in range(UNROLL):
                        first = pe.value_load(tab[0:1, bass.ds(turn * UNROLL + u, 1)], min_val=0, max_val=48)
                        end = pe.value_load(tab[0:1, bass.ds(turn * UNROLL + u + 1, 1)], min_val=1, max_val=49)
                        w = [ring[(n0 + 3 * u + j) % NS][:, :].rearrange("p (k n) -> p k n", k=FC if j == 2 else KC)
                             for j in range(3)]

                        def landed_expert(j):
                            n = n0 + 3 * u + j
                            pe.wait_ge(slot_full[n % NS], 16 * (n // NS + 1) + 16 * (3 * UNROLL // NS) * turn)

                        with pe.Fori(first, end) as v:
                            expert_block(v, w, landed_expert)
                        for j in range(3):
                            mark_used7(slot_used[(n0 + 3 * u + j) % NS])
                total = pe.value_load(tab[0:1, NE:NE + 1], min_val=NE, max_val=48)
                pe.wait_ge(y_act[l], total + 1)
                pe.wait_ge(y_dve[l], total + 1)
                pe.wait_ge(scat_ready[l], total + 1)
                scatter(0)
                scatter(1).then_inc(acc_done, 1)

            def mark_used7(used):
                mm(bank[7][0:32, 256:257], ident[:, 0:32], ident[:, 0:1], start=True, stop=True).then_inc(used, 1)

            pe.wait_ge(const_in, 16)
            pe.wait_ge(param_in, 16 * 5)
            pe.wait_ge(cact_ready, 1)
            mod_pieces([("ada", 0, i, 0) for i in range(6)])
            for l in range(DEPTH):
                transpose_h(2 * l)
                (hybrid, mlstm)[l]()
                transpose_h(2 * l + 1)
                ffn(l)

        @block.scalar
        def _(act):
            steps = [0]

            def step(ins):
                steps[0] += 1
                ins.then_inc(A, 1)
                act.wait_ge(A, steps[0])

            def copy(dst, src):
                return nc.scalar.activation(dst, src, ACT.Copy)

            modn = [0]

            def mod_pieces(layer, js):
                for j in js:
                    i = modn[0]
                    act.wait_ge(part_done, i + 1)
                    copy(modp, bank[0][:, :]).then_inc(part_copied, 1)
                    act.wait_ge(sum_done, i + 1)
                    dst = modvec(layer, j // 2)[:, 512 * (j % 2):512 * (j % 2) + 512]
                    copy(dst, bank[1][:, :]).then_inc(mod_ready, 1)
                    modn[0] += 1

            def norm(q):
                if q:
                    act.wait_ge(x_ready, q)
                for t in range(NT):
                    i = nc.scalar.activation(RC[:, 0:D], xs[:, t, :], ACT.Square, accum_out=ssq[:, t:t + 1])
                    step(i)
                nc.scalar.activation(rstd, ssq, ACT.Sqrt, scale=1.0 / D, bias=eps).then_inc(std_done, 1)

            def copy_ht(q):
                for t in range(NT):
                    act.wait_ge(ht_done, 4 * q + 2 * t + 1)
                    copy(hT[:, 0:4, t * P:(t + 1) * P], bank[2 + 2 * t][:, :].rearrange("p (k t) -> p k t", k=4)).then_inc(ht_act, 1)

            def hybrid():
                for i, (a, n) in enumerate(((0, 512), (512, 512), (1024, 200))):
                    act.wait_ge(proj_done, 2 * i + 1)
                    copy(patt[:, 0, a:a + n], bank[2 + 2 * i][:, 0:n]).then_inc(proj_act, 1)
                act.wait_ge(proj_act, 3)
                act.wait_ge(proj_dve, 3)
                for t in range(NT):
                    nc.scalar.activation(qsq[:, t, :, :], patt[:, t, 0:576].rearrange("p (g d) -> p g d", d=HD), ACT.Square).then_inc(sq_ready, 1)
                act.wait_ge(qss_ready, 1)
                nc.scalar.activation(qrs, qss, ACT.Sqrt, scale=1.0 / HD, bias=eps).then_inc(qstd_ready, 1)
                for i in range(2):
                    act.wait_ge(proj_done, 7 + i)
                    copy(yT[:, 4 + 2 * i:6 + 2 * i, :], bank[2 + i][:, :].rearrange("p (c t) -> p c t", c=2)).then_inc(bg_act, 1)
                for i in range(2):
                    act.wait_ge(proj_done, 9 + i)
                    ins = copy(cgs[:, 2 * i:2 * i + 2, :], bank[4 + i][:, :].rearrange("p (c t) -> p c t", c=2))
                    ins.then_inc(proj_act, 1)
                mod_pieces(0, range(6, 12))
                act.wait_ge(cwt_done, 1)
                copy(cwT, bank[1][:, 16:28]).then_inc(proj_act, 1)
                for t in range(NT):
                    for g in ((0, 2), (1,))[t]:
                        act.wait_ge(qt_done, 3 * t + g + 1)
                        m = 4 if g < 2 else 2
                        copy(QT[:, 4 * g:4 * g + m, t * P:(t + 1) * P],
                             bank[2 + 3 * t + g][:, 0:P * m].rearrange("p (c t) -> p c t", c=m)).then_inc(qt_act, 1)
                r = 0
                for t in range(NT):
                    nk = P * (t + 1)
                    for b in range(4):
                        act.wait_ge(score_done, 4 * t + b + 1)
                        if r >= 2:
                            act.wait_ge(relu_used, r - 1)
                        nc.scalar.activation(relu[r % 2].rearrange("p (i s) -> p i s", i=2)[:, :, 0:nk],
                                             bank[2 + b][:, :].rearrange("p (i s) -> p i s", i=2)[:, :, 0:nk],
                                             ACT.Relu, scale=HD ** -0.5).then_inc(relu_done, 1)
                        r += 1
                mod_pieces(1, range(6))
                ptn = 0
                for t in range(NT):
                    nk = P * (t + 1)
                    act.wait_ge(max_ready, t + 1)
                    for hd in range(HEADS):
                        last = nc.scalar.activation(logits[:, hd, 0:nk], logits[:, hd, 0:nk], ACT.Exp, scale=HD ** -0.5,
                                                    bias=amax[:, hd:hd + 1], accum_out=asum[:, hd:hd + 1])
                    last.then_inc(exp_done, 1)
                    for kt in range(t + 1):
                        act.wait_ge(pt_done, 2 * ptn + 1)
                        copy(PT[:, kt, 0:4, :], bank[6][:, :].rearrange("p (h q) -> p h q", h=4)).then_inc(pt_act, 1)
                        ptn += 1
                    act.wait_ge(pv_done, t + 1)
                    copy(yT[:, 0:4, t * P:(t + 1) * P], bank[2 + t][:, :].rearrange("p (c q) -> p c q", c=4)).then_inc(yt_act, 1)

            def mlstm():
                for i in range(4):
                    act.wait_ge(proj_done, 12 + i + 1)
                    ins = copy(qkT[:, 2 * i:2 * i + 2, :], bank[2 + i][:, :].rearrange("p (c t) -> p c t", c=2))
                ins.then_inc(proj_act, 1)
                for i, (half, b) in enumerate(((0, 6), (1, 2))):
                    act.wait_ge(proj_done, 17 + 2 * i)
                    copy(vx[:, 0, 4 * half:4 * half + 4, 0:VD], bank[b][:, :].rearrange("p (h v) -> p h v", h=4)).then_inc(proj_act, 1)
                act.wait_ge(gates_ready, 1)
                step(nc.scalar.activation(g3, gts[:, :, 8:16], ACT.Abs))
                step(nc.scalar.activation(g3, g3, ACT.Exp, scale=-1.0))
                nc.scalar.activation(g3, g3, ACT.Ln, bias=1.0).then_inc(absexp_done, 1)
                for i in range(2):
                    b = ((6, 7), (2, 3))[i]
                    for t in range(NT):
                        act.wait_ge(proj_done, 23 + 2 * i + t)
                        ins = nc.scalar.activation(ogs[:, t, 512 * i:512 * i + 512], bank[b[t]][:, :], ACT.Sigmoid)
                    ins.then_inc(proj_act, 1)
                mod_pieces(1, range(6, 12))
                act.wait_ge(em_in, 1)
                nc.scalar.activation(em, em, ACT.Exp, scale=-1.0).then_inc(em_ready, 1)
                for b in range(4):
                    act.wait_ge(mb_done, b + 1)
                    act.wait_ge(mbc_dve, 2 * b + 2)
                    copy(MB0[:, 2 * b:2 * b + 2, P:], bank[(2, 3, 6, 7)[b]][:, :].rearrange("p (h t) -> p h t", h=2)[:, :, P:]).then_inc(mbc_act, 1)
                for hd in range(HEADS):
                    act.wait_ge(mbc_act, hd // 2 + 1)
                    act.wait_ge(mbc_dve, 2 * (hd // 2 + 1))
                    nc.scalar.activation(MB0[:, hd, :], MB0[:, hd, :], ACT.Exp, scale=-1.0, bias=asb[:, 0, hd:hd + 1]).then_inc(w_done, 1)
                    nc.scalar.activation(MB1[:, hd, :], MB1[:, hd, :], ACT.Exp, scale=-1.0, bias=asb[:, 1, hd:hd + 1]).then_inc(w_done, 1)
                act.wait_ge(pw_ready, 16)
                for t in range(NT):
                    act.wait_ge(hn_ready, t + 1)
                    nc.scalar.activation(hsq[:, t, :, :], HN[:, t, :, :], ACT.Square).then_inc(hsq_done, 1)
                act.wait_ge(hss_ready, 1)
                nc.scalar.activation(hss, hss, ACT.Sqrt, scale=1.0 / VD, bias=eps).then_inc(hstd_done, 1)
                for t in range(NT):
                    act.wait_ge(yb_done, 2 * t + 1)
                    copy(yT[:, 0:4, t * P:(t + 1) * P], bank[4 if t == 0 else 0][:, :].rearrange("p (c q) -> p c q", c=4)).then_inc(yt_act, 1)

            def ffn(l):
                act.wait_ge(gexp_in, l + 1)
                nc.scalar.activation(R1[:, :, 0:NG], R1[:, :, 0:NG], ACT.Exp).then_inc(gexp_done, 1)
                act.wait_ge(wexp_in, l + 1)
                nc.scalar.activation(ex, ex, ACT.Exp).then_inc(wexp_done, 1)
                act.wait_ge(rows_done, l + 1)
                copy(posrow, bank[5][:, :].rearrange("p (c t) -> p c t", c=2))
                copy(wrow, bank[6][:, :].rearrange("p (c t) -> p c t", c=2)).then_inc(rows_copied, 1)
                act.wait_ge(zero_ready, l + 1)
                copy(Y[:, 0:512], zero).then_inc(y_act[l], 1)

                def copy_xt(v):
                    act.wait_ge(gather_done[l], v + 1)
                    copy(XT, bank[4][:, 0:KC * BLK].rearrange("p (k s) -> p k s", k=KC)).then_inc(xt_ready[l], 1)

                copy_xt(0)
                act.wait_ge(table_ready, l + 1)
                total = act.value_load(tab[0:1, NE:NE + 1], min_val=NE, max_val=48)
                with act.Fori(0, total) as v:
                    act.wait_ge(gate_done[l], v + 1)
                    copy(HG, bank[5][:, :]).then_inc(hg_ready[l], 1)
                    act.wait_ge(turn_done[l], v + 1)
                    nc.scalar.activation(SIL, bank[7][:, 0:P].rearrange("p (f s) -> p f s", f=FC), ACT.Silu).then_inc(silu_ready[l], 1)
                    act.wait_ge(down_done[l], 2 * v + 1)
                    copy(Y[:, 0:512], bank[5][:, :]).then_inc(y_act[l], 1)
                    copy_xt(v + 1)

            act.wait_ge(x_in, 16 * 3)
            nc.scalar.activation(cact, cact, ACT.Silu).then_inc(cact_ready, 1)
            act.wait_ge(const_in, 16)
            mod_pieces(0, range(6))
            for l in range(DEPTH):
                norm(2 * l)
                copy_ht(2 * l)
                (hybrid, mlstm)[l]()
                norm(2 * l + 1)
                copy_ht(2 * l + 1)
                ffn(l)

        @block.vector
        def _(dve):
            v = nc.vector
            steps = [0]

            def step(ins):
                steps[0] += 1
                ins.then_inc(V, 1)
                dve.wait_ge(V, steps[0])

            gain = [0]

            def norm(q):
                l, w = q // 2, q % 2
                sh, sc = modvec(l, 3 * w), modvec(l, 3 * w + 1)
                dve.wait_ge(gam_in, 16 * (gain[0] + 1))
                dve.wait_ge(mod_ready, 6 * (q + 1))
                gain[0] += 1
                ins = v.scalar_tensor_tensor(out=sc, in0=sc, scalar=1.0, in1=gam[:, :], op0=ALU.add, op1=ALU.mult)
                ins.then_inc(gam_free, 1)
                dve.wait_ge(gam_free, gain[0])
                dve.wait_ge(std_done, q + 1)
                step(v.reciprocal(rstd, rstd))
                for t in range(NT):
                    hv = h[:, t, :, :].rearrange("q k p -> q p k")
                    step(v.scalar_tensor_tensor(out=hv, in0=xs[:, t, :].rearrange("q (p k) -> q p k", k=KC), scalar=rstd[:, t:t + 1],
                                                in1=sc.rearrange("q (p k) -> q p k", k=KC), op0=ALU.mult, op1=ALU.mult))
                    v.tensor_tensor(hv, hv, sh.rearrange("q (p k) -> q p k", k=KC), ALU.add).then_inc(h_ready, 1)

            def copy_ht(q):
                for t in range(NT):
                    dve.wait_ge(ht_done, 4 * q + 2 * t + 2)
                    v.tensor_copy(hT[:, 4:8, t * P:(t + 1) * P], bank[3 + 2 * t][:, :].rearrange("p (k t) -> p k t", k=4)).then_inc(ht_dve, 1)

            def residual(l, first, g):
                for n in range(2):
                    for t in range(NT):
                        dve.wait_ge(outp_done, 4 * l + 2 * n + t + 1)
                        cols = slice(512 * n, 512 * n + 512)
                        step(v.tensor_tensor(otmp, bank[4 + 2 * n + t][:, :], g[:, cols], ALU.mult))
                        ins = v.tensor_tensor(xs[:, t, cols], xs[:, t, cols], otmp, ALU.add)
                        if n == 1 and t == 1:
                            ins.then_inc(x_ready, 1)
                        else:
                            step(ins)

            def hybrid():
                for i, (a, n) in enumerate(((0, 512), (512, 512), (1024, 200))):
                    dve.wait_ge(proj_done, 2 * i + 2)
                    v.tensor_copy(patt[:, 1, a:a + n], bank[3 + 2 * i][:, 0:n]).then_inc(proj_dve, 1)
                dve.wait_ge(proj_act, 3)
                dve.wait_ge(proj_dve, 3)
                step(v.tensor_copy(vv[:, :, 0:HD], patt[:, :, 576:640]))
                step(v.tensor_scalar(wsc, patt[:, :, 1216:1224], float(HEADS) ** -0.5, None, ALU.mult))
                dve.wait_ge(sq_ready, 2)
                v.tensor_reduce(qss.rearrange("p (t g) -> p t g", t=NT), qsq, AX, ALU.add).then_inc(qss_ready, 1)
                dve.wait_ge(qstd_ready, 1)
                step(v.reciprocal(qrs, qrs))
                dve.wait_ge(param_in, 5 * 16)
                for t in range(NT):
                    qk = patt[:, t, 0:576].rearrange("p (g d) -> p g d", d=HD)
                    step(v.tensor_tensor(qk, qk, bc(qrs[:, 9 * t:9 * t + 9], HD), ALU.mult))
                    step(v.tensor_tensor(qk, qk, gam9[:, :, :], ALU.mult))
                for t in range(NT):
                    co = rope[:, t, 0, :].unsqueeze(1).to_broadcast([P, 9, HD // 2])
                    si = rope[:, t, 1, :].unsqueeze(1).to_broadcast([P, 9, HD // 2])
                    for g in range(2):
                        src = patt[:, t, 640 * g:640 * g + 576].rearrange("p (g c d) -> p g c d", c=2, d=HD // 2)
                        dst = Q2[:, t, 10 * g:10 * g + 9, :].rearrange("p g (c d) -> p g c d", c=2)
                        for o in range(2):
                            tm = RD[:, 768 + 288 * (2 * g + o):768 + 288 * (2 * g + o) + 288].rearrange("p (g d) -> p g d", d=HD // 2)
                            step(v.tensor_tensor(tm, src[:, :, 1 - o, :], si, ALU.mult))
                            step(v.tensor_tensor(dst[:, :, o, :], src[:, :, o, :], co, ALU.mult))
                            step(v.tensor_tensor(dst[:, :, o, :], dst[:, :, o, :], tm, ALU.subtract if o == 0 else ALU.add))
                        ins = v.tensor_copy(Q2[:, t, 10 * g + 9, :], Q2[:, t, 10 * g + 8, :])
                        if g == 1:
                            ins.then_inc(q2_ready, 1)
                        else:
                            step(ins)
                dve.wait_ge(proj_act, 5)
                for i in range(2):
                    dve.wait_ge(proj_done, 11 + i)
                    ins = v.tensor_tensor(cgs[:, 2 * i:2 * i + 2, :], cgs[:, 2 * i:2 * i + 2, :],
                                          bank[6 + i][:, :].rearrange("p (c t) -> p c t", c=2), ALU.mult)
                ins.then_inc(proj_dve, 1)
                dve.wait_ge(proj_dve, 4)
                dve.wait_ge(proj_act, 6)
                dve.wait_ge(bg_act, 2)
                for ch in range(4):
                    w = [cwT[:, 4 * j + ch:4 * j + ch + 1] for j in range(3)]
                    z = cgs[:, ch, :]
                    o = ctmp[:, ch, :]
                    step(v.tensor_scalar(o, z, w[2], None, ALU.mult))
                    for j in (1, 0):
                        d = 2 - j
                        step(v.scalar_tensor_tensor(out=o[:, d:], in0=z[:, 0:SEQ - d], scalar=w[j], in1=o[:, d:],
                                                    op0=ALU.mult, op1=ALU.add))
                v.tensor_tensor(yT[:, 4:8, :], yT[:, 4:8, :], ctmp, ALU.mult).then_inc(yconv_ready, 1)
                for t in range(NT):
                    for g in ((1,), (0, 2))[t]:
                        dve.wait_ge(qt_done, 3 * t + g + 1)
                        m = 4 if g < 2 else 2
                        v.tensor_copy(QT[:, 4 * g:4 * g + m, t * P:(t + 1) * P],
                                      bank[2 + 3 * t + g][:, 0:P * m].rearrange("p (c t) -> p c t", c=m)).then_inc(qt_dve, 1)
                r = 0
                for t in range(NT):
                    nk = P * (t + 1)
                    sc = score[:, 0:nk]
                    if t:
                        step(v.memset(score[:, 0:P], 0.0))
                    step(v.tensor_copy(score[:, t * P:nk], causal))
                    for b in range(4):
                        dve.wait_ge(relu_done, r + 1)
                        for i in range(2):
                            hd = 4 * (b // 2) + 2 * i + b % 2
                            ins = v.scalar_tensor_tensor(out=sc, in0=relu[r % 2][:, 256 * i:256 * i + nk],
                                                         scalar=wsc[:, t, hd:hd + 1], in1=sc, op0=ALU.mult, op1=ALU.add)
                            if i == 0:
                                step(ins)
                        ins.then_inc(relu_used, 1)
                        dve.wait_ge(relu_used, r + 1)
                        r += 1
                    for rd in range(TOPK // 8):
                        src = sc if rd == 0 else work[:, 0:nk]
                        step(v.max(out=top8, in_=src))
                        step(v.match_replace(out=work[:, 0:nk], in_to_replace=top8, in_values=src, imm_value=TAKEN))
                    step(v.tensor_scalar(work[:, 0:nk], work[:, 0:nk], 0.5 * TAKEN, None, ALU.is_lt))
                    step(v.tensor_scalar(sc, sc, 0.1 * MASKED, None, ALU.is_gt))
                    step(v.tensor_tensor(sc, sc, work[:, 0:nk], ALU.mult))
                    step(v.tensor_scalar(selb[:, t, 0:nk], sc, -MASKED, MASKED, ALU.mult, ALU.add))
                ptn = 0
                for t in range(NT):
                    nk = P * (t + 1)
                    if t:
                        dve.wait_ge(pt_done, 2)
                    for b in range(4):
                        dve.wait_ge(logit_done, 4 * t + b + 1)
                        first = 4 * (b // 2) + b % 2
                        v.tensor_tensor(logits[:, first:first + 3:2, 0:nk],
                                        bank[2 + b][:, :].rearrange("p (i s) -> p i s", i=2)[:, :, 0:nk],
                                        mid(selb[:, t, 0:nk], 2), ALU.add).then_inc(logit_read, 1)
                    dve.wait_ge(logit_read, 4 * t + 4)
                    step(v.tensor_reduce(amax, logits[:, :, 0:nk], AX, ALU.max))
                    v.tensor_scalar(amax, amax, -(HD ** -0.5), None, ALU.mult).then_inc(max_ready, 1)
                    dve.wait_ge(exp_done, t + 1)
                    step(v.reciprocal(rsum, asum))
                    v.tensor_tensor(logits[:, :, 0:nk], logits[:, :, 0:nk], bc(rsum, nk), ALU.mult).then_inc(probs_ready, 1)
                    for kt in range(t + 1):
                        dve.wait_ge(pt_done, 2 * ptn + 2)
                        v.tensor_copy(PT[:, kt, 4:8, :], bank[7][:, :].rearrange("p (h q) -> p h q", h=4)).then_inc(pt_dve, 1)
                        ptn += 1

            def mlstm():
                dve.wait_ge(qt_done, 6)
                v.memset(vx[:, :, :, VD:VD + 1], 1.0).then_inc(vone_ready, 1)
                for i, (half, b) in enumerate(((0, 7), (1, 3))):
                    dve.wait_ge(proj_done, 18 + 2 * i)
                    v.tensor_copy(vx[:, 1, 4 * half:4 * half + 4, 0:VD], bank[b][:, :].rearrange("p (h v) -> p h v", h=4)).then_inc(proj_dve, 1)
                for t in range(NT):
                    dve.wait_ge(proj_done, 21 + t)
                    ins = v.tensor_tensor(gts[:, t, :], bank[4 + t][:, 0:16], bgate, ALU.add)
                    if t:
                        ins.then_inc(gates_ready, 1)
                    else:
                        step(ins)
                dve.wait_ge(gates_ready, 1)
                step(v.tensor_scalar(lf, gts[:, :, 8:16], 0.0, None, ALU.min))
                dve.wait_ge(absexp_done, 1)
                v.tensor_tensor(lf, lf, g3, ALU.subtract).then_inc(logf_ready, 1)
                dve.wait_ge(cumf_done, 1)
                step(v.tensor_copy(cumf, bank[4][:, 0:16].rearrange("p (t n) -> p t n", t=NT)))
                v.tensor_tensor(asb, gts[:, :, 0:8], cumf, ALU.subtract).then_inc(a_ready, 1)
                dve.wait_ge(at_done, 1)
                step(v.tensor_copy(mrow[:, 0, :], bank[5][0:8, 0:SEQ]))
                v.tensor_tensor_scan(out=mrow[:, 1, :], data0=mrow[:, 0, :], data1=mrow[:, 0, :], initial=0.0, op0=ALU.max, op1=ALU.max).then_inc(m_ready, 1)
                dve.wait_ge(at_done, 2)
                v.tensor_tensor(em, bank[5][:, 256:272].rearrange("p (t n) -> p t n", t=NT), cumf, ALU.add).then_inc(em_in, 1)
                for b in range(4):
                    dve.wait_ge(mb_done, b + 1)
                    src = bank[(2, 3, 6, 7)[b]][:, :].rearrange("p (h t) -> p h t", h=2)
                    v.tensor_tensor(MB0[:, 2 * b:2 * b + 2, 0:P], src[:, :, 0:P], mid(maskT, 2), ALU.subtract).then_inc(mbc_dve, 1)
                    v.tensor_tensor(MB1[:, 2 * b:2 * b + 2, :], src[:, :, P:], mid(maskT, 2), ALU.subtract).then_inc(mbc_dve, 1)
                sbk = (4, 5, 2, 3, 6, 7, 4, 5)
                for hd in range(HEADS):
                    dve.wait_ge(st_done, hd + 1)
                    dve.wait_ge(w_done, 2 * hd + 2)
                    v.scalar_tensor_tensor(out=MB0[:, hd, :], in0=bank[sbk[hd]][:, 0:256], scalar=HD ** -0.5, in1=MB0[:, hd, :],
                                           op0=ALU.mult, op1=ALU.mult).then_inc(pw_ready, 1)
                    v.scalar_tensor_tensor(out=MB1[:, hd, :], in0=bank[sbk[hd]][:, 256:384], scalar=HD ** -0.5, in1=MB1[:, hd, :],
                                           op0=ALU.mult, op1=ALU.mult).then_inc(pw_ready, 1)
                nb = ((0, 1, 2), (3, 6, 7))
                dve.wait_ge(em_ready, 1)
                for t in range(NT):
                    for i, m in enumerate((3, 3, 2)):
                        dve.wait_ge(num_done, 3 * t + i + 1)
                        src = bank[nb[t][i]][:, 0:129 * m].rearrange("p (h v) -> p h v", h=m)
                        dn = den[:, t, 3 * i:3 * i + m]
                        dsum = src[:, :, VD:VD + 1].rearrange("p h o -> p (h o)")
                        step(v.tensor_scalar(dn, dsum, -1.0, None, ALU.mult))
                        step(v.tensor_tensor(dn, dn, dsum, ALU.max))
                        step(v.tensor_tensor(dn, dn, em[:, t, 3 * i:3 * i + m], ALU.max))
                        step(v.reciprocal(dn, dn))
                        ins = v.tensor_tensor(HN[:, t, 3 * i:3 * i + m, :], src[:, :, 0:VD], bc(dn, VD), ALU.mult)
                        if i == 2:
                            ins.then_inc(hn_ready, 1)
                    dve.wait_ge(hsq_done, t + 1)
                    ins = v.tensor_reduce(hss[:, t, :], hsq[:, t, :, :], AX, ALU.add)
                    if t:
                        ins.then_inc(hss_ready, 1)
                dve.wait_ge(hstd_done, 1)
                step(v.reciprocal(hss, hss))
                dve.wait_ge(gam_in, 16 * (gain[0] + 1))
                gain[0] += 1
                for t in range(NT):
                    step(v.tensor_tensor(HN[:, t, :, :], HN[:, t, :, :], bc(hss[:, t, :], VD), ALU.mult))
                    flat = HN[:, t, :, :].rearrange("p h v -> p (h v)")
                    step(v.tensor_tensor(flat, flat, gam[:, :], ALU.mult))
                    v.tensor_tensor(flat, flat, ogs[:, t, :], ALU.mult).then_inc(y_ready, 1)
                dve.wait_ge(y_ready, 2)
                v.memset(small[:, 250:251], 0.0).then_inc(gam_free, 1)
                for t in range(NT):
                    dve.wait_ge(yb_done, 2 * t + 2)
                    v.tensor_copy(yT[:, 4:8, t * P:(t + 1) * P], bank[5 if t == 0 else 2][:, :].rearrange("p (c q) -> p c q", c=4)).then_inc(yt_dve, 1)

            def first_max(val, onehot, scratch, top, n):
                step(v.tensor_reduce(top, val, AX, ALU.max))
                step(v.tensor_tensor(scratch, val, bc(top, n), ALU.is_equal))
                step(v.tensor_tensor(scratch, scratch, mid(idxm[:, 0:n], NT), ALU.mult))
                step(v.tensor_reduce(mnx, scratch, AX, ALU.min))
                step(v.tensor_tensor(onehot, mid(idxm[:, 0:n], NT), bc(mnx, n), ALU.is_equal))

            def ffn(l):
                dve.wait_ge(rlog_done, l + 1)
                dve.wait_ge(rparam_in, 64 * (l + 1))
                step(v.tensor_tensor(LG, bank[6][:, 0:72].rearrange("p (t n) -> p t n", t=NT), mid(rb, NT), ALU.add))
                v.memset(small[:, 250:251], 0.0).then_inc(rparam_free, 1)
                first_max(LG[:, :, 0:NG], R2[:, :, 0:NG], R1[:, :, 0:NG], gmx, NG)
                v.tensor_tensor(R1[:, :, 0:NG], LG[:, :, 0:NG], bc(gmx, NG), ALU.subtract).then_inc(gexp_in, 1)
                group = R2[:, :, 0:NG]
                O14 = O1.rearrange("p t (g e) -> p t g e", g=NG)
                for t in range(NT):
                    step(v.tensor_tensor(O14[:, t, :, :], LG[:, t, NG:].rearrange("p (g e) -> p g e", g=NG), bc(group[:, t, :], EG), ALU.mult))
                step(v.tensor_scalar(R2[:, :, 8:8 + NG], group, -MASKED, MASKED, ALU.mult, ALU.add))
                for t in range(NT):
                    step(v.tensor_tensor(OS.rearrange("p t (g e) -> p t g e", g=NG)[:, t, :, :], O14[:, t, :, :], bc(R2[:, t, 8:8 + NG], EG), ALU.add))
                dve.wait_ge(gexp_done, l + 1)
                step(v.tensor_reduce(gsm, R1[:, :, 0:NG], AX, ALU.add))
                step(v.reciprocal(pg, gsm))
                first_max(OS, O1, R1, v1, NE)
                step(v.scalar_tensor_tensor(out=OS, in0=O1, scalar=2 * MASKED, in1=OS, op0=ALU.mult, op1=ALU.add))
                first_max(OS, O2, R1, v2, NE)
                v.tensor_tensor(ex, v2, v1, ALU.subtract).then_inc(wexp_in, 1)
                v.tensor_tensor(OS, O1, O2, ALU.add).then_inc(onehot_ready, 1)
                v.memset(zero, 0.0).then_inc(zero_ready, 1)
                v.memset(Y[:, 512:1024], 0.0).then_inc(y_dve[l], 1)
                v.memset(SC, 0.0).then_inc(scat_ready[l], 1)
                dve.wait_ge(wexp_done, l + 1)
                vl = vals.rearrange("p (r t) -> p r t", t=NT)
                step(v.tensor_scalar(s1, ex, 1.0, None, ALU.add))
                step(v.reciprocal(s1, s1))
                step(v.tensor_tensor(vl[:, 2, :], s1, pg, ALU.mult))
                step(v.tensor_tensor(vl[:, 3, :], vl[:, 2, :], ex, ALU.mult))
                dve.wait_ge(rank_done, l + 1)
                step(v.tensor_tensor(CMP, bc(bank[7][:, 64:96], 7), mid(cst[:, C_THR:C_THR + 7], NE), ALU.is_gt))
                step(v.tensor_reduce(NBL, CMP, AX, ALU.add))
                step(v.tensor_scalar(NBL, NBL, 1.0, None, ALU.add))
                step(v.memset(BBF[:, 0:1], 0.0))
                step(v.tensor_tensor_scan(out=BBF[:, 1:NE + 1], data0=ones[:, 0:NE], data1=NBL, initial=0.0, op0=ALU.mult, op1=ALU.add))
                v.tensor_copy(tab[:, :], BBF).then_inc(table_ready, 1)
                for t in range(NT):
                    step(v.scalar_tensor_tensor(out=POSM[:, t, :], in0=BBF[:, 0:NE], scalar=float(BLK), in1=bank[7][:, 32 * t:32 * t + 32],
                                                op0=ALU.mult, op1=ALU.add))
                for r, o in enumerate((O1, O2)):
                    step(v.tensor_tensor(R1, o, POSM, ALU.mult))
                    step(v.tensor_reduce(vl[:, r, :], R1, AX, ALU.add))
                step(v.tensor_copy(PR, vals[:, 0:4]))
                step(v.tensor_copy(VP, cst[:, C_PMOD:C_PMOD + 1]))
                v.tensor_tensor(DG, mid(ident, 8), bc(vals, P), ALU.mult).then_inc(diag_ready, 1)
                dve.wait_ge(diag_ready, l + 1)

                def select(n, base):
                    v.tensor_tensor(SELQ, mid(iota32, 4), bc(PR, BLK), ALU.is_equal).then_inc(selstep[l], 1)
                    dve.wait_ge(selstep[l], base + 1)
                    v.tensor_tensor(SEL, SELQ[:, 0:2, :], SELQ[:, 2:4, :], ALU.add).then_inc(sel_ready[l], 1)
                    v.tensor_scalar(PR, PR, -float(BLK), None, ALU.add).then_inc(selstep[l], 1)

                select(0, 0)
                dve.wait_ge(rows_copied, l + 1)
                dve.wait_ge(table_ready, l + 1)
                total = dve.value_load(tab[0:1, NE:NE + 1], min_val=NE, max_val=48)
                with dve.Fori(0, total) as i:
                    own = 5 * i + 2
                    dve.wait_ge(gather_done[l], i + 1)
                    dve.wait_ge(selstep[l], own)
                    select(i + 1, own)
                    dve.wait_ge(up_done[l], i + 1)
                    v.tensor_copy(HU, bank[6][:, :]).then_inc(hu_ready[l], 1)
                    dve.wait_ge(silu_ready[l], i + 1)
                    v.tensor_tensor(HID, bank[7][:, P:2 * P].rearrange("p (f s) -> p f s", f=FC), SIL, ALU.mult).then_inc(hid_ready[l], 1)
                    dve.wait_ge(down_done[l], 2 * i + 2)
                    v.tensor_copy(Y[:, 512:1024], bank[6][:, :]).then_inc(y_dve[l], 1)
                    v.scalar_tensor_tensor(out=SC, in0=posrow[:, 0, :], scalar=VP, in1=wrow[:, 0, :], op0=ALU.is_equal, op1=ALU.mult).then_inc(selstep[l], 1)
                    v.scalar_tensor_tensor(out=SCT, in0=posrow[:, 1, :], scalar=VP, in1=wrow[:, 1, :], op0=ALU.is_equal, op1=ALU.mult).then_inc(selstep[l], 1)
                    dve.wait_ge(selstep[l], own + 4)
                    v.tensor_scalar(VP, VP, float(BLK), None, ALU.add).then_inc(selstep[l], 1)
                    v.tensor_tensor(SC, SC, SCT, ALU.add).then_inc(scat_ready[l], 1)
                dve.wait_ge(acc_done, l + 1)
                g = modvec(l, 5)
                for t in range(NT):
                    for n in range(2):
                        cols = slice(512 * n, 512 * n + 512)
                        step(v.tensor_tensor(otmp, bank[2 * t + n][:, :], g[:, cols], ALU.mult))
                        ins = v.tensor_tensor(xs[:, t, cols], xs[:, t, cols], otmp, ALU.add)
                        if n == 1 and t == 1:
                            ins.then_inc(x_ready, 1)
                        else:
                            step(ins)

            dve.wait_ge(const_in, 16)
            dve.wait_ge(x_in, 16 * 3)
            for l in range(DEPTH):
                norm(2 * l)
                copy_ht(2 * l)
                (hybrid, mlstm)[l]()
                residual(l, 0, modvec(l, 2))
                norm(2 * l + 1)
                copy_ht(2 * l + 1)
                ffn(l)


_INS = ['x', 'c', 'ada_w', 'ada_b', 'norm_mix', 'norm_ffn', 'hy_w_in', 'hy_q_norm', 'hy_k_norm', 'hy_conv_w', 'hy_w_out',
        'ml_w_in', 'ml_b_gates', 'ml_out_norm', 'ml_w_out', 'moe_w_group', 'moe_b_group', 'moe_w_expert', 'moe_b_expert',
        'moe_w_gate', 'moe_w_up', 'moe_w_down']


def kernel(**inputs):
    import numpy as _np
    import concourse.bacc as _bacc
    from concourse import mybir as _mybir
    from concourse.bass_utils import run_bass_kernel_spmd as _run

    nc = _bacc.Bacc("TRN2", target_bir_lowering=False, num_devices=1, dynamic_dma_scratch_size=4096)
    arrays, args = {}, []
    for name in _INS + ["consts"]:
        a = constant_table() if name == "consts" else _np.ascontiguousarray(inputs[name])
        arrays[f"in_{name}"] = a
        args.append(nc.dram_tensor(f"in_{name}", a.shape, _mybir.dt.from_np(a.dtype), kind="ExternalInput").ap())
    args.append(nc.dram_tensor("out_x", inputs["x"].shape, _mybir.dt.float32, kind="ExternalOutput").ap())
    decoder_kernel(nc, *args)
    r = _run(nc, [arrays], core_ids=[0])
    return r.results[0]["out_x"]
```

```python
from contextlib import ExitStack

import concourse.bass as bass
from concourse import mybir

F32 = mybir.dt.float32
I32 = mybir.dt.int32
ALU = mybir.AluOpType
ACT = mybir.ActivationFunctionType
AX = mybir.AxisListType.X

P = 128
SEQ = 256
NT = SEQ // P
D = 1024
KC = D // P
DEPTH = 2
HEADS = 8
HD = 64
TOPK = SEQ // 4
CONV = 512
VD = D // HEADS
NG, NE = 4, 32
EG = NE // NG
DE = 512
FC = DE // P
BLK = 32
EPS = 1e-6
MASKED = -1.0e30
EXTRA = 2 * SEQ // BLK - 1
STEPS = 8
TAKEN = -3.0e38
SLOT = 4096
NS = 9
UNROLL = NS // 3
GRP = UNROLL * BLK
GCUT = 512 // GRP

C_IDENT, C_ONES, C_ROWSUM, C_BIAS, C_LE, C_LT = 0, 128, 256, 416, 544, 672
C_CAUSAL, C_MASKT, C_IOTA, C_IDXM, C_THR, C_PMOD, C_ROPE = 800, 928, 1056, 1152, 1184, 1192, 1194
C_FOLD = C_BIAS
NCONST = C_ROPE + NT * 2 * (HD // 2)


def constant_table():
    import numpy as np
    t = np.zeros((P, NCONST), np.float32)
    p = np.arange(P)[:, None]
    f = np.arange(P)[None, :]
    t[:, C_IDENT:C_IDENT + P] = p == f
    t[:, C_ONES:C_ONES + P] = 1.0
    t[:, C_ROWSUM + 31:C_BIAS:BLK] = 1.0 / BLK
    t[:, C_BIAS:C_BIAS + P] = (p % BLK) == (f % BLK)
    t[:, C_LE:C_LE + P] = p <= f
    t[:, C_LT:C_LT + P] = p < f
    t[:, C_CAUSAL:C_CAUSAL + P] = np.where(f <= p, 0.0, MASKED)
    t[:, C_MASKT:C_MASKT + P] = np.where(p <= f, 0.0, MASKED)
    t[:, C_IOTA:C_IOTA + GRP] = np.arange(GRP)[None, :]
    t[:, C_IDXM:C_IDXM + NE] = np.arange(NE)[None, :] - 99.0
    t[:, C_THR:C_THR + 8] = BLK * np.arange(1, 9)[None, :]
    t[:, C_PMOD] = (np.arange(P) % BLK)
    t[:, C_PMOD + 1] = EPS
    inv = (np.float32(1.0) / np.power(np.float32(10000.0), np.arange(0, HD, 2, dtype=np.float32) / np.float32(HD))).astype(np.float32)
    ang = (np.arange(SEQ, dtype=np.float32)[:, None] * inv[None, :]).astype(np.float32)
    rope = np.stack([np.cos(ang), np.sin(ang)], 1).astype(np.float32)
    t[:, C_ROPE:] = rope.reshape(NT, P, 2 * (HD // 2)).transpose(1, 0, 2).reshape(P, -1)
    return t


def weight_stream():
    ada = [[("ada", l, n, 0) for n in range(12)] for l in range(DEPTH)]
    hy_cols = [(0, 512), (512, 512), (1024, 200), (1224, 512), (1736, 512), (2248, 512)]
    ml_cols = [(2048, 16), (0, 512), (512, 512), (1024, 512), (1536, 512), (2064, 512), (2576, 512)]
    out = [[("out", l, n, 0) for n in range(2)] for l in range(DEPTH)]
    s = ada[0][:6] + [("in", 0, a, n) for a, n in hy_cols] + ada[0][6:] + out[0] + ada[1][:6]
    s += [("experts", 0, 0, 0)]
    s += ada[1][6:10] + [("in", 1, a, n) for a, n in ml_cols] + out[1] + ada[1][10:]
    s += [("experts", 1, 0, 0)]
    return s


def decoder_kernel(nc, x, c, ada_w, ada_b, norm_mix, norm_ffn, hy_w_in, hy_q_norm, hy_k_norm, hy_conv_w,
                   hy_w_out, ml_w_in, ml_b_gates, ml_out_norm, ml_w_out, moe_w_group, moe_b_group,
                   moe_w_expert, moe_b_expert, moe_w_gate, moe_w_up, moe_w_down, consts, out):
    stream = weight_stream()
    at, n = {}, 0
    for piece in stream:
        at[piece] = n
        n += 3 * NE if piece[0] == "experts" else 1

    with ExitStack() as ctx:
        def sb(name, shape, dt=F32):
            return ctx.enter_context(nc.sbuf_tensor(name, shape, dt))

        def sem(name):
            return ctx.enter_context(nc.semaphore(name))

        bank = [ctx.enter_context(nc.psum_tensor(f"bank{i}", [P, 512], F32)) for i in range(8)]

        ring = [sb(f"ring{i}", [P, SLOT]) for i in range(NS)]
        xs = sb("xs", [P, NT, D])
        hbuf = sb("hbuf", [P, NT, D])
        hTb = sb("hTb", [P, KC * SEQ])
        modr = sb("modr", [P, 512])
        gam = sb("gam", [P, D])
        cst = sb("cst", [P, NCONST])
        RA = sb("RA", [P, 2560])
        RB = sb("RB", [P, 2560])
        RC = sb("RC", [P, 2048])
        RD = sb("RD", [P, 3072])
        modp = [RC[:, 512 * i:512 * i + 512] for i in range(2)]
        small = sb("small", [P, 256])
        rw = sb("rw", [P, KC, NG + NE])
        tab = sb("tab", [P, NE + 1], I32)

        hT = hTb[:, :].rearrange("p (k t) -> p k t", k=KC)
        h = hbuf[:, :, :].rearrange("q t (k p) -> q t k p", k=KC)
        ident = cst[:, C_IDENT:C_IDENT + P]
        ones = cst[:, C_ONES:C_ONES + P]
        fold = cst[:, C_FOLD:C_FOLD + BLK]
        tri_le = cst[:, C_LE:C_LE + P]
        tri_lt = cst[:, C_LT:C_LT + P]
        causal = cst[:, C_CAUSAL:C_CAUSAL + P]
        maskT = cst[:, C_MASKT:C_MASKT + P]
        iota32 = cst[:, C_IOTA:C_IOTA + BLK]
        iota_grp = cst[:, C_IOTA:C_IOTA + GRP]
        idxm = cst[:, C_IDXM:C_IDXM + NE]
        eps = cst[:, C_PMOD + 1:C_PMOD + 2]
        rope = cst[:, C_ROPE:NCONST].rearrange("p (t c j) -> p t c j", t=NT, c=2)

        cact = small[:, 0:8]
        ssq = small[:, 8:10]
        rstd = small[:, 10:12]
        brow = hbuf[0:24, 0, 0:512]
        gam9 = RD[:, 1408:1984].rearrange("p (g d) -> p g d", g=9)
        cwT = small[:, 12:24]
        cwr = RD[0:12, 1280:1408]
        bgate = small[:, 24:40]
        rb = small[:, 40:76]

        slot_full = [sem(f"slot_full{i}") for i in range(NS)]
        slot_used = [sem(f"slot_used{i}") for i in range(NS)]
        x_in = sem("x_in")
        const_in = sem("const_in")
        param_in = sem("param_in")
        gam_in = sem("gam_in")
        gam_free = sem("gam_free")
        rparam_in = sem("rparam_in")
        rparam_free = sem("rparam_free")
        out_done = sem("out_done")
        cact_ready = sem("cact_ready")
        brow_in = sem("brow_in")
        c_in = sem("c_in")
        part_done = sem("part_done")
        part_copied = sem("part_copied")
        rowsum_done = sem("rowsum_done")
        modr_ready = sem("modr_ready")
        scale_done = sem("scale_done")
        scale_read = sem("scale_read")
        shift_done = sem("shift_done")
        gatev_done = sem("gatev_done")
        gv_act = sem("gv_act")
        std_done = sem("std_done")
        gsc_ready = sem("gsc_ready")
        h_ready = sem("h_ready")
        ht_done = sem("ht_done")
        ht_act = sem("ht_act")
        ht_dve = sem("ht_dve")
        V = sem("dve_step")
        A = sem("act_step")
        proj_done = sem("proj_done")
        proj_act = sem("proj_act")
        proj_dve = sem("proj_dve")
        bg_act = sem("bg_act")
        vone_ready = sem("vone_ready")
        sq_ready = sem("sq_ready")
        qss_ready = sem("qss_ready")
        qstd_ready = sem("qstd_ready")
        q2_ready = sem("q2_ready")
        cwt_done = sem("cwt_done")
        cwt_act = sem("cwt_act")
        qt_done = sem("qt_done")
        qt_act = sem("qt_act")
        qt_dve = sem("qt_dve")
        score_done = sem("score_done")
        relu_done = sem("relu_done")
        relu_used = sem("relu_used")
        yconv_ready = sem("yconv_ready")
        logit_done = sem("logit_done")
        logit_read = sem("logit_read")
        max_ready = sem("max_ready")
        exp_done = sem("exp_done")
        probs_ready = sem("probs_ready")
        pt_done = sem("pt_done")
        pt_act = sem("pt_act")
        pt_dve = sem("pt_dve")
        pv_done = sem("pv_done")
        yt_act = sem("yt_act")
        yt_dve = sem("yt_dve")
        outp_done = sem("outp_done")
        x_ready = sem("x_ready")
        gates_ready = sem("gates_ready")
        absexp_done = sem("absexp_done")
        logf_ready = sem("logf_ready")
        cumf_done = sem("cumf_done")
        a_ready = sem("a_ready")
        at_done = sem("at_done")
        m_ready = sem("m_ready")
        mb_done = sem("mb_done")
        mbc_dve = sem("mbc_dve")
        mbc_act = sem("mbc_act")
        em_in = sem("em_in")
        em_ready = sem("em_ready")
        w_done = sem("w_done")
        st_done = sem("st_done")
        pw_ready = sem("pw_ready")
        num_done = sem("num_done")
        hn_ready = sem("hn_ready")
        hsq_done = sem("hsq_done")
        hss_ready = sem("hss_ready")
        hstd_done = sem("hstd_done")
        y_ready = sem("y_ready")
        yb_done = sem("yb_done")
        rlog_done = sem("rlog_done")
        gexp_in = sem("gexp_in")
        gexp_done = sem("gexp_done")
        wexp_in = sem("wexp_in")
        wexp_done = sem("wexp_done")
        onehot_ready = sem("onehot_ready")
        rank_done = sem("rank_done")
        table_ready = sem("table_ready")
        diag_ready = sem("diag_ready")
        rows_done = sem("rows_done")
        rows_copied = sem("rows_copied")
        zero_ready = sem("zero_ready")
        acc_done = sem("acc_done")

        def per_layer(name):
            return [sem(f"{name}_{l}") for l in range(DEPTH)]
        gate_done = per_layer("gate_done")
        up_done = per_layer("up_done")
        hg_ready = per_layer("hg_ready")
        hu_ready = per_layer("hu_ready")
        turn_done = per_layer("turn_done")
        silu_ready = per_layer("silu_ready")
        hid_ready = per_layer("hid_ready")
        down_done = per_layer("down_done")
        y_act = per_layer("y_act")
        y_dve = per_layer("y_dve")
        scat_ready = per_layer("scat_ready")
        next_sel = per_layer("next_sel")
        block_step = per_layer("block_step")
        group_step = per_layer("group_step")
        group_sel = per_layer("group_sel")
        group_done = per_layer("group_done")
        group_ready = per_layer("group_ready")
        extra_done = per_layer("extra_done")
        extra_xt = per_layer("extra_xt")

        patt = RA[:, 0:NT * 1224].rearrange("p (t n) -> p t n", t=NT)
        QT = RA[:, :].rearrange("p (c t) -> p c t", c=10)
        Q2 = RB[:, :].rearrange("p (t g d) -> p t g d", t=NT, g=20)
        qsq = RB[:, 0:NT * 576].rearrange("p (t g d) -> p t g d", t=NT, g=9)
        yT = RC[:, :].rearrange("p (c t) -> p c t", c=8)
        vv = RD[:, 0:NT * 72].rearrange("p (t n) -> p t n", t=NT)
        relu = [RB[:, 512 * i:512 * i + 512] for i in range(4)]
        score = RD[:, 256:512]
        work = RD[:, 512:768]
        selb = RD[:, 768:1280].rearrange("p (t s) -> p t s", t=NT)
        cgs = hbuf[:, 0, :].rearrange("p (c t) -> p c t", c=4)
        ctmp = hbuf[:, 1, :].rearrange("p (c t) -> p c t", c=4)
        logits = hTb[:, :].rearrange("p (h s) -> p h s", h=HEADS)
        PT = hbuf[:, :, :].rearrange("p k (h q) -> p k h q", h=HEADS)
        amax = small[:, 76:84]
        asum = small[:, 84:92]
        rsum = small[:, 92:100]
        qss = small[:, 100:118]
        qrs = small[:, 118:136]
        top8 = small[:, 136:144]
        wsc = small[:, 144:160].rearrange("p (t n) -> p t n", t=NT)
        otmp = RD[:, 2560:3072]
        gv = (RA[:, 0:D], RC[:, D:2 * D])

        qkT = RA[:, 0:2048].rearrange("p (c t) -> p c t", c=8)
        vx = RB[:, 0:NT * HEADS * (VD + 1)].rearrange("p (t h v) -> p t h v", t=NT, h=HEADS)
        ogs = hbuf
        MB0 = RD[:, 0:2048].rearrange("p (h t) -> p h t", h=HEADS)
        MB1 = RD[:, 2048:3072].rearrange("p (h t) -> p h t", h=HEADS)
        HN = RA[:, 0:2048].rearrange("p (t h v) -> p t h v", t=NT, h=HEADS)
        hsq = RC[:, :].rearrange("p (t h v) -> p t h v", t=NT, h=HEADS)
        gts = small[:, 76:108].rearrange("p (t n) -> p t n", t=NT)
        g3 = small[:, 108:124].rearrange("p (t n) -> p t n", t=NT)
        lf = small[:, 124:140].rearrange("p (t n) -> p t n", t=NT)
        cumf = small[:, 140:156].rearrange("p (t n) -> p t n", t=NT)
        asb = small[:, 156:172].rearrange("p (t n) -> p t n", t=NT)
        mrow = RA[0:HEADS, 2048:2560].rearrange("p (c t) -> p c t", c=2)
        em = small[:, 172:188].rearrange("p (t n) -> p t n", t=NT)
        den = small[:, 188:204].rearrange("p (t n) -> p t n", t=NT)
        hss = small[:, 204:220].rearrange("p (t n) -> p t n", t=NT)

        XT = RA[:, 0:KC * BLK].rearrange("p (k s) -> p k s", k=KC)
        HG = RA[:, 256:768]
        HU = RA[:, 768:1280]
        SIL = RA[:, 1280:1408].rearrange("p (f s) -> p f s", f=FC)
        HID = RA[:, 1408:1536].rearrange("p (f s) -> p f s", f=FC)
        SC = RA[:, 1536:1792]
        SCT = RA[:, 1792:2048]
        SEL = RA[:, 2048:2112].rearrange("p (t s) -> p t s", t=NT)
        SELQ = RA[:, 2112:2240].rearrange("p (c s) -> p c s", c=4)
        XG = hTb[:, 0:KC * GRP].rearrange("p (k s) -> p k s", k=KC)
        SELG = hTb[:, KC * GRP:(KC + NT) * GRP].rearrange("p (t s) -> p t s", t=NT)
        SELGQ = hTb[:, (KC + NT) * GRP:(KC + NT + 4) * GRP].rearrange("p (c s) -> p c s", c=4)
        Y = RB[:, 0:1024]
        posrow = RB[:, 1024:1536].rearrange("p (c t) -> p c t", c=2)
        wrow = RB[:, 1536:2048].rearrange("p (c t) -> p c t", c=2)
        DG = RC[:, 1024:2048].rearrange("p (r t) -> p r t", r=8)
        LG = RD[:, 0:72].rearrange("p (t n) -> p t n", t=NT)
        R1 = RD[:, 72:136].rearrange("p (t n) -> p t n", t=NT)
        R2 = RD[:, 136:200].rearrange("p (t n) -> p t n", t=NT)
        O1 = RD[:, 200:264].rearrange("p (t n) -> p t n", t=NT)
        O2 = RD[:, 264:328].rearrange("p (t n) -> p t n", t=NT)
        POSG = RD[:, 1280:1344].rearrange("p (t n) -> p t n", t=NT)
        OS = RD[:, 328:392].rearrange("p (t n) -> p t n", t=NT)
        CMP = RD[:, 392:392 + NE * 7].rearrange("p (e b) -> p e b", b=7)
        NBL = RD[:, 616:648]
        BBF = RD[:, 648:681]
        POSM = RD[:, 684:748].rearrange("p (t n) -> p t n", t=NT)
        zero = RD[:, 768:1280]
        s1 = small[:, 204:206]
        vals = small[:, 208:216]
        PR = small[:, 216:220]
        VP = small[:, 220:221]
        gmx, gsm, pg, v1, v2, ex = [small[:, 222 + 2 * i:224 + 2 * i] for i in range(6)]
        mnx = small[:, 234:236]
        PG = small[:, 236:240]

        qt_banks = (6, 7, 2, 3, 4, 5)
        score_banks = ((6, 7, 2, 3), (4, 5, 6, 7))
        logit_banks = ((4, 5, 6, 7), (2, 3, 4, 5))
        st_banks = (5, 6, 4, 7, 2, 3, 5, 6)
        num_banks = ((2, 3, 4), (5, 6, 7))
        ht_banks = (((4, 5), (6, 7)), ((4, 5), (6, 7)), ((4, 7), (2, 3)), ((4, 5), (6, 7)))
        scale_banks = ((0, 1), (0, 1), (4, 7), (0, 1))
        shift_banks = ((2, 3), (2, 3), (5, 6), (2, 3))

        def bc(ap, n):
            return ap.unsqueeze(2).to_broadcast([ap.shape[0], ap.shape[1], n])

        def mid(ap, n):
            return ap.unsqueeze(1).to_broadcast([ap.shape[0], n, ap.shape[1]])

        block = ctx.enter_context(nc.Block())

        @block.sync
        def _(sp):
            def load(n, turn, per_turn, src, cols, rows=KC):
                s = n % NS
                k = n // NS
                if turn is not None or k > 0:
                    sp.wait_ge(slot_used[s], k + turn * per_turn if turn is not None else k)
                dst = ring[s][:, 0:rows * cols].rearrange("p (k n) -> p k n", k=rows)
                sp.dma_start(dst, src).then_inc(slot_full[s], 16)

            for piece in stream:
                kind, l, a, w = piece
                n = at[piece]
                if kind == "ada":
                    load(n, None, 0, ada_w[l].rearrange("(p k) n -> p k n", k=KC)[:, :, 512 * a:512 * a + 512], 512)
                elif kind == "in":
                    src = hy_w_in[0] if l == 0 else ml_w_in[0]
                    load(n, None, 0, src.rearrange("(p k) n -> p k n", k=KC)[:, :, a:a + w], w)
                elif kind == "out":
                    src = hy_w_out[0] if l == 0 else ml_w_out[0]
                    load(n, None, 0, src.rearrange("(k p) n -> p k n", k=KC)[:, :, 512 * a:512 * a + 512], 512)
                else:
                    def load_expert(turn, u, e):
                        for j, m in enumerate((moe_w_gate, moe_w_up, moe_w_down)):
                            rows = FC if j == 2 else KC
                            src = m[l, bass.ds(e, 1)].rearrange("a (p k) n -> p (a k) n", k=rows)
                            load(n + 3 * u + j, turn, 1, src, m.shape[-1], rows)

                    with sp.Fori(0, NE // UNROLL) as turn:
                        for u in range(UNROLL):
                            load_expert(turn, u, turn * UNROLL + u)
                    for u in range(NE % UNROLL):
                        load_expert(NE // UNROLL, u, NE - NE % UNROLL + u)
            for t in range(NT):
                sp.wait_ge(x_ready, 2 * NT * DEPTH - NT + t + 1)
                sp.dma_start(out[0, t * P:(t + 1) * P, :], xs[:, t, :]).then_inc(out_done, 16)
            sp.wait_ge(out_done, 16 * NT)

        @block.gpsimd
        def _(pool):
            for t in range(NT):
                pool.dma_start(xs[:, t, :], x[0, t * P:(t + 1) * P, :]).then_inc(x_in, 16)
            pool.dma_start(gam9[:, 0:8, :], hy_q_norm.unsqueeze(1).to_broadcast([P, 8, HD])).then_inc(param_in, 16)
            pool.dma_start(gam9[:, 8, :], hy_k_norm.to_broadcast([P, HD])).then_inc(param_in, 16)
            pool.dma_start(cwr[:, :], hy_conv_w[0].rearrange("j (c p) -> (j c) p", p=P)).then_inc(param_in, 16)
            pool.dma_start(bgate, ml_b_gates.to_broadcast([P, 2 * HEADS])).then_inc(param_in, 16)
            gi = 0
            for l in range(DEPTH):
                for w in range(2):
                    if gi:
                        pool.wait_ge(gam_free, gi)
                    src = (norm_mix if w == 0 else norm_ffn)[l:l + 1, :]
                    pool.dma_start(gam[:, :], src.to_broadcast([P, D])).then_inc(gam_in, 16)
                    gi += 1
                    if l == 1 and w == 0:
                        pool.wait_ge(gam_free, gi)
                        pool.dma_start(gam[:, :], ml_out_norm.to_broadcast([P, D])).then_inc(gam_in, 16)
                        gi += 1
                if l:
                    pool.wait_ge(rparam_free, l)
                pool.dma_start(rw[:, :, 0:NG], moe_w_group[l].rearrange("(p k) n -> p k n", k=KC)).then_inc(rparam_in, 16)
                pool.dma_start(rw[:, :, NG:], moe_w_expert[l].rearrange("(p k) n -> p k n", k=KC)).then_inc(rparam_in, 16)
                pool.dma_start(rb[:, 0:NG], moe_b_group[l:l + 1, :].to_broadcast([P, NG])).then_inc(rparam_in, 16)
                pool.dma_start(rb[:, NG:], moe_b_expert[l:l + 1, :].to_broadcast([P, NE])).then_inc(rparam_in, 16)

        @block.tensor
        def _(pe):
            mm = nc.tensor.matmul
            state = {"mod": 0, "session": 0, "used": None}

            def landed(piece):
                n = at[piece]
                pe.wait_ge(slot_full[n % NS], 16 * (n // NS + 1))
                cols = piece[3] or 512
                return ring[n % NS][:, 0:KC * cols].rearrange("p (k n) -> p k n", k=KC), slot_used[n % NS]

            def behind(ins):
                if state["used"] is not None:
                    ins.then_inc(state["used"], 1)
                    state["used"] = None

            def mod_sum(i, first, last):
                pe.wait_ge(part_copied, i + 1)
                if first and i:
                    pe.wait_ge(modr_ready, state["session"])
                elif first:
                    pe.wait_ge(brow_in, 16)
                    mm(bank[1][:, :], cst[0:24, C_BIAS:C_BIAS + P], brow, start=True, stop=False)
                pick = cst[:, C_ROWSUM + 31 - i:C_ROWSUM + 31 - i + P]
                ins = mm(bank[1][:, :], pick, modp[i % 2], start=first and i > 0, stop=last)
                if last:
                    ins.then_inc(rowsum_done, 1)
                    state["session"] += 1
                else:
                    behind(ins)

            def mod_pieces(layer, js, opens, closes):
                before = None
                for j in js:
                    i = state["mod"]
                    w, used = landed(("ada", layer, j, 0))
                    if i:
                        pe.wait_ge(part_copied, i)
                    for k in range(KC):
                        g = k % 4
                        last = mm(bank[0][32 * g:32 * g + 32, :], cact[:, k:k + 1].to_broadcast([P, 32]), w[:, k, :],
                                  start=(k < 4), stop=(k >= 4))
                        if k == 0 and before is None:
                            behind(last)
                    last.then_inc(part_done, 1)
                    if before is not None:
                        mod_sum(before, opens and before == state["mod"] - 1 and j == js[1], False)
                    state["used"] = used
                    before = i
                    state["mod"] += 1
                mod_sum(before, False, closes)
                if closes:
                    mm(bank[0][0:32, 0:1], ident[:, 0:32], ident[:, 0:1], start=True, stop=True).then_inc(state["used"], 1)
                    state["used"] = None

            def spread(row, group, b):
                q = slice(32 * group, 32 * group + 32)
                return mm(bank[b][:, :], ident[q, 32 * group + row:32 * group + row + 1].to_broadcast([32, P]), modr[q, :],
                          start=True, stop=True)

            def spread_scale(q):
                l, w = q // 2, q % 2
                for n in range(2):
                    ins = spread(12 * l + 2 * (3 * w + 1) + n, n, scale_banks[q][n])
                ins.then_inc(scale_done, 1)

            def spread_shift(q):
                l, w = q // 2, q % 2
                for n in range(2):
                    ins = spread(12 * l + 2 * (3 * w) + n, 2 + n, shift_banks[q][n])
                    if n == 0:
                        behind(ins)
                ins.then_inc(shift_done, 1)

            def spread_gate(l, w, banks):
                for n in range(2):
                    ins = spread(12 * l + 2 * (3 * w + 2) + n, 2 + n, banks[n])
                ins.then_inc(gatev_done, 1)

            def transpose_h(q):
                for t in range(NT):
                    pe.wait_ge(h_ready, NT * q + t + 1)
                    for g in range(2):
                        for j in range(4):
                            last = nc.tensor.transpose(bank[ht_banks[q][t][g]][:, P * j:P * j + P], h[:, t, 4 * g + j, :], ident)
                        last.then_inc(ht_done, 1)

            def out_proj(l):
                pe.wait_ge(yt_act, 2 * (l + 1))
                if l == 0:
                    pe.wait_ge(yconv_ready, 1)
                else:
                    pe.wait_ge(yt_dve, 2)
                pe.wait_ge(modr_ready, 2 * (l + 1))
                spread_scale(2 * l + 1)
                spread_gate(l, 0, (2, 3))
                w, used = zip(*[landed(("out", l, n, 0)) for n in range(2)])
                for t in range(NT):
                    for n in range(2):
                        for k in range(KC):
                            last = mm(bank[4 + 2 * t + n][:, :], yT[:, k, t * P:(t + 1) * P], w[n][:, k, :],
                                      start=(k == 0), stop=(k == KC - 1))
                            if k == 0:
                                behind(last)
                        last.then_inc(outp_done, 1)
                        if t == 1:
                            state["used"] = used[n]
                pe.wait_ge(gv_act, 2 * l + 1)
                spread_shift(2 * l + 1)

            def project_tokens(piece, banks, n):
                w, used = landed(piece)
                for t in range(NT):
                    for k in range(KC):
                        last = mm(bank[banks[t][0]][:, banks[t][1]:banks[t][1] + n], hT[:, k, t * P:(t + 1) * P], w[:, k, :],
                                  start=(k == 0), stop=(k == KC - 1))
                        if t == 0 and k == 0:
                            behind(last)
                    last.then_inc(proj_done, 1)
                state["used"] = used

            def project_features(piece, banks):
                w, used = landed(piece)
                for f in range(4):
                    for k in range(KC):
                        last = mm(bank[banks[f // 2]][:, 256 * (f % 2):256 * (f % 2) + 256],
                                  w[:, k, P * f:P * f + P], hT[:, k, :], start=(k == 0), stop=(k == KC - 1))
                        if f == 0 and k == 0:
                            behind(last)
                    if f % 2:
                        last.then_inc(proj_done, 1)
                state["used"] = used

            def hybrid():
                l = 0
                pe.wait_ge(param_in, 16 * 4)
                nc.tensor.transpose(bank[1][:, 16:28], cwr, ident[0:12, 0:12]).then_inc(cwt_done, 1)
                pe.wait_ge(ht_act, 2)
                pe.wait_ge(ht_dve, 2)
                for i, (a, n) in enumerate([(0, 512), (512, 512), (1024, 200)]):
                    project_tokens(("in", 0, a, n), ((2 + 2 * i, 0), (3 + 2 * i, 0)), n)
                for i, a in enumerate((1224, 1736)):
                    pe.wait_ge(proj_act, i + 1)
                    pe.wait_ge(proj_dve, i + 1)
                    project_features(("in", 0, a, 512), (2 + 2 * i, 3 + 2 * i))
                pe.wait_ge(q2_ready, 2)
                pe.wait_ge(proj_act, 3)
                pe.wait_ge(proj_dve, 3)
                for t in range(NT):
                    for g in range(3):
                        if 3 * t + g == 2:
                            pe.wait_ge(bg_act, 2)
                        if 3 * t + g == 4:
                            pe.wait_ge(proj_act, 5)
                        for j in range(4 if g < 2 else 2):
                            ch = 4 * g + j
                            last = nc.tensor.transpose(bank[qt_banks[3 * t + g]][:, P * j:P * j + P], Q2[:, t, 2 * ch:2 * ch + 2, :], ident)
                        last.then_inc(qt_done, 1)
                pe.wait_ge(qt_act, 3)
                pe.wait_ge(qt_dve, 3)

                def head_products(t, first, key, signal, banks, b):
                    g, par = b // 2, b % 2
                    nk = P * (t + 1)
                    r = slice(64 * par, 64 * par + 64)
                    for i in range(2):
                        hd = 4 * g + 2 * i + par
                        last = mm(bank[banks[b]][:, 256 * i:256 * i + nk],
                                  QT[r, first + hd // 2, t * P:(t + 1) * P], QT[r, key, 0:nk], start=True, stop=True)
                    last.then_inc(signal, 1)
                for t in range(NT):
                    for b in range(4):
                        if t and b >= 2:
                            pe.wait_ge(relu_done, b - 1)
                        head_products(t, 5, 9, score_done, score_banks[t], b)
                pe.wait_ge(relu_done, 4)
                project_features(("in", 0, 2248, 512), (2, 3))
                mod_pieces(0, range(6, 12), True, True)
                pe.wait_ge(relu_done, 8)
                for t in range(NT):
                    if t:
                        pe.wait_ge(proj_dve, 4)
                    for b in range(4):
                        if t and b >= 2:
                            pe.wait_ge(logit_read, b - 1)
                        head_products(t, 0, 4, logit_done, logit_banks[t], b)
                pe.wait_ge(modr_ready, 2)
                ptn = 0
                for t in range(NT):
                    pe.wait_ge(probs_ready, t + 1)
                    for kt in range(t + 1):
                        for g in range(2):
                            if ptn >= 2:
                                pe.wait_ge((pt_act, pt_dve)[g], ptn // 2)
                            for j in range(4):
                                last = nc.tensor.transpose(bank[6 + g][:, P * j:P * j + P],
                                                           logits[:, 4 * g + j, kt * P:(kt + 1) * P], ident)
                            last.then_inc(pt_done, 1)
                            ptn += 1
                    pe.wait_ge(pt_act, ptn // 2)
                    pe.wait_ge(pt_dve, ptn // 2)
                    for par in range(2):
                        for kt in range(t + 1):
                            last = mm(bank[t][64 * par:64 * par + 64, :], vv[:, kt, 0:HD],
                                      PT[:, kt, par:HEADS:2, :], start=(kt == 0), stop=(kt == t))
                    last.then_inc(pv_done, 1)
                out_proj(l)

            def mlstm():
                l = 1
                pe.wait_ge(ht_act, 2 + 2 * 2)
                pe.wait_ge(ht_dve, 2 + 2 * 2)
                project_tokens(("in", 1, 2048, 16), ((4, 0), (4, 16)), 16)
                pe.wait_ge(modr_ready, 4)
                project_features(("in", 1, 0, 512), (0, 1))
                pe.wait_ge(logf_ready, 1)
                mm(bank[5][:, 0:8], tri_le, lf[:, 0, :], start=True, stop=True)
                mm(bank[5][:, 8:16], ones, lf[:, 0, :], start=True, stop=False)
                mm(bank[5][:, 8:16], tri_le, lf[:, 1, :], start=False, stop=True).then_inc(cumf_done, 1)
                project_features(("in", 1, 512, 512), (2, 3))
                pe.wait_ge(a_ready, 1)
                for t in range(NT):
                    last = nc.tensor.transpose(bank[6][0:8, t * P:(t + 1) * P], asb[:, t, :], ident)
                last.then_inc(at_done, 1)
                pe.wait_ge(gates_ready, 1)
                project_tokens(("in", 1, 1024, 512), ((4, 0), (7, 0)), 512)
                pe.wait_ge(m_ready, 1)
                for t in range(NT):
                    last = nc.tensor.transpose(bank[6][:, 256 + 8 * t:264 + 8 * t], mrow[:, 1, t * P:(t + 1) * P], ident[0:8, 0:8])
                last.then_inc(at_done, 1)
                pe.wait_ge(proj_act, 7)
                project_tokens(("in", 1, 1536, 512), ((2, 0), (3, 0)), 512)
                for hd in range(HEADS):
                    if hd == 4:
                        pe.wait_ge(proj_act, 9)
                        pe.wait_ge(proj_dve, 6)
                    last = mm(bank[hd // 2][:, 256 * (hd % 2):256 * (hd % 2) + 256],
                              ident[0:8, hd:hd + 1].to_broadcast([8, P]), mrow[:, 1, :], start=True, stop=True)
                    if hd == 0:
                        behind(last)
                    if hd % 2:
                        last.then_inc(mb_done, 1)
                pe.wait_ge(em_in, 1)
                for hd in range(HEADS):
                    if 4 <= hd < 6:
                        pe.wait_ge(mbc_act, hd - 1)
                    if hd >= 6:
                        pe.wait_ge(pw_ready, 2 * (hd - 5))
                    r = slice(64 * (hd % 2), 64 * (hd % 2) + 64)
                    b = bank[st_banks[hd]]
                    mm(b[:, 0:256], qkT[r, 4 + hd // 2, 0:P], qkT[r, hd // 2, :], start=True, stop=True)
                    mm(b[:, 256:384], qkT[r, 4 + hd // 2, P:], qkT[r, hd // 2, P:], start=True, stop=True).then_inc(st_done, 1)
                project_tokens(("in", 1, 2064, 512), ((0, 0), (1, 0)), 512)
                pe.wait_ge(pw_ready, 16)
                pe.wait_ge(vone_ready, 1)
                for t in range(NT):
                    for hd in range(HEADS):
                        b = bank[num_banks[t][hd // 3]]
                        o = b[:, 129 * (hd % 3):129 * (hd % 3) + 129]
                        if t == 0:
                            last = mm(o, MB0[:, hd, 0:P], vx[:, 0, hd, :], start=True, stop=True)
                        else:
                            mm(o, MB0[:, hd, P:], vx[:, 0, hd, :], start=True, stop=False)
                            last = mm(o, MB1[:, hd, :], vx[:, 1, hd, :], start=False, stop=True)
                        if hd in (2, 5, 7):
                            last.then_inc(num_done, 1)
                pe.wait_ge(proj_act, 10)
                project_tokens(("in", 1, 2576, 512), ((0, 0), (1, 0)), 512)
                for t in range(NT):
                    pe.wait_ge(y_ready, t + 1)
                    for g in range(2):
                        for j in range(4):
                            last = nc.tensor.transpose(bank[2 * t + g][:, P * j:P * j + P], HN[:, t, 4 * g + j, :], ident)
                        last.then_inc(yb_done, 1)
                out_proj(l)

            def ffn(l):
                pe.wait_ge(ht_act, 2 * (2 * l + 2))
                pe.wait_ge(ht_dve, 2 * (2 * l + 2))
                pe.wait_ge(rparam_in, 64 * (l + 1))
                for t in range(NT):
                    for k in range(KC):
                        last = mm(bank[6][:, 36 * t:36 * t + 36], hT[:, k, t * P:(t + 1) * P], rw[:, k, :],
                                  start=(k == 0), stop=(k == KC - 1))
                last.then_inc(rlog_done, 1)
                if l == 0:
                    mod_pieces(1, range(3, 6), False, True)
                pe.wait_ge(onehot_ready, l + 1)
                mm(bank[7][:, 0:32], tri_lt, OS[:, 0, :], start=True, stop=True)
                mm(bank[7][:, 32:64], ones, OS[:, 0, :], start=True, stop=False)
                mm(bank[7][:, 32:64], tri_lt, OS[:, 1, :], start=False, stop=True)
                mm(bank[7][:, 64:96], ones, OS[:, 0, :], start=True, stop=False)
                mm(bank[7][:, 64:96], ones, OS[:, 1, :], start=False, stop=True).then_inc(rank_done, 1)
                pe.wait_ge(zero_ready, l + 1)
                pe.wait_ge(modr_ready, 3 + 2 * l)
                for b in range(4):
                    mm(bank[b][:, :], zero[:, 0:P], zero, start=True, stop=True)

                def gather_group(g, half):
                    if half:
                        pe.wait_ge(group_ready[l], 2 * g + 1)
                    else:
                        pe.wait_ge(group_sel[l], g + 1)
                    chunks = range(GCUT, KC) if half else range(GCUT)
                    for k in chunks:
                        o = GRP * (k - chunks[0])
                        for t in range(NT):
                            last = mm(bank[4][:, o:o + GRP], h[:, t, k, :], SELG[:, t, :], start=(t == 0), stop=(t == NT - 1))
                    last.then_inc(group_done[l], 1)

                def gather_extra(v):
                    pe.wait_ge(next_sel[l], v)
                    for k in range(KC):
                        for t in range(NT):
                            last = mm(bank[4][:, BLK * k:BLK * k + BLK], h[:, t, k, :], SEL[:, t, :],
                                      start=(t == 0), stop=(t == NT - 1))
                    last.then_inc(extra_done[l], 1)

                def scatter(t, n):
                    return mm(bank[2 * t + n][:, :], SC[:, t * P:(t + 1) * P], Y[:, 512 * n:512 * n + 512],
                              start=False, stop=False, skip_group_check=True)

                def expert_block(v, tokens, weights, landed_expert, group=None):
                    pe.wait_ge(y_act[l], v + 1)
                    pe.wait_ge(y_dve[l], v + 1)
                    for j, (b, done) in enumerate(((5, gate_done[l]), (6, up_done[l]))):
                        w = weights[j]
                        landed_expert(j)
                        for k in range(KC):
                            g = k % 4
                            last = mm(bank[b][32 * g:32 * g + 32, :], tokens[:, k, :], w[:, k, :], start=(k < 4), stop=(k >= 4))
                        last.then_inc(done, 1)
                    if group is not None:
                        gather_group(group, 0)
                    pe.wait_ge(scat_ready[l], v + 1)
                    scatter(0, 0)
                    pe.wait_ge(hg_ready[l], v + 1)
                    for f in range(FC):
                        mm(bank[7][:, BLK * f:BLK * f + BLK], HG[:, f:DE:FC], fold, start=True, stop=True)
                    pe.wait_ge(hu_ready[l], v + 1)
                    for f in range(FC):
                        last = mm(bank[7][:, P + BLK * f:P + BLK * f + BLK], HU[:, f:DE:FC], fold, start=True, stop=True)
                    last.then_inc(turn_done[l], 1)
                    scatter(0, 1)
                    scatter(1, 0)
                    scatter(1, 1)
                    if group is not None:
                        gather_group(group, 1)
                    landed_expert(2)
                    pe.wait_ge(hid_ready[l], v + 1)
                    for n in range(2):
                        for f in range(FC):
                            last = mm(bank[5 + n][32 * f:32 * f + 32, :], HID[:, f, :], weights[2][:, f, 512 * n:512 * n + 512],
                                      start=True, stop=True)
                        last.then_inc(down_done[l], 1)

                gather_group(0, 0)
                gather_group(0, 1)
                pe.wait_ge(diag_ready, l + 1)
                for g in range(2):
                    last = mm(bank[5 + g][:, :], ones, DG[:, 4 * g:4 * g + 4, :], start=True, stop=True)
                last.then_inc(rows_done, 1)
                pe.wait_ge(table_ready, l + 1)
                n0 = at[("experts", l, 0, 0)]

                def expert(turn, u, more):
                    e = turn * UNROLL + u
                    x0 = pe.value_load(tab[0:1, bass.ds(e, 1)], min_val=0, max_val=EXTRA)
                    x1 = pe.value_load(tab[0:1, bass.ds(e + 1, 1)], min_val=0, max_val=EXTRA)
                    w = [ring[(n0 + 3 * u + j) % NS][:, :].rearrange("p (k n) -> p k n", k=FC if j == 2 else KC)
                         for j in range(3)]

                    def landed_expert(j):
                        n = n0 + 3 * u + j
                        pe.wait_ge(slot_full[n % NS], 16 * (n // NS + 1) + 16 * turn)

                    if u == 0:
                        pe.wait_ge(group_ready[l], 2 * turn + 2)
                    gathers = more and u == UNROLL - 1
                    expert_block(x0 + e, XG[:, :, BLK * u:BLK * u + BLK], w, landed_expert, turn + 1 if gathers else None)
                    with pe.If(x0 < x1):
                        with pe.Fori(x0, x1) as x:
                            if gathers:
                                pe.wait_ge(group_ready[l], 2 * turn + 4)
                            gather_extra(x + e + 1)
                            pe.wait_ge(extra_xt[l], x + 1)
                            expert_block(x + e + 1, XT, w, landed_expert)
                    for j in range(3):
                        mark_used7(slot_used[(n0 + 3 * u + j) % NS])

                with pe.Fori(0, NE // UNROLL) as turn:
                    for u in range(UNROLL):
                        expert(turn, u, True)
                for u in range(NE % UNROLL):
                    expert(NE // UNROLL, u, False)
                extra = pe.value_load(tab[0:1, NE:NE + 1], min_val=0, max_val=EXTRA)
                pe.wait_ge(y_act[l], extra + NE + 1)
                pe.wait_ge(y_dve[l], extra + NE + 1)
                pe.wait_ge(scat_ready[l], extra + NE + 1)
                for t in range(NT):
                    for n in range(2):
                        last = scatter(t, n)
                last.then_inc(acc_done, 1)
                spread_gate(l, 1, (5, 6))
                if l + 1 < DEPTH:
                    spread_scale(2 * l + 2)
                    pe.wait_ge(gv_act, 2 * l + 2)
                    spread_shift(2 * l + 2)

            def mark_used7(used):
                mm(bank[7][0:32, 256:257], ident[:, 0:32], ident[:, 0:1], start=True, stop=True).then_inc(used, 1)

            pe.wait_ge(const_in, 16)
            pe.wait_ge(cact_ready, 1)
            mod_pieces(0, range(6), True, True)
            pe.wait_ge(modr_ready, 1)
            spread_scale(0)
            spread_shift(0)
            for l in range(DEPTH):
                if l:
                    pe.wait_ge(x_ready, 2 * NT * l - NT + 1)
                    mod_pieces(l, range(6, 10), True, True)
                transpose_h(2 * l)
                (hybrid, mlstm)[l]()
                pe.wait_ge(scale_read, 2 * l + 2)
                mod_pieces(1, range(3) if l == 0 else range(10, 12), True, l == 1)
                transpose_h(2 * l + 1)
                ffn(l)

        @block.scalar
        def _(act):
            steps = [0]

            def step(ins):
                steps[0] += 1
                ins.then_inc(A, 1)
                act.wait_ge(A, steps[0])

            def copy(dst, src):
                return nc.scalar.activation(dst, src, ACT.Copy)

            modn = [0]

            def mod_pieces(n):
                for _ in range(n):
                    i = modn[0]
                    act.wait_ge(part_done, i + 1)
                    copy(modp[i % 2], bank[0][:, :]).then_inc(part_copied, 1)
                    modn[0] += 1

            def norm(q, pieces=0):
                for t in range(NT):
                    if q:
                        act.wait_ge(x_ready, NT * (q - 1) + t + 1)
                    step(nc.scalar.activation(RB[:, 0:D], xs[:, t, :], ACT.Square, accum_out=ssq[:, t:t + 1]))
                    nc.scalar.activation(rstd[:, t:t + 1], ssq[:, t:t + 1], ACT.Sqrt, scale=1.0 / D, bias=eps).then_inc(std_done, 1)
                    if pieces:
                        mod_pieces(1 if t == 0 else pieces - 1)

            def gate_vector(i, banks):
                act.wait_ge(gatev_done, i)
                for n in range(2):
                    ins = copy(gv[(i - 1) % 2][:, 512 * n:512 * n + 512], bank[banks[n]][:, :])
                ins.then_inc(gv_act, 1)

            def copy_ht(q):
                for t in range(NT):
                    act.wait_ge(ht_done, 4 * q + 2 * t + 1)
                    copy(hT[:, 0:4, t * P:(t + 1) * P], bank[ht_banks[q][t][0]][:, :].rearrange("p (k t) -> p k t", k=4)).then_inc(ht_act, 1)

            def hybrid():
                for i, (a, n) in enumerate(((0, 512), (512, 512), (1024, 200))):
                    act.wait_ge(proj_done, 2 * i + 1)
                    copy(patt[:, 0, a:a + n], bank[2 + 2 * i][:, 0:n]).then_inc(proj_act, 1)
                act.wait_ge(proj_act, 3)
                act.wait_ge(proj_dve, 3)
                for t in range(NT):
                    nc.scalar.activation(qsq[:, t, :, :], patt[:, t, 0:576].rearrange("p (g d) -> p g d", d=HD), ACT.Square).then_inc(sq_ready, 1)
                act.wait_ge(qss_ready, 1)
                nc.scalar.activation(qrs, qss, ACT.Sqrt, scale=1.0 / HD, bias=eps).then_inc(qstd_ready, 1)
                act.wait_ge(cwt_done, 1)
                copy(cwT, bank[1][:, 16:28]).then_inc(cwt_act, 1)
                for i in range(2):
                    act.wait_ge(proj_done, 7 + i)
                    copy(yT[:, 4 + 2 * i:6 + 2 * i, :], bank[2 + i][:, :].rearrange("p (c t) -> p c t", c=2)).then_inc(bg_act, 1)
                for i in range(2):
                    act.wait_ge(proj_done, 9 + i)
                    ins = copy(cgs[:, 2 * i:2 * i + 2, :], bank[4 + i][:, :].rearrange("p (c t) -> p c t", c=2))
                    ins.then_inc(proj_act, 1)
                for g in (0, 2, 4):
                    act.wait_ge(qt_done, g + 1)
                    t, c = g // 3, g % 3
                    m = 4 if c < 2 else 2
                    copy(QT[:, 4 * c:4 * c + m, t * P:(t + 1) * P],
                         bank[qt_banks[g]][:, 0:P * m].rearrange("p (c t) -> p c t", c=m)).then_inc(qt_act, 1)
                r = 0
                for t in range(NT):
                    nk = P * (t + 1)
                    for b in range(4):
                        act.wait_ge(score_done, 4 * t + b + 1)
                        if r >= 4:
                            act.wait_ge(relu_used, r - 3)
                        nc.scalar.activation(relu[r % 4].rearrange("p (i s) -> p i s", i=2)[:, :, 0:nk],
                                             bank[score_banks[t][b]][:, :].rearrange("p (i s) -> p i s", i=2)[:, :, 0:nk],
                                             ACT.Relu, scale=HD ** -0.5).then_inc(relu_done, 1)
                        r += 1
                mod_pieces(6)
                ptn = 0
                for t in range(NT):
                    nk = P * (t + 1)
                    act.wait_ge(max_ready, t + 1)
                    for hd in range(HEADS):
                        last = nc.scalar.activation(logits[:, hd, 0:nk], logits[:, hd, 0:nk], ACT.Exp, scale=HD ** -0.5,
                                                    bias=amax[:, hd:hd + 1], accum_out=asum[:, hd:hd + 1])
                    last.then_inc(exp_done, 1)
                    for kt in range(t + 1):
                        act.wait_ge(pt_done, 2 * ptn + 1)
                        copy(PT[:, kt, 0:4, :], bank[6][:, :].rearrange("p (h q) -> p h q", h=4)).then_inc(pt_act, 1)
                        ptn += 1
                    act.wait_ge(pv_done, t + 1)
                    copy(yT[:, 0:4, t * P:(t + 1) * P], bank[t][:, :].rearrange("p (c q) -> p c q", c=4)).then_inc(yt_act, 1)

            def mlstm():
                act.wait_ge(gates_ready, 1)
                step(nc.scalar.activation(g3, gts[:, :, 8:16], ACT.Abs))
                step(nc.scalar.activation(g3, g3, ACT.Exp, scale=-1.0))
                nc.scalar.activation(g3, g3, ACT.Ln, bias=1.0).then_inc(absexp_done, 1)
                for i in range(4):
                    act.wait_ge(proj_done, 14 + i + 1)
                    ins = copy(qkT[:, 2 * i:2 * i + 2, :], bank[i][:, :].rearrange("p (c t) -> p c t", c=2))
                    if i % 2:
                        ins.then_inc(proj_act, 1)
                for half, b in ((0, 4), (1, 2)):
                    act.wait_ge(proj_done, 19 + 2 * half)
                    copy(vx[:, 0, 4 * half:4 * half + 4, 0:VD], bank[b][:, :].rearrange("p (h v) -> p h v", h=4)).then_inc(proj_act, 1)
                act.wait_ge(em_in, 1)
                nc.scalar.activation(em, em, ACT.Exp, scale=-1.0).then_inc(em_ready, 1)
                for b in range(4):
                    act.wait_ge(mbc_dve, 2 * b + 2)
                    copy(MB0[:, 2 * b:2 * b + 2, P:], bank[b][:, :].rearrange("p (h t) -> p h t", h=2)[:, :, P:]).then_inc(mbc_act, 1)
                for b in range(4):
                    act.wait_ge(mbc_act, b + 1)
                    for hd in (2 * b, 2 * b + 1):
                        nc.scalar.activation(MB0[:, hd, :], MB0[:, hd, :], ACT.Exp, scale=-1.0, bias=asb[:, 0, hd:hd + 1]).then_inc(w_done, 1)
                        nc.scalar.activation(MB1[:, hd, :], MB1[:, hd, :], ACT.Exp, scale=-1.0, bias=asb[:, 1, hd:hd + 1]).then_inc(w_done, 1)

                def output_gate(half):
                    for t in range(NT):
                        act.wait_ge(proj_done, 23 + 2 * half + t)
                        ins = nc.scalar.activation(ogs[:, t, 512 * half:512 * half + 512], bank[t][:, :], ACT.Sigmoid)
                    ins.then_inc(proj_act, 1)

                output_gate(0)
                for t in range(NT):
                    act.wait_ge(hn_ready, t + 1)
                    nc.scalar.activation(hsq[:, t, :, :], HN[:, t, :, :], ACT.Square).then_inc(hsq_done, 1)
                act.wait_ge(hss_ready, 1)
                nc.scalar.activation(hss, hss, ACT.Sqrt, scale=1.0 / VD, bias=eps).then_inc(hstd_done, 1)
                output_gate(1)
                for t in range(NT):
                    act.wait_ge(yb_done, 2 * t + 1)
                    copy(yT[:, 0:4, t * P:(t + 1) * P], bank[2 * t][:, :].rearrange("p (c q) -> p c q", c=4)).then_inc(yt_act, 1)

            def ffn(l):
                act.wait_ge(gexp_in, l + 1)
                nc.scalar.activation(R1[:, :, 0:NG], R1[:, :, 0:NG], ACT.Exp).then_inc(gexp_done, 1)
                if l == 0:
                    mod_pieces(3)
                act.wait_ge(wexp_in, l + 1)
                nc.scalar.activation(ex, ex, ACT.Exp).then_inc(wexp_done, 1)

                def copy_group(g, half):
                    act.wait_ge(group_done[l], 2 * g + 1 + half)
                    c0, n = (GCUT, KC - GCUT) if half else (0, GCUT)
                    copy(XG[:, c0:c0 + n, :], bank[4][:, 0:n * GRP].rearrange("p (k s) -> p k s", k=n)).then_inc(group_ready[l], 1)

                copy_group(0, 0)
                copy_group(0, 1)
                act.wait_ge(rows_done, l + 1)
                copy(posrow, bank[5][:, :].rearrange("p (c t) -> p c t", c=2))
                copy(wrow, bank[6][:, :].rearrange("p (c t) -> p c t", c=2)).then_inc(rows_copied, 1)
                act.wait_ge(zero_ready, l + 1)
                copy(Y[:, 0:512], zero).then_inc(y_act[l], 1)

                def expert_block(v, group=None):
                    act.wait_ge(gate_done[l], v + 1)
                    copy(HG, bank[5][:, :]).then_inc(hg_ready[l], 1)
                    if group is not None:
                        copy_group(group, 0)
                    act.wait_ge(turn_done[l], v + 1)
                    nc.scalar.activation(SIL, bank[7][:, 0:P].rearrange("p (f s) -> p f s", f=FC), ACT.Exp, scale=-1.0).then_inc(silu_ready[l], 1)
                    if group is not None:
                        copy_group(group, 1)
                    act.wait_ge(down_done[l], 2 * v + 1)
                    copy(Y[:, 0:512], bank[5][:, :]).then_inc(y_act[l], 1)

                def expert(turn, u, more):
                    e = turn * UNROLL + u
                    x0 = act.value_load(tab[0:1, bass.ds(e, 1)], min_val=0, max_val=EXTRA)
                    x1 = act.value_load(tab[0:1, bass.ds(e + 1, 1)], min_val=0, max_val=EXTRA)
                    expert_block(x0 + e, turn + 1 if more and u == UNROLL - 1 else None)
                    with act.If(x0 < x1):
                        with act.Fori(x0, x1) as x:
                            act.wait_ge(extra_done[l], x + 1)
                            copy(XT, bank[4][:, 0:KC * BLK].rearrange("p (k s) -> p k s", k=KC)).then_inc(extra_xt[l], 1)
                            expert_block(x + e + 1)

                act.wait_ge(table_ready, l + 1)
                with act.Fori(0, NE // UNROLL) as turn:
                    for u in range(UNROLL):
                        expert(turn, u, True)
                for u in range(NE % UNROLL):
                    expert(NE // UNROLL, u, False)

            act.dma_start(cact, c[0].rearrange("(p k) -> p k", k=KC)).then_inc(c_in, 16)
            act.dma_start(cst[:, :], consts).then_inc(const_in, 16)
            act.dma_start(brow, ada_b.rearrange("l (r n) -> (l r) n", n=512)).then_inc(brow_in, 16)
            act.wait_ge(c_in, 16)
            nc.scalar.activation(cact, cact, ACT.Silu).then_inc(cact_ready, 1)
            mod_pieces(6)
            act.wait_ge(const_in, 16)
            act.wait_ge(x_in, 16 * NT)
            norm(0)
            for l in range(DEPTH):
                copy_ht(2 * l)
                (hybrid, mlstm)[l]()
                gate_vector(2 * l + 1, (2, 3))
                norm(2 * l + 1, 3 - l)
                copy_ht(2 * l + 1)
                ffn(l)
                gate_vector(2 * l + 2, (5, 6))
                if l + 1 < DEPTH:
                    norm(2 * l + 2, 4)

        @block.vector
        def _(dve):
            v = nc.vector
            steps = [0]

            def step(ins):
                steps[0] += 1
                ins.then_inc(V, 1)
                dve.wait_ge(V, steps[0])

            gain = [0]
            tiles = [0]

            def rows(s):
                dve.wait_ge(rowsum_done, s)
                if s == 1:
                    v.tensor_copy(modr[:, :], bank[1][:, :]).then_inc(modr_ready, 1)
                else:
                    v.tensor_tensor(modr[:, :], modr[:, :], bank[1][:, :], ALU.add).then_inc(modr_ready, 1)

            def gain_scale(q):
                dve.wait_ge(gam_in, 16 * (gain[0] + 1))
                dve.wait_ge(scale_done, q + 1)
                gain[0] += 1
                for n in range(2):
                    cols = slice(512 * n, 512 * n + 512)
                    ins = v.scalar_tensor_tensor(out=gam[:, cols], in0=bank[scale_banks[q][n]][:, :], scalar=1.0, in1=gam[:, cols],
                                                 op0=ALU.add, op1=ALU.mult)
                ins.then_inc(scale_read, 1)
                dve.wait_ge(scale_read, q + 1)

            def norm_tile(q, t):
                dve.wait_ge(std_done, NT * q + t + 1)
                step(v.reciprocal(rstd[:, t:t + 1], rstd[:, t:t + 1]))
                hv = h[:, t, :, :].rearrange("q k p -> q p k")
                ins = v.scalar_tensor_tensor(out=hv, in0=xs[:, t, :].rearrange("q (p k) -> q p k", k=KC), scalar=rstd[:, t:t + 1],
                                             in1=gam[:, :].rearrange("q (p k) -> q p k", k=KC), op0=ALU.mult, op1=ALU.mult)
                if t == NT - 1:
                    ins.then_inc(gam_free, 1)
                    dve.wait_ge(gam_free, gain[0])
                else:
                    step(ins)
                dve.wait_ge(shift_done, q + 1)
                for n in range(2):
                    hn = hv[:, 64 * n:64 * n + 64, :]
                    ins = v.tensor_tensor(hn, hn, bank[shift_banks[q][n]][:, :].rearrange("q (p k) -> q p k", k=KC), ALU.add)
                ins.then_inc(h_ready, 1)

            def copy_ht(q):
                for t in range(NT):
                    dve.wait_ge(ht_done, 4 * q + 2 * t + 2)
                    v.tensor_copy(hT[:, 4:8, t * P:(t + 1) * P], bank[ht_banks[q][t][1]][:, :].rearrange("p (k t) -> p k t", k=4)).then_inc(ht_dve, 1)

            def residual_tile(t, banks, gv):
                for n in range(2):
                    cols = slice(512 * n, 512 * n + 512)
                    step(v.tensor_tensor(otmp, bank[banks[n]][:, :], gv[:, cols], ALU.mult))
                    ins = v.tensor_tensor(xs[:, t, cols], xs[:, t, cols], otmp, ALU.add)
                    if n == 1:
                        ins.then_inc(x_ready, 1)
                        tiles[0] += 1
                        dve.wait_ge(x_ready, tiles[0])
                    else:
                        step(ins)

            def mixer_end(l):
                q = 2 * l + 1
                gain_scale(q)
                dve.wait_ge(gv_act, q)
                for t in range(NT):
                    dve.wait_ge(outp_done, 4 * l + 2 * t + 2)
                    residual_tile(t, (4 + 2 * t, 5 + 2 * t), gv[0])
                    norm_tile(q, t)

            def hybrid():
                for i, (a, n) in enumerate(((0, 512), (512, 512), (1024, 200))):
                    dve.wait_ge(proj_done, 2 * i + 2)
                    v.tensor_copy(patt[:, 1, a:a + n], bank[3 + 2 * i][:, 0:n]).then_inc(proj_dve, 1)
                dve.wait_ge(proj_act, 3)
                dve.wait_ge(proj_dve, 3)
                step(v.tensor_copy(vv[:, :, 0:HD], patt[:, :, 576:640]))
                step(v.tensor_scalar(wsc, patt[:, :, 1216:1224], float(HEADS) ** -0.5, None, ALU.mult))
                dve.wait_ge(sq_ready, 2)
                v.tensor_reduce(qss.rearrange("p (t g) -> p t g", t=NT), qsq, AX, ALU.add).then_inc(qss_ready, 1)
                dve.wait_ge(qstd_ready, 1)
                step(v.reciprocal(qrs, qrs))
                dve.wait_ge(param_in, 4 * 16)
                for t in range(NT):
                    qk = patt[:, t, 0:576].rearrange("p (g d) -> p g d", d=HD)
                    step(v.tensor_tensor(qk, qk, bc(qrs[:, 9 * t:9 * t + 9], HD), ALU.mult))
                    step(v.tensor_tensor(qk, qk, gam9[:, :, :], ALU.mult))
                for t in range(NT):
                    co = rope[:, t, 0, :].unsqueeze(1).to_broadcast([P, 9, HD // 2])
                    si = rope[:, t, 1, :].unsqueeze(1).to_broadcast([P, 9, HD // 2])
                    for g in range(2):
                        src = patt[:, t, 640 * g:640 * g + 576].rearrange("p (g c d) -> p g c d", c=2, d=HD // 2)
                        dst = Q2[:, t, 10 * g:10 * g + 9, :].rearrange("p g (c d) -> p g c d", c=2)
                        for o in range(2):
                            tm = RC[:, 288 * ((2 * g + o) % 3):288 * ((2 * g + o) % 3) + 288].rearrange("p (g d) -> p g d", d=HD // 2)
                            step(v.tensor_tensor(tm, src[:, :, 1 - o, :], si, ALU.mult))
                            step(v.tensor_tensor(dst[:, :, o, :], src[:, :, o, :], co, ALU.mult))
                            step(v.tensor_tensor(dst[:, :, o, :], dst[:, :, o, :], tm, ALU.subtract if o == 0 else ALU.add))
                        ins = v.tensor_copy(Q2[:, t, 10 * g + 9, :], Q2[:, t, 10 * g + 8, :])
                        if g == 1:
                            ins.then_inc(q2_ready, 1)
                        else:
                            step(ins)
                for g in (1, 3, 5):
                    dve.wait_ge(qt_done, g + 1)
                    t, c = g // 3, g % 3
                    m = 4 if c < 2 else 2
                    v.tensor_copy(QT[:, 4 * c:4 * c + m, t * P:(t + 1) * P],
                                  bank[qt_banks[g]][:, 0:P * m].rearrange("p (c t) -> p c t", c=m)).then_inc(qt_dve, 1)
                r = 0
                for t in range(NT):
                    nk = P * (t + 1)
                    sc = score[:, 0:nk]
                    if t:
                        step(v.memset(score[:, 0:P], 0.0))
                    step(v.tensor_copy(score[:, t * P:nk], causal))
                    for b in range(4):
                        dve.wait_ge(relu_done, r + 1)
                        for i in range(2):
                            hd = 4 * (b // 2) + 2 * i + b % 2
                            ins = v.scalar_tensor_tensor(out=sc, in0=relu[r % 4][:, 256 * i:256 * i + nk],
                                                         scalar=wsc[:, t, hd:hd + 1], in1=sc, op0=ALU.mult, op1=ALU.add)
                            if i == 0:
                                step(ins)
                        ins.then_inc(relu_used, 1)
                        dve.wait_ge(relu_used, r + 1)
                        r += 1
                    for rd in range(TOPK // 8):
                        src = sc if rd == 0 else work[:, 0:nk]
                        step(v.max(out=top8, in_=src))
                        step(v.match_replace(out=work[:, 0:nk], in_to_replace=top8, in_values=src, imm_value=TAKEN))
                    step(v.tensor_scalar(work[:, 0:nk], work[:, 0:nk], 0.5 * TAKEN, None, ALU.is_lt))
                    step(v.tensor_scalar(sc, sc, 0.1 * MASKED, None, ALU.is_gt))
                    step(v.tensor_tensor(sc, sc, work[:, 0:nk], ALU.mult))
                    step(v.tensor_scalar(selb[:, t, 0:nk], sc, -MASKED, MASKED, ALU.mult, ALU.add))
                dve.wait_ge(proj_act, 5)
                for i in range(2):
                    dve.wait_ge(proj_done, 11 + i)
                    ins = v.tensor_tensor(cgs[:, 2 * i:2 * i + 2, :], cgs[:, 2 * i:2 * i + 2, :],
                                          bank[2 + i][:, :].rearrange("p (c t) -> p c t", c=2), ALU.mult)
                ins.then_inc(proj_dve, 1)
                dve.wait_ge(proj_dve, 4)
                dve.wait_ge(cwt_act, 1)
                dve.wait_ge(bg_act, 2)
                for ch in range(4):
                    w = [cwT[:, 4 * j + ch:4 * j + ch + 1] for j in range(3)]
                    z = cgs[:, ch, :]
                    o = ctmp[:, ch, :]
                    step(v.tensor_scalar(o, z, w[2], None, ALU.mult))
                    for j in (1, 0):
                        d = 2 - j
                        step(v.scalar_tensor_tensor(out=o[:, d:], in0=z[:, 0:SEQ - d], scalar=w[j], in1=o[:, d:],
                                                    op0=ALU.mult, op1=ALU.add))
                v.tensor_tensor(yT[:, 4:8, :], yT[:, 4:8, :], ctmp, ALU.mult).then_inc(yconv_ready, 1)
                rows(2)
                ptn = 0
                for t in range(NT):
                    nk = P * (t + 1)
                    if t:
                        dve.wait_ge(pt_done, 2)
                    for b in range(4):
                        dve.wait_ge(logit_done, 4 * t + b + 1)
                        first = 4 * (b // 2) + b % 2
                        v.tensor_tensor(logits[:, first:first + 3:2, 0:nk],
                                        bank[logit_banks[t][b]][:, :].rearrange("p (i s) -> p i s", i=2)[:, :, 0:nk],
                                        mid(selb[:, t, 0:nk], 2), ALU.add).then_inc(logit_read, 1)
                    dve.wait_ge(logit_read, 4 * t + 4)
                    step(v.tensor_reduce(amax, logits[:, :, 0:nk], AX, ALU.max))
                    v.tensor_scalar(amax, amax, -(HD ** -0.5), None, ALU.mult).then_inc(max_ready, 1)
                    dve.wait_ge(exp_done, t + 1)
                    step(v.reciprocal(rsum, asum))
                    v.tensor_tensor(logits[:, :, 0:nk], logits[:, :, 0:nk], bc(rsum, nk), ALU.mult).then_inc(probs_ready, 1)
                    for kt in range(t + 1):
                        dve.wait_ge(pt_done, 2 * ptn + 2)
                        v.tensor_copy(PT[:, kt, 4:8, :], bank[7][:, :].rearrange("p (h q) -> p h q", h=4)).then_inc(pt_dve, 1)
                        ptn += 1

            def mlstm():
                rows(4)
                dve.wait_ge(proj_done, 14)
                step(v.tensor_tensor(gts, bank[4][:, 0:32].rearrange("p (t n) -> p t n", t=NT), mid(bgate, NT), ALU.add))
                v.tensor_scalar(lf, gts[:, :, 8:16], 0.0, None, ALU.min).then_inc(gates_ready, 1)
                dve.wait_ge(gates_ready, 1)
                v.memset(vx[:, :, :, VD:VD + 1], 1.0).then_inc(vone_ready, 1)
                dve.wait_ge(absexp_done, 1)
                v.tensor_tensor(lf, lf, g3, ALU.subtract).then_inc(logf_ready, 1)
                dve.wait_ge(cumf_done, 1)
                step(v.tensor_copy(cumf, bank[5][:, 0:16].rearrange("p (t n) -> p t n", t=NT)))
                v.tensor_tensor(asb, gts[:, :, 0:8], cumf, ALU.subtract).then_inc(a_ready, 1)
                dve.wait_ge(at_done, 1)
                step(v.tensor_copy(mrow[:, 0, :], bank[6][0:8, 0:SEQ]))
                v.tensor_tensor_scan(out=mrow[:, 1, :], data0=mrow[:, 0, :], data1=mrow[:, 0, :], initial=0.0, op0=ALU.max, op1=ALU.max).then_inc(m_ready, 1)
                dve.wait_ge(proj_done, 20)
                v.tensor_copy(vx[:, 1, 0:4, 0:VD], bank[7][:, :].rearrange("p (h v) -> p h v", h=4)).then_inc(proj_dve, 1)
                dve.wait_ge(at_done, 2)
                v.tensor_tensor(em, bank[6][:, 256:272].rearrange("p (t n) -> p t n", t=NT), cumf, ALU.add).then_inc(em_in, 1)
                dve.wait_ge(proj_done, 22)
                v.tensor_copy(vx[:, 1, 4:8, 0:VD], bank[3][:, :].rearrange("p (h v) -> p h v", h=4)).then_inc(proj_dve, 1)
                for b in range(4):
                    dve.wait_ge(mb_done, b + 1)
                    src = bank[b][:, :].rearrange("p (h t) -> p h t", h=2)
                    v.tensor_tensor(MB0[:, 2 * b:2 * b + 2, 0:P], src[:, :, 0:P], mid(maskT, 2), ALU.subtract).then_inc(mbc_dve, 1)
                    v.tensor_tensor(MB1[:, 2 * b:2 * b + 2, :], src[:, :, P:], mid(maskT, 2), ALU.subtract).then_inc(mbc_dve, 1)
                for hd in range(HEADS):
                    dve.wait_ge(st_done, hd + 1)
                    dve.wait_ge(w_done, 2 * hd + 2)
                    v.scalar_tensor_tensor(out=MB0[:, hd, :], in0=bank[st_banks[hd]][:, 0:256], scalar=HD ** -0.5, in1=MB0[:, hd, :],
                                           op0=ALU.mult, op1=ALU.mult).then_inc(pw_ready, 1)
                    v.scalar_tensor_tensor(out=MB1[:, hd, :], in0=bank[st_banks[hd]][:, 256:384], scalar=HD ** -0.5, in1=MB1[:, hd, :],
                                           op0=ALU.mult, op1=ALU.mult).then_inc(pw_ready, 1)
                dve.wait_ge(em_ready, 1)
                for t in range(NT):
                    for i, m in enumerate((3, 3, 2)):
                        dve.wait_ge(num_done, 3 * t + i + 1)
                        src = bank[num_banks[t][i]][:, 0:129 * m].rearrange("p (h v) -> p h v", h=m)
                        dn = den[:, t, 3 * i:3 * i + m]
                        dsum = src[:, :, VD:VD + 1].rearrange("p h o -> p (h o)")
                        step(v.tensor_scalar(dn, dsum, -1.0, None, ALU.mult))
                        step(v.tensor_tensor(dn, dn, dsum, ALU.max))
                        step(v.tensor_tensor(dn, dn, em[:, t, 3 * i:3 * i + m], ALU.max))
                        step(v.reciprocal(dn, dn))
                        ins = v.tensor_tensor(HN[:, t, 3 * i:3 * i + m, :], src[:, :, 0:VD], bc(dn, VD), ALU.mult)
                        if i == 2:
                            ins.then_inc(hn_ready, 1)
                    dve.wait_ge(hsq_done, t + 1)
                    ins = v.tensor_reduce(hss[:, t, :], hsq[:, t, :, :], AX, ALU.add)
                    if t:
                        ins.then_inc(hss_ready, 1)
                dve.wait_ge(hstd_done, 1)
                step(v.reciprocal(hss, hss))
                dve.wait_ge(gam_in, 16 * (gain[0] + 1))
                gain[0] += 1
                for t in range(NT):
                    step(v.tensor_tensor(HN[:, t, :, :], HN[:, t, :, :], bc(hss[:, t, :], VD), ALU.mult))
                    flat = HN[:, t, :, :].rearrange("p h v -> p (h v)")
                    step(v.tensor_tensor(flat, flat, gam[:, :], ALU.mult))
                    if t == 0:
                        dve.wait_ge(proj_act, 11)
                    v.tensor_tensor(flat, flat, ogs[:, t, :], ALU.mult).then_inc(y_ready, 1)
                dve.wait_ge(y_ready, 2)
                v.memset(small[:, 250:251], 0.0).then_inc(gam_free, 1)
                for t in range(NT):
                    dve.wait_ge(yb_done, 2 * t + 2)
                    v.tensor_copy(yT[:, 4:8, t * P:(t + 1) * P], bank[2 * t + 1][:, :].rearrange("p (c q) -> p c q", c=4)).then_inc(yt_dve, 1)

            def first_max(val, onehot, scratch, top, n):
                step(v.tensor_reduce(top, val, AX, ALU.max))
                step(v.tensor_tensor(scratch, val, bc(top, n), ALU.is_equal))
                step(v.tensor_tensor(scratch, scratch, mid(idxm[:, 0:n], NT), ALU.mult))
                step(v.tensor_reduce(mnx, scratch, AX, ALU.min))
                step(v.tensor_tensor(onehot, mid(idxm[:, 0:n], NT), bc(mnx, n), ALU.is_equal))

            def ffn(l):
                dve.wait_ge(rlog_done, l + 1)
                dve.wait_ge(rparam_in, 64 * (l + 1))
                step(v.tensor_tensor(LG, bank[6][:, 0:72].rearrange("p (t n) -> p t n", t=NT), mid(rb, NT), ALU.add))
                v.memset(small[:, 250:251], 0.0).then_inc(rparam_free, 1)
                first_max(LG[:, :, 0:NG], R2[:, :, 0:NG], R1[:, :, 0:NG], gmx, NG)
                v.tensor_tensor(R1[:, :, 0:NG], LG[:, :, 0:NG], bc(gmx, NG), ALU.subtract).then_inc(gexp_in, 1)
                group = R2[:, :, 0:NG]
                O14 = O1.rearrange("p t (g e) -> p t g e", g=NG)
                for t in range(NT):
                    step(v.tensor_tensor(O14[:, t, :, :], LG[:, t, NG:].rearrange("p (g e) -> p g e", g=NG), bc(group[:, t, :], EG), ALU.mult))
                step(v.tensor_scalar(R2[:, :, 8:8 + NG], group, -MASKED, MASKED, ALU.mult, ALU.add))
                for t in range(NT):
                    step(v.tensor_tensor(OS.rearrange("p t (g e) -> p t g e", g=NG)[:, t, :, :], O14[:, t, :, :], bc(R2[:, t, 8:8 + NG], EG), ALU.add))
                dve.wait_ge(gexp_done, l + 1)
                step(v.tensor_reduce(gsm, R1[:, :, 0:NG], AX, ALU.add))
                step(v.reciprocal(pg, gsm))
                first_max(OS, O1, R1, v1, NE)
                step(v.scalar_tensor_tensor(out=OS, in0=O1, scalar=2 * MASKED, in1=OS, op0=ALU.mult, op1=ALU.add))
                first_max(OS, O2, R1, v2, NE)
                v.tensor_tensor(ex, v2, v1, ALU.subtract).then_inc(wexp_in, 1)
                v.tensor_tensor(OS, O1, O2, ALU.add).then_inc(onehot_ready, 1)
                v.memset(zero, 0.0).then_inc(zero_ready, 1)
                v.memset(Y[:, 512:1024], 0.0).then_inc(y_dve[l], 1)
                v.memset(SC, 0.0).then_inc(scat_ready[l], 1)
                rows(3 + 2 * l)
                vl = vals.rearrange("p (r t) -> p r t", t=NT)
                dve.wait_ge(rank_done, l + 1)
                rank = bank[7][:, 0:64].rearrange("p (t n) -> p t n", t=NT)
                step(v.tensor_scalar(POSG, rank, BLK - 0.5, 1.0e6, ALU.is_gt, ALU.mult))
                step(v.tensor_tensor(POSG, POSG, rank, ALU.add))
                step(v.scalar_tensor_tensor(out=POSG, in0=mid(idxm, NT), scalar=float(BLK), in1=POSG, op0=ALU.mult, op1=ALU.add))
                for r, o in enumerate((O1, O2)):
                    step(v.tensor_tensor(R1, o, POSG, ALU.mult))
                    step(v.tensor_reduce(PG[:, 2 * r:2 * r + 2], R1, AX, ALU.add))
                step(v.tensor_scalar(PG, PG, 99.0 * BLK, None, ALU.add))

                def select_group(g):
                    v.tensor_tensor(SELGQ, mid(iota_grp, 4), bc(PG, GRP), ALU.is_equal).then_inc(group_step[l], 1)
                    dve.wait_ge(group_step[l], 2 * g + 1)
                    v.tensor_tensor(SELG, SELGQ[:, 0:2, :], SELGQ[:, 2:4, :], ALU.add).then_inc(group_sel[l], 1)
                    v.tensor_scalar(PG, PG, -float(GRP), None, ALU.add).then_inc(group_step[l], 1)

                select_group(0)
                step(v.tensor_tensor(CMP, bc(bank[7][:, 64:96], 7), mid(cst[:, C_THR:C_THR + 7], NE), ALU.is_gt))
                step(v.tensor_reduce(NBL, CMP, AX, ALU.add))
                step(v.tensor_scalar(NBL, NBL, 1.0, None, ALU.add))
                step(v.memset(BBF[:, 0:1], 0.0))
                step(v.tensor_tensor_scan(out=BBF[:, 1:NE + 1], data0=ones[:, 0:NE], data1=NBL, initial=0.0, op0=ALU.mult, op1=ALU.add))
                v.tensor_tensor(tab[:, :], BBF, iota_grp[:, 0:NE + 1], ALU.subtract).then_inc(table_ready, 1)
                for t in range(NT):
                    step(v.scalar_tensor_tensor(out=POSM[:, t, :], in0=BBF[:, 0:NE], scalar=float(BLK), in1=bank[7][:, 32 * t:32 * t + 32],
                                                op0=ALU.mult, op1=ALU.add))
                for r, o in enumerate((O1, O2)):
                    step(v.tensor_tensor(R1, o, POSM, ALU.mult))
                    step(v.tensor_reduce(vl[:, r, :], R1, AX, ALU.add))
                dve.wait_ge(wexp_done, l + 1)
                step(v.tensor_scalar(s1, ex, 1.0, None, ALU.add))
                step(v.reciprocal(s1, s1))
                step(v.tensor_tensor(vl[:, 2, :], s1, pg, ALU.mult))
                step(v.tensor_tensor(vl[:, 3, :], vl[:, 2, :], ex, ALU.mult))
                step(v.tensor_copy(PR, vals[:, 0:4]))
                step(v.tensor_copy(VP, cst[:, C_PMOD:C_PMOD + 1]))
                v.tensor_tensor(DG, mid(ident, 8), bc(vals, P), ALU.mult).then_inc(diag_ready, 1)
                dve.wait_ge(diag_ready, l + 1)

                def expert_block(n, group=None):
                    own = STEPS * n
                    dve.wait_ge(up_done[l], n + 1)
                    v.tensor_copy(HU, bank[6][:, :]).then_inc(hu_ready[l], 1)
                    v.tensor_scalar(PR, PR, -float(BLK), None, ALU.add).then_inc(block_step[l], 1)
                    dve.wait_ge(block_step[l], own + 1)
                    v.tensor_tensor(SELQ, mid(iota32, 4), bc(PR, BLK), ALU.is_equal).then_inc(block_step[l], 1)
                    dve.wait_ge(block_step[l], own + 2)
                    v.tensor_tensor(SEL, SELQ[:, 0:2, :], SELQ[:, 2:4, :], ALU.add).then_inc(next_sel[l], 1)
                    dve.wait_ge(silu_ready[l], n + 1)
                    gate = bank[7][:, 0:P].rearrange("p (f s) -> p f s", f=FC)
                    up = bank[7][:, P:2 * P].rearrange("p (f s) -> p f s", f=FC)
                    v.tensor_scalar(SIL, SIL, 1.0, None, ALU.add).then_inc(block_step[l], 1)
                    dve.wait_ge(block_step[l], own + 3)
                    v.reciprocal(SIL, SIL).then_inc(block_step[l], 1)
                    dve.wait_ge(block_step[l], own + 4)
                    v.tensor_tensor(SIL, gate, SIL, ALU.mult).then_inc(block_step[l], 1)
                    dve.wait_ge(block_step[l], own + 5)
                    v.tensor_tensor(HID, up, SIL, ALU.mult).then_inc(hid_ready[l], 1)
                    dve.wait_ge(down_done[l], 2 * n + 2)
                    v.tensor_copy(Y[:, 512:1024], bank[6][:, :]).then_inc(y_dve[l], 1)
                    v.scalar_tensor_tensor(out=SC, in0=posrow[:, 0, :], scalar=VP, in1=wrow[:, 0, :], op0=ALU.is_equal, op1=ALU.mult).then_inc(block_step[l], 1)
                    v.scalar_tensor_tensor(out=SCT, in0=posrow[:, 1, :], scalar=VP, in1=wrow[:, 1, :], op0=ALU.is_equal, op1=ALU.mult).then_inc(block_step[l], 1)
                    dve.wait_ge(block_step[l], own + 7)
                    v.tensor_tensor(SC, SC, SCT, ALU.add).then_inc(scat_ready[l], 1)
                    v.tensor_scalar(VP, VP, float(BLK), None, ALU.add).then_inc(block_step[l], 1)
                    if group is not None:
                        select_group(group)

                def expert(turn, u, more):
                    e = turn * UNROLL + u
                    x0 = dve.value_load(tab[0:1, bass.ds(e, 1)], min_val=0, max_val=EXTRA)
                    x1 = dve.value_load(tab[0:1, bass.ds(e + 1, 1)], min_val=0, max_val=EXTRA)
                    expert_block(x0 + e, turn + 1 if more and u == 0 else None)
                    with dve.If(x0 < x1):
                        with dve.Fori(x0, x1) as x:
                            expert_block(x + e + 1)

                dve.wait_ge(rows_copied, l + 1)
                dve.wait_ge(table_ready, l + 1)
                with dve.Fori(0, NE // UNROLL) as turn:
                    for u in range(UNROLL):
                        expert(turn, u, True)
                for u in range(NE % UNROLL):
                    expert(NE // UNROLL, u, False)
                if l + 1 < DEPTH:
                    gain_scale(2 * l + 2)
                dve.wait_ge(gv_act, 2 * l + 2)
                dve.wait_ge(acc_done, l + 1)
                for t in range(NT):
                    residual_tile(t, (2 * t, 2 * t + 1), gv[1])
                    if l + 1 < DEPTH:
                        norm_tile(2 * l + 2, t)

            dve.wait_ge(const_in, 16)
            rows(1)
            gain_scale(0)
            dve.wait_ge(x_in, 16 * NT)
            for t in range(NT):
                norm_tile(0, t)
            for l in range(DEPTH):
                copy_ht(2 * l)
                (hybrid, mlstm)[l]()
                mixer_end(l)
                copy_ht(2 * l + 1)
                ffn(l)



_INS = ['x', 'c', 'ada_w', 'ada_b', 'norm_mix', 'norm_ffn', 'hy_w_in', 'hy_q_norm', 'hy_k_norm', 'hy_conv_w', 'hy_w_out',
        'ml_w_in', 'ml_b_gates', 'ml_out_norm', 'ml_w_out', 'moe_w_group', 'moe_b_group', 'moe_w_expert', 'moe_b_expert',
        'moe_w_gate', 'moe_w_up', 'moe_w_down']


def kernel(**inputs):
    import numpy as _np
    import concourse.bacc as _bacc
    from concourse import mybir as _mybir
    from concourse.bass_utils import run_bass_kernel_spmd as _run

    nc = _bacc.Bacc("TRN2", target_bir_lowering=False, num_devices=1, dynamic_dma_scratch_size=2048)
    arrays, args = {}, []
    for name in _INS + ["consts"]:
        a = constant_table() if name == "consts" else _np.ascontiguousarray(inputs[name])
        arrays[f"in_{name}"] = a
        args.append(nc.dram_tensor(f"in_{name}", a.shape, _mybir.dt.from_np(a.dtype), kind="ExternalInput").ap())
    args.append(nc.dram_tensor("out_x", inputs["x"].shape, _mybir.dt.float32, kind="ExternalOutput").ap())
    decoder_kernel(nc, *args)
    r = _run(nc, [arrays], core_ids=[0])
    return r.results[0]["out_x"]
```

```python
from contextlib import ExitStack

import concourse.bass as bass
from concourse import mybir

F32 = mybir.dt.float32
I32 = mybir.dt.int32
ALU = mybir.AluOpType
ACT = mybir.ActivationFunctionType
AX = mybir.AxisListType.X

P = 128
SEQ = 256
NT = SEQ // P
D = 1024
KC = D // P
DEPTH = 2
HEADS = 8
HD = 64
TOPK = SEQ // 4
CONV = 512
VD = D // HEADS
NG, NE = 4, 32
EG = NE // NG
DE = 512
FC = DE // P
BLK = 32
EPS = 1e-6
MASKED = -1.0e30
EXTRA = 2 * SEQ // BLK - 1
STEPS = 8
TAKEN = -3.0e38
SLOT = 4096
NS = 9
UNROLL = NS // 3
GRP = UNROLL * BLK
GCUT = 512 // GRP

C_IDENT, C_ONES, C_FOLD, C_LE, C_LT = 0, 128, 256, 384, 512
C_CAUSAL, C_MASKT, C_IOTA, C_IDXM, C_THR, C_PMOD, C_ROPE = 640, 768, 896, 992, 1024, 1031, 1032
NCONST = C_ROPE + NT * 2 * (HD // 2)


def constant_table():
    import numpy as np
    t = np.zeros((P, NCONST), np.float32)
    p = np.arange(P)[:, None]
    f = np.arange(P)[None, :]
    t[:, C_IDENT:C_IDENT + P] = p == f
    t[:, C_ONES:C_ONES + P] = 1.0
    t[:, C_FOLD:C_FOLD + P] = (p % BLK) == (f % BLK)
    t[:, C_LE:C_LE + P] = p <= f
    t[:, C_LT:C_LT + P] = p < f
    t[:, C_CAUSAL:C_CAUSAL + P] = np.where(f <= p, 0.0, MASKED)
    t[:, C_MASKT:C_MASKT + P] = np.where(p <= f, 0.0, MASKED)
    t[:, C_IOTA:C_IOTA + GRP] = np.arange(GRP)[None, :]
    t[:, C_IDXM:C_IDXM + NE] = np.arange(NE)[None, :] - 99.0
    t[:, C_THR:C_THR + 7] = BLK * np.arange(1, 8)[None, :]
    t[:, C_PMOD] = (np.arange(P) % BLK)
    inv = (np.float32(1.0) / np.power(np.float32(10000.0), np.arange(0, HD, 2, dtype=np.float32) / np.float32(HD))).astype(np.float32)
    ang = (np.arange(SEQ, dtype=np.float32)[:, None] * inv[None, :]).astype(np.float32)
    rope = np.stack([np.cos(ang), np.sin(ang)], 1).astype(np.float32)
    t[:, C_ROPE:] = rope.reshape(NT, P, 2 * (HD // 2)).transpose(1, 0, 2).reshape(P, -1)
    return t


def weight_stream():
    ada = [[("ada", l, n, 0) for n in range(12)] for l in range(DEPTH)]
    hy = [("in", 0, a, n) for a, n in ((0, 512), (512, 512), (1024, 200), (1224, 512), (1736, 512), (2248, 512))]
    ml = [("in", 1, a, n) for a, n in ((2048, 16), (0, 512), (512, 512), (1024, 512), (1536, 512), (2064, 512), (2576, 512))]
    out = [[("out", l, n, 0) for n in range(2)] for l in range(DEPTH)]
    s = ada[0][:4] + hy[:4] + ada[0][4:6] + hy[4:] + ada[0][6:] + out[0] + ada[1][:6]
    s += [("experts", 0, 0, 0)]
    s += ada[1][6:8] + ml + ada[1][8:10] + out[1] + ada[1][10:]
    s += [("experts", 1, 0, 0)]
    return s


def decoder_kernel(nc, x, c, ada_w, ada_b, norm_mix, norm_ffn, hy_w_in, hy_q_norm, hy_k_norm, hy_conv_w,
                   hy_w_out, ml_w_in, ml_b_gates, ml_out_norm, ml_w_out, moe_w_group, moe_b_group,
                   moe_w_expert, moe_b_expert, moe_w_gate, moe_w_up, moe_w_down, consts, out):
    stream = weight_stream()
    at, n = {}, 0
    for piece in stream:
        at[piece] = n
        n += 3 * NE if piece[0] == "experts" else 1

    with ExitStack() as ctx:
        def sb(name, shape, dt=F32):
            return ctx.enter_context(nc.sbuf_tensor(name, shape, dt))

        def sem(name):
            return ctx.enter_context(nc.semaphore(name))

        bank = [ctx.enter_context(nc.psum_tensor(f"bank{i}", [P, 512], F32)) for i in range(8)]

        ring = [sb(f"ring{i}", [P, SLOT]) for i in range(NS)]
        xs = sb("xs", [P, NT, D])
        hbuf = sb("hbuf", [P, NT, D])
        hTb = sb("hTb", [P, KC * SEQ])
        modr = sb("modr", [P, 512])
        gam = sb("gam", [P, D])
        cst = sb("cst", [P, NCONST])
        RA = sb("RA", [P, 2560])
        RB = sb("RB", [P, 2560])
        RC = sb("RC", [P, 2048])
        RD = sb("RD", [P, 3072])
        modp = [RC[:, 0:512]] * 4 + [hTb[:, 0:512], RC[:, 0:512]]
        cz = sb("cz", [P, BLK * KC + 23])
        small = sb("small", [P, 240])
        rw = sb("rw", [P, KC, NG + NE])
        tab = sb("tab", [P, NE + 1], I32)

        hT = hTb[:, :].rearrange("p (k t) -> p k t", k=KC)
        h = hbuf[:, :, :].rearrange("q t (k p) -> q t k p", k=KC)
        ident = cst[:, C_IDENT:C_IDENT + P]
        ones = cst[:, C_ONES:C_ONES + P]
        fold_all = cst[:, C_FOLD:C_FOLD + P]
        fold = fold_all[:, 0:BLK]
        tri_le = cst[:, C_LE:C_LE + P]
        tri_lt = cst[:, C_LT:C_LT + P]
        causal = cst[:, C_CAUSAL:C_CAUSAL + P]
        maskT = cst[:, C_MASKT:C_MASKT + P]
        iota32 = cst[:, C_IOTA:C_IOTA + BLK]
        iota_grp = cst[:, C_IOTA:C_IOTA + GRP]
        idxm = cst[:, C_IDXM:C_IDXM + NE]
        rope = cst[:, C_ROPE:NCONST].rearrange("p (t c j) -> p t c j", t=NT, c=2)

        cact = small[:, 0:8]
        eps = small[:, 221:222]
        ssq = small[:, 8:10]
        rstd = small[:, 10:12]
        brow = hbuf[0:24, 0, 0:512]
        gam9 = RD[:, 1408:1984].rearrange("p (g d) -> p g d", g=9)
        cwT = small[:, 12:24]
        cwr = RD[0:12, 1280:1408]
        bgate = small[:, 24:40]
        rb = small[:, 40:76]

        slot_full = [sem(f"slot_full{i}") for i in range(NS)]
        slot_used = [sem(f"slot_used{i}") for i in range(NS)]
        x_in = sem("x_in")
        const_in = sem("const_in")
        param_in = sem("param_in")
        gam_in = sem("gam_in")
        gam_free = sem("gam_free")
        rparam_in = sem("rparam_in")
        rparam_free = sem("rparam_free")
        out_done = sem("out_done")
        fill_ready = sem("fill_ready")
        cact_ready = sem("cact_ready")
        brow_in = sem("brow_in")
        c_in = sem("c_in")
        part_done = sem("part_done")
        part_copied = sem("part_copied")
        rowsum_done = sem("rowsum_done")
        modr_ready = sem("modr_ready")
        scale_done = sem("scale_done")
        scale_read = sem("scale_read")
        shift_done = sem("shift_done")
        gatev_done = sem("gatev_done")
        gv_act = sem("gv_act")
        std_done = sem("std_done")
        h_ready = sem("h_ready")
        ht_done = sem("ht_done")
        ht_act = sem("ht_act")
        ht_dve = sem("ht_dve")
        V = sem("dve_step")
        A = sem("act_step")
        proj_done = sem("proj_done")
        proj_act = sem("proj_act")
        proj_dve = sem("proj_dve")
        bg_act = sem("bg_act")
        vone_ready = sem("vone_ready")
        sq_ready = sem("sq_ready")
        qss_ready = sem("qss_ready")
        qstd_ready = sem("qstd_ready")
        q2_ready = sem("q2_ready")
        cwt_done = sem("cwt_done")
        cwt_act = sem("cwt_act")
        qt_done = sem("qt_done")
        qt_act = sem("qt_act")
        qt_dve = sem("qt_dve")
        score_done = sem("score_done")
        relu_done = sem("relu_done")
        relu_used = sem("relu_used")
        yconv_ready = sem("yconv_ready")
        logit_done = sem("logit_done")
        logit_read = sem("logit_read")
        max_ready = sem("max_ready")
        exp_done = sem("exp_done")
        probs_ready = sem("probs_ready")
        pt_done = sem("pt_done")
        pt_act = sem("pt_act")
        pt_dve = sem("pt_dve")
        pv_done = sem("pv_done")
        yt_act = sem("yt_act")
        yt_dve = sem("yt_dve")
        outp_done = sem("outp_done")
        x_ready = sem("x_ready")
        gates_ready = sem("gates_ready")
        absexp_done = sem("absexp_done")
        logf_ready = sem("logf_ready")
        cumf_done = sem("cumf_done")
        a_ready = sem("a_ready")
        at_done = sem("at_done")
        m_ready = sem("m_ready")
        mb_done = sem("mb_done")
        mbc_dve = sem("mbc_dve")
        mbc_act = sem("mbc_act")
        em_in = sem("em_in")
        em_ready = sem("em_ready")
        w_done = sem("w_done")
        st_done = sem("st_done")
        pw_ready = sem("pw_ready")
        num_done = sem("num_done")
        hn_ready = sem("hn_ready")
        hsq_done = sem("hsq_done")
        hss_ready = sem("hss_ready")
        hstd_done = sem("hstd_done")
        y_ready = sem("y_ready")
        yb_done = sem("yb_done")
        rlog_done = sem("rlog_done")
        gexp_in = sem("gexp_in")
        gexp_done = sem("gexp_done")
        wexp_in = sem("wexp_in")
        wexp_done = sem("wexp_done")
        onehot_ready = sem("onehot_ready")
        rank_done = sem("rank_done")
        table_ready = sem("table_ready")
        diag_ready = sem("diag_ready")
        rows_done = sem("rows_done")
        rows_copied = sem("rows_copied")
        zero_ready = sem("zero_ready")
        acc_done = sem("acc_done")

        def per_layer(name):
            return [sem(f"{name}_{l}") for l in range(DEPTH)]
        gate_done = per_layer("gate_done")
        up_done = per_layer("up_done")
        hg_ready = per_layer("hg_ready")
        hu_ready = per_layer("hu_ready")
        turn_done = per_layer("turn_done")
        silu_ready = per_layer("silu_ready")
        hid_ready = per_layer("hid_ready")
        down_done = per_layer("down_done")
        y_act = per_layer("y_act")
        y_dve = per_layer("y_dve")
        scat_ready = per_layer("scat_ready")
        next_sel = per_layer("next_sel")
        block_step = per_layer("block_step")
        group_step = per_layer("group_step")
        group_sel = per_layer("group_sel")
        group_done = per_layer("group_done")
        group_ready = per_layer("group_ready")
        extra_done = per_layer("extra_done")
        extra_xt = per_layer("extra_xt")

        patt = RA[:, 0:NT * 1224].rearrange("p (t n) -> p t n", t=NT)
        QT = RA[:, :].rearrange("p (c t) -> p c t", c=10)
        Q2 = RB[:, :].rearrange("p (t g d) -> p t g d", t=NT, g=20)
        qsq = RB[:, 0:NT * 576].rearrange("p (t g d) -> p t g d", t=NT, g=9)
        yT = RC[:, :].rearrange("p (c t) -> p c t", c=8)
        vv = RD[:, 0:NT * 72].rearrange("p (t n) -> p t n", t=NT)
        relu = [RB[:, 512 * i:512 * i + 512] for i in range(4)]
        score = RD[:, 256:512]
        work = RD[:, 512:768]
        selb = RD[:, 768:1280].rearrange("p (t s) -> p t s", t=NT)
        cgs = hbuf[:, 0, :].rearrange("p (c t) -> p c t", c=4)
        ctmp = hbuf[:, 1, :].rearrange("p (c t) -> p c t", c=4)
        logits = (RB[:, 0:HEADS * P].rearrange("p (h s) -> p h s", h=HEADS),
                  hTb[:, :].rearrange("p (h s) -> p h s", h=HEADS))
        PT = hbuf[:, :, :].rearrange("p k (h q) -> p k h q", h=HEADS)
        amax = [small[:, 76 + 8 * t:84 + 8 * t] for t in range(NT)]
        rsum = small[:, 92:100]
        asum = [small[:, 100 + 8 * t:108 + 8 * t] for t in range(NT)]
        qss = small[:, 100:118]
        qrs = small[:, 118:136]
        top8 = small[:, 136:144]
        wsc = small[:, 144:160].rearrange("p (t n) -> p t n", t=NT)
        otmp = RD[:, 2560:3072]
        gv = (RA[:, 0:D], RD[:, 1536:1536 + D])

        qkT = RA[:, 0:2048].rearrange("p (c t) -> p c t", c=8)
        vx = RB[:, 0:NT * HEADS * (VD + 1)].rearrange("p (t h v) -> p t h v", t=NT, h=HEADS)
        ogs = hbuf
        MB0 = RD[:, 0:2048].rearrange("p (h t) -> p h t", h=HEADS)
        MB1 = RD[:, 2048:3072].rearrange("p (h t) -> p h t", h=HEADS)
        HN = RA[:, 0:2048].rearrange("p (t h v) -> p t h v", t=NT, h=HEADS)
        hsq = RC[:, :].rearrange("p (t h v) -> p t h v", t=NT, h=HEADS)
        gts = small[:, 76:108].rearrange("p (t n) -> p t n", t=NT)
        g3 = small[:, 108:124].rearrange("p (t n) -> p t n", t=NT)
        lf = small[:, 124:140].rearrange("p (t n) -> p t n", t=NT)
        cumf = small[:, 140:156].rearrange("p (t n) -> p t n", t=NT)
        asb = small[:, 156:172].rearrange("p (t n) -> p t n", t=NT)
        mrow = RA[0:HEADS, 2048:2560].rearrange("p (c t) -> p c t", c=2)
        em = small[:, 172:188].rearrange("p (t n) -> p t n", t=NT)
        den = small[:, 188:204].rearrange("p (t n) -> p t n", t=NT)
        hss = small[:, 204:220].rearrange("p (t n) -> p t n", t=NT)

        XT = RA[:, 0:KC * BLK].rearrange("p (k s) -> p k s", k=KC)
        HG = RA[:, 256:768]
        HU = RA[:, 768:1280]
        SIL = RA[:, 1280:1408].rearrange("p (f s) -> p f s", f=FC)
        HID = RA[:, 1408:1536].rearrange("p (f s) -> p f s", f=FC)
        SC = RA[:, 1536:1792]
        SCT = RA[:, 1792:2048]
        SEL = RA[:, 2048:2112].rearrange("p (t s) -> p t s", t=NT)
        SELQ = RA[:, 2112:2240].rearrange("p (c s) -> p c s", c=4)
        XG = hTb[:, 0:KC * GRP].rearrange("p (k s) -> p k s", k=KC)
        SELG = hTb[:, KC * GRP:(KC + NT) * GRP].rearrange("p (t s) -> p t s", t=NT)
        SELGQ = hTb[:, (KC + NT) * GRP:(KC + NT + 4) * GRP].rearrange("p (c s) -> p c s", c=4)
        Y = RB[:, 0:1024]
        posrow = RB[:, 1024:1536].rearrange("p (c t) -> p c t", c=2)
        wrow = RB[:, 1536:2048].rearrange("p (c t) -> p c t", c=2)
        DG = RC[:, 1024:2048].rearrange("p (r t) -> p r t", r=8)
        LG = RD[:, 0:72].rearrange("p (t n) -> p t n", t=NT)
        R1 = RD[:, 72:136].rearrange("p (t n) -> p t n", t=NT)
        R2 = RD[:, 136:200].rearrange("p (t n) -> p t n", t=NT)
        O1 = RD[:, 200:264].rearrange("p (t n) -> p t n", t=NT)
        O2 = RD[:, 264:328].rearrange("p (t n) -> p t n", t=NT)
        POSG = RD[:, 1280:1344].rearrange("p (t n) -> p t n", t=NT)
        GE = RD[:, 1344:1344 + NT * NG].rearrange("p (t n) -> p t n", t=NT)
        OS = RD[:, 328:392].rearrange("p (t n) -> p t n", t=NT)
        CMP = RD[:, 392:392 + NE * 7].rearrange("p (e b) -> p e b", b=7)
        NBL = RD[:, 616:648]
        BBF = RD[:, 648:681]
        POSM = RD[:, 684:748].rearrange("p (t n) -> p t n", t=NT)
        zero = RD[:, 768:1280]
        s1 = small[:, 204:206]
        vals = small[:, 208:216]
        PR = small[:, 216:220]
        VP = small[:, 220:221]
        gmx, gsm, pg, v1, v2, ex = [small[:, 222 + 2 * i:224 + 2 * i] for i in range(6)]
        mnx = small[:, 234:236]
        PG = small[:, 236:240]

        qt_banks = (6, 7, 2, 3, 4, 5)
        score_banks = ((6, 7, 2, 3), (4, 5, 6, 7))
        logit_banks = ((4, 5, 6, 7), (2, 3, 4, 5))
        pv_banks = (4, 7)
        st_banks = (5, 6, 4, 7, 2, 3, 5, 6)
        num_banks = ((2, 3, 4), (5, 6, 7))
        ht_banks = (((4, 5), (6, 7)), ((4, 5), (6, 7)), ((4, 7), (2, 3)), ((4, 5), (6, 7)))
        scale_banks = ((0, 1), (0, 1), (4, 7), (0, 1))
        shift_banks = ((2, 3), (2, 3), (5, 6), (2, 3))

        def bc(ap, n):
            return ap.unsqueeze(2).to_broadcast([ap.shape[0], ap.shape[1], n])

        def mid(ap, n):
            return ap.unsqueeze(1).to_broadcast([ap.shape[0], n, ap.shape[1]])

        block = ctx.enter_context(nc.Block())

        @block.sync
        def _(sp):
            def load(n, turn, per_turn, src, cols, rows=KC):
                s = n % NS
                k = n // NS
                if turn is not None or k > 0:
                    sp.wait_ge(slot_used[s], k + turn * per_turn if turn is not None else k)
                dst = ring[s][:, 0:rows * cols].rearrange("p (k n) -> p k n", k=rows)
                sp.dma_start(dst, src).then_inc(slot_full[s], 16)

            for piece in stream:
                kind, l, a, w = piece
                n = at[piece]
                if kind == "ada":
                    load(n, None, 0, ada_w[l].rearrange("(p k) n -> p k n", k=KC)[:, :, 512 * a:512 * a + 512], 512)
                elif kind == "in":
                    src = hy_w_in[0] if l == 0 else ml_w_in[0]
                    load(n, None, 0, src.rearrange("(p k) n -> p k n", k=KC)[:, :, a:a + w], w)
                elif kind == "out":
                    src = hy_w_out[0] if l == 0 else ml_w_out[0]
                    load(n, None, 0, src.rearrange("(k p) n -> p k n", k=KC)[:, :, 512 * a:512 * a + 512], 512)
                else:
                    def load_expert(turn, u, e):
                        for j, m in enumerate((moe_w_gate, moe_w_up, moe_w_down)):
                            rows = FC if j == 2 else KC
                            src = m[l, bass.ds(e, 1)].rearrange("a (p k) n -> p (a k) n", k=rows)
                            load(n + 3 * u + j, turn, 1, src, m.shape[-1], rows)

                    with sp.Fori(0, NE // UNROLL) as turn:
                        for u in range(UNROLL):
                            load_expert(turn, u, turn * UNROLL + u)
                    for u in range(NE % UNROLL):
                        load_expert(NE // UNROLL, u, NE - NE % UNROLL + u)
            for t in range(NT):
                sp.wait_ge(x_ready, 2 * NT * DEPTH - NT + t + 1)
                sp.dma_start(out[0, t * P:(t + 1) * P, :], xs[:, t, :]).then_inc(out_done, 16)
            sp.wait_ge(out_done, 16 * NT)

        @block.gpsimd
        def _(pool):
            pool.dma_start(gam[:, :], norm_mix[0:1, :].to_broadcast([P, D])).then_inc(gam_in, 16)
            pool.dma_start(gam9[:, 0:8, :], hy_q_norm.unsqueeze(1).to_broadcast([P, 8, HD])).then_inc(param_in, 16)
            pool.dma_start(gam9[:, 8, :], hy_k_norm.to_broadcast([P, HD])).then_inc(param_in, 16)
            pool.dma_start(cwr[:, :], hy_conv_w[0].rearrange("j (c p) -> (j c) p", p=P)).then_inc(param_in, 16)
            pool.dma_start(bgate, ml_b_gates.to_broadcast([P, 2 * HEADS])).then_inc(param_in, 16)
            gi = 0
            for l in range(DEPTH):
                for w in range(2):
                    if gi:
                        pool.wait_ge(gam_free, gi)
                        src = (norm_mix if w == 0 else norm_ffn)[l:l + 1, :]
                        pool.dma_start(gam[:, :], src.to_broadcast([P, D])).then_inc(gam_in, 16)
                    gi += 1
                    if l == 1 and w == 0:
                        pool.wait_ge(gam_free, gi)
                        pool.dma_start(gam[:, :], ml_out_norm.to_broadcast([P, D])).then_inc(gam_in, 16)
                        gi += 1
                if l:
                    pool.wait_ge(rparam_free, l)
                pool.dma_start(rw[:, :, 0:NG], moe_w_group[l].rearrange("(p k) n -> p k n", k=KC)).then_inc(rparam_in, 16)
                pool.dma_start(rw[:, :, NG:], moe_w_expert[l].rearrange("(p k) n -> p k n", k=KC)).then_inc(rparam_in, 16)
                pool.dma_start(rb[:, 0:NG], moe_b_group[l:l + 1, :].to_broadcast([P, NG])).then_inc(rparam_in, 16)
                pool.dma_start(rb[:, NG:], moe_b_expert[l:l + 1, :].to_broadcast([P, NE])).then_inc(rparam_in, 16)

        @block.tensor
        def _(pe):
            mm = nc.tensor.matmul
            state = {"session": 0, "used": None}

            def landed(piece):
                n = at[piece]
                pe.wait_ge(slot_full[n % NS], 16 * (n // NS + 1))
                cols = piece[3] or 512
                return ring[n % NS][:, 0:KC * cols].rearrange("p (k n) -> p k n", k=KC), slot_used[n % NS]

            def behind(ins):
                if state["used"] is not None:
                    ins.then_inc(state["used"], 1)
                    state["used"] = None

            def mod_pieces(layer, js, opens, closes):
                for j in js:
                    if (layer, j) in ((0, 2), (0, 3)):
                        pe.wait_ge(const_in, 16)
                        for _ in range(2):
                            mm(bank[2][:, :], ident, cst[:, 0:512], start=True, stop=True)
                    w, used = landed(("ada", layer, j, 0))
                    row = 12 * layer + j
                    for k in range(KC):
                        g = k % 4
                        start = opens and j == js[0] and k < 4
                        stop = closes and j == js[-1] and k >= 4
                        c0 = BLK * k + 23 - row
                        last = mm(bank[0][32 * g:32 * g + 32, :], cz[:, c0:c0 + BLK], w[:, k, :], start=start, stop=stop)
                        if k == 0:
                            behind(last)
                    state["used"] = used
                if closes:
                    last.then_inc(part_done, 1)

            def mod_rows():
                s = state["session"]
                pe.wait_ge(part_copied, s + 1)
                if s:
                    pe.wait_ge(modr_ready, s)
                    ins = mm(bank[1][:, :], fold_all, modp[s], start=True, stop=True)
                else:
                    pe.wait_ge(const_in, 16)
                    mm(bank[1][:, :], fold_all, modp[s], start=True, stop=False)
                    pe.wait_ge(brow_in, 16)
                    ins = mm(bank[1][:, :], fold_all[0:24, :], brow, start=False, stop=True)
                ins.then_inc(rowsum_done, 1)
                state["session"] += 1

            def spread(row, group, b):
                q = slice(32 * group, 32 * group + 32)
                return mm(bank[b][:, :], ident[q, 32 * group + row:32 * group + row + 1].to_broadcast([32, P]), modr[q, :],
                          start=True, stop=True)

            def spread_scale(q):
                l, w = q // 2, q % 2
                for n in range(2):
                    ins = spread(12 * l + 2 * (3 * w + 1) + n, n, scale_banks[q][n])
                    if n == 0:
                        behind(ins)
                ins.then_inc(scale_done, 1)

            def spread_shift(q):
                l, w = q // 2, q % 2
                for n in range(2):
                    ins = spread(12 * l + 2 * (3 * w) + n, 2 + n, shift_banks[q][n])
                    if n == 0:
                        behind(ins)
                ins.then_inc(shift_done, 1)

            def spread_gate(l, w, banks):
                for n in range(2):
                    ins = spread(12 * l + 2 * (3 * w + 2) + n, 2 + n, banks[n])
                ins.then_inc(gatev_done, 1)

            def router_logits(l, t):
                pe.wait_ge(ht_act, NT * (2 * l + 1) + t + 1)
                pe.wait_ge(ht_dve, NT * (2 * l + 1) + t + 1)
                pe.wait_ge(rparam_in, 64 * (l + 1))
                for k in range(KC):
                    last = mm(bank[5][:, 36 * t:36 * t + 36], hT[:, k, t * P:(t + 1) * P], rw[:, k, :],
                              start=(k == 0), stop=(k == KC - 1))
                if t == NT - 1:
                    last.then_inc(rlog_done, 1)

            def transpose_h(q):
                for t in range(NT):
                    pe.wait_ge(h_ready, NT * q + t + 1)
                    for g in range(2):
                        for j in range(4):
                            last = nc.tensor.transpose(bank[ht_banks[q][t][g]][:, P * j:P * j + P], h[:, t, 4 * g + j, :], ident)
                            if j == 0:
                                behind(last)
                        last.then_inc(ht_done, 1)

            def out_proj(l):
                pe.wait_ge(modr_ready, (2, 5)[l])
                spread_gate(l, 0, (2, 3))
                w, used = zip(*[landed(("out", l, n, 0)) for n in range(2)])
                if l == 0:
                    pe.wait_ge(yconv_ready, 1)
                for t in range(NT):
                    pe.wait_ge(yt_act, NT * l + t + 1)
                    if l == 1:
                        pe.wait_ge(yt_dve, t + 1)
                    for n in range(2):
                        for k in range(KC):
                            last = mm(bank[4 + 2 * t + n][:, :], yT[:, k, t * P:(t + 1) * P], w[n][:, k, :],
                                      start=(k == 0), stop=(k == KC - 1))
                            if k == 0:
                                behind(last)
                        last.then_inc(outp_done, 1)
                        if t == 1:
                            state["used"] = used[n]
                    if t == 0:
                        spread_scale(2 * l + 1)
                pe.wait_ge(gv_act, 2 * l + 1)
                spread_shift(2 * l + 1)

            def project_tokens(piece, banks, n):
                w, used = landed(piece)
                for t in range(NT):
                    for k in range(KC):
                        last = mm(bank[banks[t][0]][:, banks[t][1]:banks[t][1] + n], hT[:, k, t * P:(t + 1) * P], w[:, k, :],
                                  start=(k == 0), stop=(k == KC - 1))
                        if t == 0 and k == 0:
                            behind(last)
                    last.then_inc(proj_done, 1)
                state["used"] = used

            def project_features(piece, banks):
                w, used = landed(piece)
                for f in range(4):
                    for k in range(KC):
                        last = mm(bank[banks[f // 2]][:, 256 * (f % 2):256 * (f % 2) + 256],
                                  w[:, k, P * f:P * f + P], hT[:, k, :], start=(k == 0), stop=(k == KC - 1))
                        if f == 0 and k == 0:
                            behind(last)
                    if f % 2:
                        last.then_inc(proj_done, 1)
                state["used"] = used

            def hybrid():
                l = 0
                pe.wait_ge(ht_act, 2)
                pe.wait_ge(ht_dve, 2)
                for i, (a, n) in enumerate([(0, 512), (512, 512), (1024, 200)]):
                    project_tokens(("in", 0, a, n), ((2 + 2 * i, 0), (3 + 2 * i, 0)), n)
                pe.wait_ge(param_in, 16 * 4)
                nc.tensor.transpose(bank[1][:, 16:28], cwr, ident[0:12, 0:12]).then_inc(cwt_done, 1)
                pe.wait_ge(proj_act, 1)
                pe.wait_ge(proj_dve, 1)
                project_features(("in", 0, 1224, 512), (2, 3))
                mod_pieces(0, range(4, 6), True, False)
                pe.wait_ge(q2_ready, 2)
                pe.wait_ge(proj_act, 3)
                pe.wait_ge(proj_dve, 3)
                for t in range(NT):
                    for g in range(3):
                        if 3 * t + g == 2:
                            pe.wait_ge(bg_act, 2)
                        for j in range(4 if g < 2 else 2):
                            ch = 4 * g + j
                            last = nc.tensor.transpose(bank[qt_banks[3 * t + g]][:, P * j:P * j + P], Q2[:, t, 2 * ch:2 * ch + 2, :], ident)
                        last.then_inc(qt_done, 1)
                pe.wait_ge(qt_act, 3)
                pe.wait_ge(qt_dve, 3)

                def head_products(t, first, key, signal, banks, b):
                    g, par = b // 2, b % 2
                    nk = P * (t + 1)
                    r = slice(64 * par, 64 * par + 64)
                    for i in range(2):
                        hd = 4 * g + 2 * i + par
                        last = mm(bank[banks[b]][:, 256 * i:256 * i + nk],
                                  QT[r, first + hd // 2, t * P:(t + 1) * P], QT[r, key, 0:nk], start=True, stop=True)
                    last.then_inc(signal, 1)
                for t in range(NT):
                    for b in range(4):
                        if t and b >= 2:
                            pe.wait_ge(relu_done, b - 1)
                        head_products(t, 5, 9, score_done, score_banks[t], b)
                pe.wait_ge(relu_done, 6)
                project_features(("in", 0, 1736, 512), (4, 5))
                project_features(("in", 0, 2248, 512), (2, 3))
                mod_pieces(0, range(6, 9), False, False)
                pe.wait_ge(relu_done, 8)
                pe.wait_ge(proj_act, 5)
                for t in range(NT):
                    if t:
                        pe.wait_ge(proj_dve, 4)
                    for b in range(4):
                        if t and b >= 2:
                            pe.wait_ge(logit_read, b - 1)
                        head_products(t, 0, 4, logit_done, logit_banks[t], b)
                mod_pieces(0, range(9, 12), False, True)
                ptn = 0
                for t in range(NT):
                    pe.wait_ge(probs_ready, t + 1)
                    for kt in range(t + 1):
                        for g in range(2):
                            if ptn >= 2:
                                pe.wait_ge((pt_act, pt_dve)[g], ptn // 2)
                            for j in range(4):
                                last = nc.tensor.transpose(bank[6 + g][:, P * j:P * j + P],
                                                           logits[t][:, 4 * g + j, kt * P:(kt + 1) * P], ident)
                                if j == 0:
                                    behind(last)
                            last.then_inc(pt_done, 1)
                            ptn += 1
                    if t == 0:
                        mod_rows()
                    pe.wait_ge(pt_act, ptn // 2)
                    pe.wait_ge(pt_dve, ptn // 2)
                    for par in range(2):
                        for kt in range(t + 1):
                            last = mm(bank[pv_banks[t]][64 * par:64 * par + 64, :], vv[:, kt, 0:HD],
                                      PT[:, kt, par:HEADS:2, :], start=(kt == 0), stop=(kt == t))
                    last.then_inc(pv_done, 1)
                out_proj(l)

            def mlstm():
                l = 1
                pe.wait_ge(ht_act, 2 + 2 * 2)
                pe.wait_ge(ht_dve, 2 + 2 * 2)
                project_tokens(("in", 1, 2048, 16), ((4, 0), (4, 16)), 16)
                pe.wait_ge(modr_ready, 4)
                project_features(("in", 1, 0, 512), (0, 1))
                pe.wait_ge(logf_ready, 1)
                mm(bank[5][:, 0:8], tri_le, lf[:, 0, :], start=True, stop=True)
                mm(bank[5][:, 8:16], ones, lf[:, 0, :], start=True, stop=False)
                mm(bank[5][:, 8:16], tri_le, lf[:, 1, :], start=False, stop=True).then_inc(cumf_done, 1)
                project_features(("in", 1, 512, 512), (2, 3))
                pe.wait_ge(a_ready, 1)
                for t in range(NT):
                    last = nc.tensor.transpose(bank[6][0:8, t * P:(t + 1) * P], asb[:, t, :], ident)
                last.then_inc(at_done, 1)
                pe.wait_ge(gates_ready, 1)
                project_tokens(("in", 1, 1024, 512), ((4, 0), (7, 0)), 512)
                pe.wait_ge(m_ready, 1)
                for t in range(NT):
                    last = nc.tensor.transpose(bank[6][:, 256 + 8 * t:264 + 8 * t], mrow[:, 1, t * P:(t + 1) * P], ident[0:8, 0:8])
                last.then_inc(at_done, 1)
                pe.wait_ge(proj_act, 7)
                project_tokens(("in", 1, 1536, 512), ((2, 0), (3, 0)), 512)
                for hd in range(HEADS):
                    if hd == 4:
                        pe.wait_ge(proj_act, 9)
                        pe.wait_ge(proj_dve, 6)
                    last = mm(bank[hd // 2][:, 256 * (hd % 2):256 * (hd % 2) + 256],
                              ident[0:8, hd:hd + 1].to_broadcast([8, P]), mrow[:, 1, :], start=True, stop=True)
                    if hd == 0:
                        behind(last)
                    if hd % 2:
                        last.then_inc(mb_done, 1)
                pe.wait_ge(em_in, 1)
                for hd in range(HEADS):
                    if 4 <= hd < 6:
                        pe.wait_ge(mbc_act, hd - 1)
                    if hd >= 6:
                        pe.wait_ge(pw_ready, 2 * (hd - 5))
                    r = slice(64 * (hd % 2), 64 * (hd % 2) + 64)
                    b = bank[st_banks[hd]]
                    mm(b[:, 0:256], qkT[r, 4 + hd // 2, 0:P], qkT[r, hd // 2, :], start=True, stop=True)
                    mm(b[:, 256:384], qkT[r, 4 + hd // 2, P:], qkT[r, hd // 2, P:], start=True, stop=True).then_inc(st_done, 1)
                project_tokens(("in", 1, 2064, 512), ((0, 0), (1, 0)), 512)
                pe.wait_ge(pw_ready, 16)
                pe.wait_ge(vone_ready, 1)
                for t in range(NT):
                    for hd in range(HEADS):
                        b = bank[num_banks[t][hd // 3]]
                        o = b[:, 129 * (hd % 3):129 * (hd % 3) + 129]
                        if t == 0:
                            last = mm(o, MB0[:, hd, 0:P], vx[:, 0, hd, :], start=True, stop=True)
                        else:
                            mm(o, MB0[:, hd, P:], vx[:, 0, hd, :], start=True, stop=False)
                            last = mm(o, MB1[:, hd, :], vx[:, 1, hd, :], start=False, stop=True)
                        if hd in (2, 5, 7):
                            last.then_inc(num_done, 1)
                pe.wait_ge(proj_act, 11)
                project_tokens(("in", 1, 2576, 512), ((0, 0), (1, 0)), 512)
                pe.wait_ge(proj_act, 13)
                mod_pieces(1, range(8, 10), True, True)
                mod_rows()
                for t in range(NT):
                    pe.wait_ge(y_ready, t + 1)
                    for g in range(2):
                        for j in range(4):
                            last = nc.tensor.transpose(bank[4 + 2 * t + g][:, P * j:P * j + P], HN[:, t, 4 * g + j, :], ident)
                        last.then_inc(yb_done, 1)
                out_proj(l)

            def ffn(l):
                for t in range(NT):
                    router_logits(l, t)

                def zero_sums(banks):
                    for b in banks:
                        mm(bank[b][:, :], zero[:, 0:P], zero, start=True, stop=True)

                if l == 0:
                    mod_pieces(1, range(4, 5), False, False)
                else:
                    pe.wait_ge(modr_ready, 6)
                spread_gate(l, 1, (6, 7))
                pe.wait_ge(zero_ready, l + 1)
                zero_sums((2, 3) if l else (2,))
                pe.wait_ge(gv_act, 2 * l + 2)
                pe.wait_ge(onehot_ready, l + 1)
                mm(bank[7][:, 0:32], tri_lt, OS[:, 0, :], start=True, stop=True)
                mm(bank[7][:, 32:64], ones, OS[:, 0, :], start=True, stop=False)
                mm(bank[7][:, 32:64], tri_lt, OS[:, 1, :], start=False, stop=True)
                mm(bank[7][:, 64:96], ones, OS[:, 0, :], start=True, stop=False)
                mm(bank[7][:, 64:96], ones, OS[:, 1, :], start=False, stop=True).then_inc(rank_done, 1)
                if l == 0:
                    mod_pieces(1, range(5, 6), False, True)

                def gather_group(g, half):
                    if half:
                        pe.wait_ge(group_ready[l], 2 * g + 1)
                    else:
                        pe.wait_ge(group_sel[l], g + 1)
                    chunks = range(GCUT, KC) if half else range(GCUT)
                    for k in chunks:
                        o = GRP * (k - chunks[0])
                        for t in range(NT):
                            last = mm(bank[4][:, o:o + GRP], h[:, t, k, :], SELG[:, t, :], start=(t == 0), stop=(t == NT - 1))
                            if t == 0:
                                behind(last)
                    last.then_inc(group_done[l], 1)

                def gather_extra(v):
                    pe.wait_ge(next_sel[l], v + 1)
                    for k in range(KC):
                        for t in range(NT):
                            last = mm(bank[4][:, BLK * k:BLK * k + BLK], h[:, t, k, :], SEL[:, t, :],
                                      start=(t == 0), stop=(t == NT - 1))
                    last.then_inc(extra_done[l], 1)

                def scatter(t, n):
                    return mm(bank[2 * t + n][:, :], SC[:, t * P:(t + 1) * P], Y[:, 512 * n:512 * n + 512],
                              start=False, stop=False, skip_group_check=True)

                def scatters(v, tiles, used=None):
                    pe.wait_ge(scat_ready[l], v + 1)
                    for i, (t, n) in enumerate(tiles):
                        ins = scatter(t, n)
                        if i == 0 and used:
                            ins.then_inc(used, 1)

                def expert_block(v, tokens, weights, landed_expert, group=None, used=(None, None), last_one=False, further=False):
                    for j, (b, done, read) in enumerate(((5, gate_done[l], y_act[l]), (6, up_done[l], y_dve[l]))):
                        w = weights[j]
                        pe.wait_ge(read, v + 1)
                        if j == 1:
                            pe.wait_ge(rows_copied, l + 1)
                            if last_one:
                                scatters(v, ((0, 0), (0, 1), (1, 0), (1, 1)), used[0])
                        landed_expert(j)
                        for k in range(KC):
                            g = k % 4
                            last = mm(bank[b][32 * g:32 * g + 32, :], tokens[:, k, :], w[:, k, :], start=(k < 4), stop=(k >= 4))
                        last.then_inc(done, 1)
                    if group is not None:
                        gather_group(group, 0)
                    if not last_one and not further:
                        scatters(v, ((0, 0),), used[0])
                    pe.wait_ge(hg_ready[l], v + 1)
                    for f in range(FC):
                        ins = mm(bank[7][:, BLK * f:BLK * f + BLK], HG[:, f:DE:FC], fold, start=True, stop=True)
                        if f == 0 and used[1]:
                            ins.then_inc(used[1], 1)
                    pe.wait_ge(hu_ready[l], v + 1)
                    for f in range(FC):
                        last = mm(bank[7][:, P + BLK * f:P + BLK * f + BLK], HU[:, f:DE:FC], fold, start=True, stop=True)
                    last.then_inc(turn_done[l], 1)
                    if not last_one:
                        scatters(v, ((0, 1), (1, 0), (1, 1)))
                    if group is not None:
                        gather_group(group, 1)
                    landed_expert(2)
                    pe.wait_ge(hid_ready[l], v + 1)
                    for n in range(2):
                        for f in range(FC):
                            last = mm(bank[5 + n][32 * f:32 * f + 32, :], HID[:, f, :], weights[2][:, f, 512 * n:512 * n + 512],
                                      start=True, stop=True)
                        last.then_inc(down_done[l], 1)

                gather_group(0, 0)
                gather_group(0, 1)
                if l == 0:
                    mod_rows()
                zero_sums((0,) if l == 0 else (0, 1))
                pe.wait_ge(diag_ready, l + 1)
                mm(bank[7][:, :], ones, DG[:, 4:8, :], start=True, stop=True)
                mm(bank[6][:, :], ones, DG[:, 0:4, :], start=True, stop=True).then_inc(rows_done, 1)
                if l == 0:
                    pe.wait_ge(modr_ready, 3)
                    zero_sums((1, 3))
                pe.wait_ge(table_ready, l + 1)
                n0 = at[("experts", l, 0, 0)]

                def expert(turn, u, more):
                    e = turn * UNROLL + u
                    x0 = pe.value_load(tab[0:1, bass.ds(e, 1)], min_val=0, max_val=EXTRA)
                    x1 = pe.value_load(tab[0:1, bass.ds(e + 1, 1)], min_val=0, max_val=EXTRA)
                    w = [ring[(n0 + 3 * u + j) % NS][:, :].rearrange("p (k n) -> p k n", k=FC if j == 2 else KC)
                         for j in range(3)]

                    def landed_expert(j):
                        n = n0 + 3 * u + j
                        pe.wait_ge(slot_full[n % NS], 16 * (n // NS + 1) + 16 * turn)

                    with pe.If(x0 < x1):
                        with pe.Fori(x0, x1) as x:
                            if u == 0:
                                pe.wait_ge(group_ready[l], 2 * turn + 2)
                            gather_extra(x + e)
                            pe.wait_ge(y_act[l], x + e + 1)
                            scatters(x + e, ((0, 0),))
                            pe.wait_ge(extra_xt[l], x + 1)
                            expert_block(x + e, XT, w, landed_expert, further=True)
                    if u == 0:
                        pe.wait_ge(group_ready[l], 2 * turn + 2)
                    gathers = more and u == UNROLL - 1
                    used = [slot_used[(n0 + 3 * u + j) % NS] for j in range(3)]
                    expert_block(x1 + e, XG[:, :, BLK * u:BLK * u + BLK], w, landed_expert, turn + 1 if gathers else None, used,
                                 last_one=not more and u == NE % UNROLL - 1)
                    mark_used7(used[2])

                with pe.Fori(0, NE // UNROLL) as turn:
                    for u in range(UNROLL):
                        expert(turn, u, True)
                for u in range(NE % UNROLL):
                    expert(NE // UNROLL, u, False)
                if l + 1 < DEPTH:
                    spread_scale(2 * l + 2)
                extra = pe.value_load(tab[0:1, NE:NE + 1], min_val=0, max_val=EXTRA)
                pe.wait_ge(y_act[l], extra + NE + 1)
                pe.wait_ge(y_dve[l], extra + NE + 1)
                pe.wait_ge(scat_ready[l], extra + NE + 1)
                for t in range(NT):
                    for n in range(2):
                        scatter(t, n).then_inc(acc_done, 1)
                if l + 1 < DEPTH:
                    spread_shift(2 * l + 2)

            def mark_used7(used):
                mm(bank[7][0:32, 256:257], ident[:, 0:32], ident[:, 0:1], start=True, stop=True).then_inc(used, 1)

            pe.wait_ge(cact_ready, 1)
            mod_pieces(0, range(4), True, True)
            mod_rows()
            pe.wait_ge(modr_ready, 1)
            spread_scale(0)
            spread_shift(0)
            for l in range(DEPTH):
                if l:
                    pe.wait_ge(x_ready, 2 * NT * l - NT + 1)
                    mod_pieces(l, range(6, 8), True, True)
                    mod_rows()
                transpose_h(2 * l)
                (hybrid, mlstm)[l]()
                pe.wait_ge(scale_read, 2 * l + 2)
                mod_pieces(1, range(4) if l == 0 else range(10, 12), True, l == 1)
                if l:
                    mod_rows()
                transpose_h(2 * l + 1)
                ffn(l)

        @block.scalar
        def _(act):
            steps = [0]

            def step(ins):
                steps[0] += 1
                ins.then_inc(A, 1)
                act.wait_ge(A, steps[0])

            def copy(dst, src):
                return nc.scalar.activation(dst, src, ACT.Copy)

            session = [0]

            def mod_parts():
                session[0] += 1
                act.wait_ge(part_done, session[0])
                copy(modp[session[0] - 1], bank[0][:, :]).then_inc(part_copied, 1)

            def norm(q):
                for t in range(NT):
                    if q:
                        act.wait_ge(x_ready, NT * (q - 1) + t + 1)
                    step(nc.scalar.activation(RB[:, 1536:1536 + D], xs[:, t, :], ACT.Square, accum_out=ssq[:, t:t + 1]))
                    nc.scalar.activation(rstd[:, t:t + 1], ssq[:, t:t + 1], ACT.Sqrt, scale=1.0 / D, bias=eps).then_inc(std_done, 1)

            def gate_vector(i, banks):
                act.wait_ge(gatev_done, i)
                for n in range(2):
                    ins = copy(gv[(i - 1) % 2][:, 512 * n:512 * n + 512], bank[banks[n]][:, :])
                ins.then_inc(gv_act, 1)

            def copy_ht(q):
                for t in range(NT):
                    act.wait_ge(ht_done, 4 * q + 2 * t + 1)
                    copy(hT[:, 0:4, t * P:(t + 1) * P], bank[ht_banks[q][t][0]][:, :].rearrange("p (k t) -> p k t", k=4)).then_inc(ht_act, 1)

            def hybrid():
                for i, (a, n) in enumerate(((0, 512), (512, 512), (1024, 200))):
                    act.wait_ge(proj_done, 2 * i + 1)
                    copy(patt[:, 0, a:a + n], bank[2 + 2 * i][:, 0:n]).then_inc(proj_act, 1)
                act.wait_ge(proj_act, 3)
                act.wait_ge(proj_dve, 3)
                for t in range(NT):
                    nc.scalar.activation(qsq[:, t, :, :], patt[:, t, 0:576].rearrange("p (g d) -> p g d", d=HD), ACT.Square).then_inc(sq_ready, 1)
                act.wait_ge(qss_ready, 1)
                nc.scalar.activation(qrs, qss, ACT.Sqrt, scale=1.0 / HD, bias=eps).then_inc(qstd_ready, 1)
                act.wait_ge(cwt_done, 1)
                copy(cwT, bank[1][:, 16:28]).then_inc(cwt_act, 1)
                for i in range(2):
                    act.wait_ge(proj_done, 7 + i)
                    copy(yT[:, 4 + 2 * i:6 + 2 * i, :], bank[2 + i][:, :].rearrange("p (c t) -> p c t", c=2)).then_inc(bg_act, 1)
                for g in (0, 2, 4):
                    act.wait_ge(qt_done, g + 1)
                    t, c = g // 3, g % 3
                    m = 4 if c < 2 else 2
                    copy(QT[:, 4 * c:4 * c + m, t * P:(t + 1) * P],
                         bank[qt_banks[g]][:, 0:P * m].rearrange("p (c t) -> p c t", c=m)).then_inc(qt_act, 1)
                r = 0
                for t in range(NT):
                    nk = P * (t + 1)
                    for b in range(4):
                        act.wait_ge(score_done, 4 * t + b + 1)
                        if r >= 4:
                            act.wait_ge(relu_used, r - 3)
                        nc.scalar.activation(relu[r % 4].rearrange("p (i s) -> p i s", i=2)[:, :, 0:nk],
                                             bank[score_banks[t][b]][:, :].rearrange("p (i s) -> p i s", i=2)[:, :, 0:nk],
                                             ACT.Relu, scale=HD ** -0.5).then_inc(relu_done, 1)
                        r += 1
                for i in range(2):
                    act.wait_ge(proj_done, 9 + i)
                    ins = copy(cgs[:, 2 * i:2 * i + 2, :], bank[4 + i][:, :].rearrange("p (c t) -> p c t", c=2))
                    ins.then_inc(proj_act, 1)
                for t in range(NT):
                    nk = P * (t + 1)
                    act.wait_ge(max_ready, t + 1)
                    for hd in range(HEADS):
                        last = nc.scalar.activation(logits[t][:, hd, 0:nk], logits[t][:, hd, 0:nk], ACT.Exp, scale=HD ** -0.5,
                                                    bias=amax[t][:, hd:hd + 1], accum_out=asum[t][:, hd:hd + 1])
                    last.then_inc(exp_done, 1)
                mod_parts()
                ptn = 0
                for t in range(NT):
                    for kt in range(t + 1):
                        act.wait_ge(pt_done, 2 * ptn + 1)
                        copy(PT[:, kt, 0:4, :], bank[6][:, :].rearrange("p (h q) -> p h q", h=4)).then_inc(pt_act, 1)
                        ptn += 1
                    act.wait_ge(pv_done, t + 1)
                    copy(yT[:, 0:4, t * P:(t + 1) * P], bank[pv_banks[t]][:, :].rearrange("p (c q) -> p c q", c=4)).then_inc(yt_act, 1)

            def mlstm():
                act.wait_ge(gates_ready, 1)
                step(nc.scalar.activation(g3, gts[:, :, 8:16], ACT.Abs))
                step(nc.scalar.activation(g3, g3, ACT.Exp, scale=-1.0))
                nc.scalar.activation(g3, g3, ACT.Ln, bias=1.0).then_inc(absexp_done, 1)
                for i in range(4):
                    act.wait_ge(proj_done, 14 + i + 1)
                    ins = copy(qkT[:, 2 * i:2 * i + 2, :], bank[i][:, :].rearrange("p (c t) -> p c t", c=2))
                    if i % 2:
                        ins.then_inc(proj_act, 1)
                for half, b in ((0, 4), (1, 2)):
                    act.wait_ge(proj_done, 19 + 2 * half)
                    copy(vx[:, 0, 4 * half:4 * half + 4, 0:VD], bank[b][:, :].rearrange("p (h v) -> p h v", h=4)).then_inc(proj_act, 1)
                act.wait_ge(em_in, 1)
                nc.scalar.activation(em, em, ACT.Exp, scale=-1.0).then_inc(em_ready, 1)
                for b in range(4):
                    act.wait_ge(mbc_dve, 2 * b + 2)
                    copy(MB0[:, 2 * b:2 * b + 2, P:], bank[b][:, :].rearrange("p (h t) -> p h t", h=2)[:, :, P:]).then_inc(mbc_act, 1)
                for b in range(4):
                    act.wait_ge(mbc_act, b + 1)
                    for hd in (2 * b, 2 * b + 1):
                        nc.scalar.activation(MB0[:, hd, :], MB0[:, hd, :], ACT.Exp, scale=-1.0, bias=asb[:, 0, hd:hd + 1]).then_inc(w_done, 1)
                        nc.scalar.activation(MB1[:, hd, :], MB1[:, hd, :], ACT.Exp, scale=-1.0, bias=asb[:, 1, hd:hd + 1]).then_inc(w_done, 1)

                def output_gate(half):
                    for t in range(NT):
                        act.wait_ge(proj_done, 23 + 2 * half + t)
                        nc.scalar.activation(ogs[:, t, 512 * half:512 * half + 512], bank[t][:, :], ACT.Sigmoid).then_inc(proj_act, 1)

                output_gate(0)
                for t in range(NT):
                    act.wait_ge(hn_ready, t + 1)
                    nc.scalar.activation(hsq[:, t, :, :], HN[:, t, :, :], ACT.Square).then_inc(hsq_done, 1)
                act.wait_ge(hss_ready, 1)
                nc.scalar.activation(hss, hss, ACT.Sqrt, scale=1.0 / VD, bias=eps).then_inc(hstd_done, 1)
                output_gate(1)
                mod_parts()
                for t in range(NT):
                    act.wait_ge(yb_done, 2 * t + 1)
                    copy(yT[:, 0:4, t * P:(t + 1) * P], bank[4 + 2 * t][:, :].rearrange("p (c q) -> p c q", c=4)).then_inc(yt_act, 1)

            def ffn(l):
                act.wait_ge(gexp_in, l + 1)
                nc.scalar.activation(GE, GE, ACT.Exp).then_inc(gexp_done, 1)
                gate_vector(2 * l + 2, (6, 7))
                act.wait_ge(zero_ready, l + 1)
                copy(Y[:, 0:512], zero).then_inc(y_act[l], 1)
                act.wait_ge(wexp_in, l + 1)
                nc.scalar.activation(ex, ex, ACT.Exp).then_inc(wexp_done, 1)
                if l == 0:
                    mod_parts()

                def copy_group(g, half):
                    act.wait_ge(group_done[l], 2 * g + 1 + half)
                    c0, n = (GCUT, KC - GCUT) if half else (0, GCUT)
                    copy(XG[:, c0:c0 + n, :], bank[4][:, 0:n * GRP].rearrange("p (k s) -> p k s", k=n)).then_inc(group_ready[l], 1)

                copy_group(0, 0)
                copy_group(0, 1)
                act.wait_ge(rows_done, l + 1)
                copy(posrow, bank[6][:, :].rearrange("p (c t) -> p c t", c=2))
                copy(wrow, bank[7][:, :].rearrange("p (c t) -> p c t", c=2)).then_inc(rows_copied, 1)

                def expert_block(v, group=None):
                    act.wait_ge(gate_done[l], v + 1)
                    copy(HG, bank[5][:, :]).then_inc(hg_ready[l], 1)
                    if group is not None:
                        copy_group(group, 0)
                    act.wait_ge(turn_done[l], v + 1)
                    nc.scalar.activation(SIL, bank[7][:, 0:P].rearrange("p (f s) -> p f s", f=FC), ACT.Exp, scale=-1.0).then_inc(silu_ready[l], 1)
                    if group is not None:
                        copy_group(group, 1)
                    act.wait_ge(down_done[l], 2 * v + 1)
                    copy(Y[:, 0:512], bank[5][:, :]).then_inc(y_act[l], 1)

                def expert(turn, u, more):
                    e = turn * UNROLL + u
                    x0 = act.value_load(tab[0:1, bass.ds(e, 1)], min_val=0, max_val=EXTRA)
                    x1 = act.value_load(tab[0:1, bass.ds(e + 1, 1)], min_val=0, max_val=EXTRA)
                    with act.If(x0 < x1):
                        with act.Fori(x0, x1) as x:
                            act.wait_ge(extra_done[l], x + 1)
                            copy(XT, bank[4][:, 0:KC * BLK].rearrange("p (k s) -> p k s", k=KC)).then_inc(extra_xt[l], 1)
                            expert_block(x + e)
                    expert_block(x1 + e, turn + 1 if more and u == UNROLL - 1 else None)

                act.wait_ge(table_ready, l + 1)
                with act.Fori(0, NE // UNROLL) as turn:
                    for u in range(UNROLL):
                        expert(turn, u, True)
                for u in range(NE % UNROLL):
                    expert(NE // UNROLL, u, False)

            act.dma_start(cact, c[0].rearrange("(p k) -> p k", k=KC)).then_inc(c_in, 16)
            act.dma_start(cst[:, :], consts).then_inc(const_in, 16)
            act.dma_start(brow, ada_b.rearrange("l (r n) -> (l r) n", n=512)).then_inc(brow_in, 16)
            for t in range(NT):
                act.dma_start(xs[:, t, :], x[0, t * P:(t + 1) * P, :]).then_inc(x_in, 16)
            act.wait_ge(c_in, 16)
            act.wait_ge(fill_ready, 2)
            nc.scalar.activation(cz[:, 23:BLK * KC:BLK], cact, ACT.Silu).then_inc(cact_ready, 1)
            mod_parts()
            act.wait_ge(const_in, 16)
            act.wait_ge(x_in, 16 * NT)
            norm(0)
            for l in range(DEPTH):
                copy_ht(2 * l)
                (hybrid, mlstm)[l]()
                gate_vector(2 * l + 1, (2, 3))
                norm(2 * l + 1)
                if l:
                    mod_parts()
                copy_ht(2 * l + 1)
                ffn(l)
                if l + 1 < DEPTH:
                    norm(2 * l + 2)
                    mod_parts()

        @block.vector
        def _(dve):
            v = nc.vector
            steps = [0]

            def step(ins):
                steps[0] += 1
                ins.then_inc(V, 1)
                dve.wait_ge(V, steps[0])

            gain = [0]
            tiles = [0]

            def rows(s):
                dve.wait_ge(rowsum_done, s)
                if s == 1:
                    v.tensor_copy(modr[:, :], bank[1][:, :]).then_inc(modr_ready, 1)
                else:
                    v.tensor_tensor(modr[:, :], modr[:, :], bank[1][:, :], ALU.add).then_inc(modr_ready, 1)

            def gain_scale(q):
                dve.wait_ge(gam_in, 16 * (gain[0] + 1))
                dve.wait_ge(scale_done, q + 1)
                gain[0] += 1
                for n in range(2):
                    cols = slice(512 * n, 512 * n + 512)
                    ins = v.scalar_tensor_tensor(out=gam[:, cols], in0=bank[scale_banks[q][n]][:, :], scalar=1.0, in1=gam[:, cols],
                                                 op0=ALU.add, op1=ALU.mult)
                ins.then_inc(scale_read, 1)
                dve.wait_ge(scale_read, q + 1)

            def norm_tile(q, t):
                dve.wait_ge(std_done, NT * q + t + 1)
                step(v.reciprocal(rstd[:, t:t + 1], rstd[:, t:t + 1]))
                hv = h[:, t, :, :].rearrange("q k p -> q p k")
                ins = v.scalar_tensor_tensor(out=hv, in0=xs[:, t, :].rearrange("q (p k) -> q p k", k=KC), scalar=rstd[:, t:t + 1],
                                             in1=gam[:, :].rearrange("q (p k) -> q p k", k=KC), op0=ALU.mult, op1=ALU.mult)
                if t == NT - 1:
                    ins.then_inc(gam_free, 1)
                    dve.wait_ge(gam_free, gain[0])
                else:
                    step(ins)
                dve.wait_ge(shift_done, q + 1)
                for n in range(2):
                    hn = hv[:, 64 * n:64 * n + 64, :]
                    ins = v.tensor_tensor(hn, hn, bank[shift_banks[q][n]][:, :].rearrange("q (p k) -> q p k", k=KC), ALU.add)
                ins.then_inc(h_ready, 1)

            def copy_ht(q):
                for t in range(NT):
                    dve.wait_ge(ht_done, 4 * q + 2 * t + 2)
                    v.tensor_copy(hT[:, 4:8, t * P:(t + 1) * P], bank[ht_banks[q][t][1]][:, :].rearrange("p (k t) -> p k t", k=4)).then_inc(ht_dve, 1)

            def residual_tile(t, banks, gv, done, before):
                for n in range(2):
                    dve.wait_ge(done, before + n + 1)
                    cols = slice(512 * n, 512 * n + 512)
                    step(v.tensor_tensor(otmp, bank[banks[n]][:, :], gv[:, cols], ALU.mult))
                    ins = v.tensor_tensor(xs[:, t, cols], xs[:, t, cols], otmp, ALU.add)
                    if n == 1:
                        ins.then_inc(x_ready, 1)
                        tiles[0] += 1
                        dve.wait_ge(x_ready, tiles[0])
                    else:
                        step(ins)

            def mixer_end(l):
                q = 2 * l + 1
                gain_scale(q)
                dve.wait_ge(gv_act, q)
                for t in range(NT):
                    residual_tile(t, (4 + 2 * t, 5 + 2 * t), gv[0], outp_done, 4 * l + 2 * t)
                    norm_tile(q, t)

            def hybrid():
                for i, (a, n) in enumerate(((0, 512), (512, 512), (1024, 200))):
                    dve.wait_ge(proj_done, 2 * i + 2)
                    v.tensor_copy(patt[:, 1, a:a + n], bank[3 + 2 * i][:, 0:n]).then_inc(proj_dve, 1)
                dve.wait_ge(proj_act, 3)
                dve.wait_ge(proj_dve, 3)
                step(v.tensor_copy(vv[:, :, 0:HD], patt[:, :, 576:640]))
                step(v.tensor_scalar(wsc, patt[:, :, 1216:1224], float(HEADS) ** -0.5, None, ALU.mult))
                dve.wait_ge(sq_ready, 2)
                v.tensor_reduce(qss.rearrange("p (t g) -> p t g", t=NT), qsq, AX, ALU.add).then_inc(qss_ready, 1)
                dve.wait_ge(qstd_ready, 1)
                step(v.reciprocal(qrs, qrs))
                dve.wait_ge(param_in, 4 * 16)
                for t in range(NT):
                    qk = patt[:, t, 0:576].rearrange("p (g d) -> p g d", d=HD)
                    step(v.tensor_tensor(qk, qk, bc(qrs[:, 9 * t:9 * t + 9], HD), ALU.mult))
                    step(v.tensor_tensor(qk, qk, gam9[:, :, :], ALU.mult))
                for t in range(NT):
                    co = rope[:, t, 0, :].unsqueeze(1).to_broadcast([P, 9, HD // 2])
                    si = rope[:, t, 1, :].unsqueeze(1).to_broadcast([P, 9, HD // 2])
                    for g in range(2):
                        src = patt[:, t, 640 * g:640 * g + 576].rearrange("p (g c d) -> p g c d", c=2, d=HD // 2)
                        dst = Q2[:, t, 10 * g:10 * g + 9, :].rearrange("p g (c d) -> p g c d", c=2)
                        for o in range(2):
                            tm = RD[:, 256 + 288 * ((2 * g + o) % 3):544 + 288 * ((2 * g + o) % 3)].rearrange("p (g d) -> p g d", d=HD // 2)
                            step(v.tensor_tensor(tm, src[:, :, 1 - o, :], si, ALU.mult))
                            step(v.tensor_tensor(dst[:, :, o, :], src[:, :, o, :], co, ALU.mult))
                            step(v.tensor_tensor(dst[:, :, o, :], dst[:, :, o, :], tm, ALU.subtract if o == 0 else ALU.add))
                        ins = v.tensor_copy(Q2[:, t, 10 * g + 9, :], Q2[:, t, 10 * g + 8, :])
                        if g == 1:
                            ins.then_inc(q2_ready, 1)
                        else:
                            step(ins)
                for g in (1, 3, 5):
                    dve.wait_ge(qt_done, g + 1)
                    t, c = g // 3, g % 3
                    m = 4 if c < 2 else 2
                    v.tensor_copy(QT[:, 4 * c:4 * c + m, t * P:(t + 1) * P],
                                  bank[qt_banks[g]][:, 0:P * m].rearrange("p (c t) -> p c t", c=m)).then_inc(qt_dve, 1)
                r = 0
                for t in range(NT):
                    nk = P * (t + 1)
                    sc = score[:, 0:nk]
                    if t:
                        step(v.memset(score[:, 0:P], 0.0))
                    step(v.tensor_copy(score[:, t * P:nk], causal))
                    for b in range(4):
                        dve.wait_ge(relu_done, r + 1)
                        for i in range(2):
                            hd = 4 * (b // 2) + 2 * i + b % 2
                            ins = v.scalar_tensor_tensor(out=sc, in0=relu[r % 4][:, 256 * i:256 * i + nk],
                                                         scalar=wsc[:, t, hd:hd + 1], in1=sc, op0=ALU.mult, op1=ALU.add)
                            if i == 0:
                                step(ins)
                        ins.then_inc(relu_used, 1)
                        dve.wait_ge(relu_used, r + 1)
                        r += 1
                    for rd in range(TOPK // 8):
                        src = sc if rd == 0 else work[:, 0:nk]
                        step(v.max(out=top8, in_=src))
                        step(v.match_replace(out=work[:, 0:nk], in_to_replace=top8, in_values=src, imm_value=TAKEN))
                    step(v.tensor_scalar(work[:, 0:nk], work[:, 0:nk], 0.5 * TAKEN, None, ALU.is_lt))
                    step(v.tensor_scalar(sc, sc, 0.1 * MASKED, None, ALU.is_gt))
                    step(v.tensor_tensor(sc, sc, work[:, 0:nk], ALU.mult))
                    step(v.tensor_scalar(selb[:, t, 0:nk], sc, -MASKED, MASKED, ALU.mult, ALU.add))
                dve.wait_ge(proj_act, 5)
                for i in range(2):
                    dve.wait_ge(proj_done, 11 + i)
                    ins = v.tensor_tensor(cgs[:, 2 * i:2 * i + 2, :], cgs[:, 2 * i:2 * i + 2, :],
                                          bank[2 + i][:, :].rearrange("p (c t) -> p c t", c=2), ALU.mult)
                ins.then_inc(proj_dve, 1)
                dve.wait_ge(proj_dve, 4)
                dve.wait_ge(cwt_act, 1)
                dve.wait_ge(bg_act, 2)
                for ch in range(4):
                    w = [cwT[:, 4 * j + ch:4 * j + ch + 1] for j in range(3)]
                    z = cgs[:, ch, :]
                    o = ctmp[:, ch, :]
                    step(v.tensor_scalar(o, z, w[2], None, ALU.mult))
                    for j in (1, 0):
                        d = 2 - j
                        step(v.scalar_tensor_tensor(out=o[:, d:], in0=z[:, 0:SEQ - d], scalar=w[j], in1=o[:, d:],
                                                    op0=ALU.mult, op1=ALU.add))
                v.tensor_tensor(yT[:, 4:8, :], yT[:, 4:8, :], ctmp, ALU.mult).then_inc(yconv_ready, 1)
                for t in range(NT):
                    nk = P * (t + 1)
                    for b in range(4):
                        dve.wait_ge(logit_done, 4 * t + b + 1)
                        first = 4 * (b // 2) + b % 2
                        v.tensor_tensor(logits[t][:, first:first + 3:2, 0:nk],
                                        bank[logit_banks[t][b]][:, :].rearrange("p (i s) -> p i s", i=2)[:, :, 0:nk],
                                        mid(selb[:, t, 0:nk], 2), ALU.add).then_inc(logit_read, 1)
                    dve.wait_ge(logit_read, 4 * t + 4)
                    step(v.tensor_reduce(amax[t], logits[t][:, :, 0:nk], AX, ALU.max))
                    v.tensor_scalar(amax[t], amax[t], -(HD ** -0.5), None, ALU.mult).then_inc(max_ready, 1)
                ptn = 0
                for t in range(NT):
                    nk = P * (t + 1)
                    dve.wait_ge(exp_done, t + 1)
                    step(v.reciprocal(rsum, asum[t]))
                    v.tensor_tensor(logits[t][:, :, 0:nk], logits[t][:, :, 0:nk], bc(rsum, nk), ALU.mult).then_inc(probs_ready, 1)
                    for kt in range(t + 1):
                        dve.wait_ge(pt_done, 2 * ptn + 2)
                        v.tensor_copy(PT[:, kt, 4:8, :], bank[7][:, :].rearrange("p (h q) -> p h q", h=4)).then_inc(pt_dve, 1)
                        ptn += 1
                    if t == 0:
                        rows(2)

            def mlstm():
                rows(4)
                dve.wait_ge(proj_done, 14)
                step(v.tensor_tensor(gts, bank[4][:, 0:32].rearrange("p (t n) -> p t n", t=NT), mid(bgate, NT), ALU.add))
                v.tensor_scalar(lf, gts[:, :, 8:16], 0.0, None, ALU.min).then_inc(gates_ready, 1)
                dve.wait_ge(gates_ready, 1)
                v.memset(vx[:, :, :, VD:VD + 1], 1.0).then_inc(vone_ready, 1)
                dve.wait_ge(absexp_done, 1)
                v.tensor_tensor(lf, lf, g3, ALU.subtract).then_inc(logf_ready, 1)
                dve.wait_ge(cumf_done, 1)
                step(v.tensor_copy(cumf, bank[5][:, 0:16].rearrange("p (t n) -> p t n", t=NT)))
                v.tensor_tensor(asb, gts[:, :, 0:8], cumf, ALU.subtract).then_inc(a_ready, 1)
                dve.wait_ge(at_done, 1)
                step(v.tensor_copy(mrow[:, 0, :], bank[6][0:8, 0:SEQ]))
                v.tensor_tensor_scan(out=mrow[:, 1, :], data0=mrow[:, 0, :], data1=mrow[:, 0, :], initial=0.0, op0=ALU.max, op1=ALU.max).then_inc(m_ready, 1)
                dve.wait_ge(proj_done, 20)
                v.tensor_copy(vx[:, 1, 0:4, 0:VD], bank[7][:, :].rearrange("p (h v) -> p h v", h=4)).then_inc(proj_dve, 1)
                dve.wait_ge(at_done, 2)
                v.tensor_tensor(em, bank[6][:, 256:272].rearrange("p (t n) -> p t n", t=NT), cumf, ALU.add).then_inc(em_in, 1)
                dve.wait_ge(proj_done, 22)
                v.tensor_copy(vx[:, 1, 4:8, 0:VD], bank[3][:, :].rearrange("p (h v) -> p h v", h=4)).then_inc(proj_dve, 1)
                for b in range(4):
                    dve.wait_ge(mb_done, b + 1)
                    src = bank[b][:, :].rearrange("p (h t) -> p h t", h=2)
                    v.tensor_tensor(MB0[:, 2 * b:2 * b + 2, 0:P], src[:, :, 0:P], mid(maskT, 2), ALU.subtract).then_inc(mbc_dve, 1)
                    v.tensor_tensor(MB1[:, 2 * b:2 * b + 2, :], src[:, :, P:], mid(maskT, 2), ALU.subtract).then_inc(mbc_dve, 1)
                for hd in range(HEADS):
                    dve.wait_ge(st_done, hd + 1)
                    dve.wait_ge(w_done, 2 * hd + 2)
                    v.scalar_tensor_tensor(out=MB0[:, hd, :], in0=bank[st_banks[hd]][:, 0:256], scalar=HD ** -0.5, in1=MB0[:, hd, :],
                                           op0=ALU.mult, op1=ALU.mult).then_inc(pw_ready, 1)
                    v.scalar_tensor_tensor(out=MB1[:, hd, :], in0=bank[st_banks[hd]][:, 256:384], scalar=HD ** -0.5, in1=MB1[:, hd, :],
                                           op0=ALU.mult, op1=ALU.mult).then_inc(pw_ready, 1)
                dve.wait_ge(em_ready, 1)
                for t in range(NT):
                    for i, m in enumerate((3, 3, 2)):
                        dve.wait_ge(num_done, 3 * t + i + 1)
                        src = bank[num_banks[t][i]][:, 0:129 * m].rearrange("p (h v) -> p h v", h=m)
                        dn = den[:, t, 3 * i:3 * i + m]
                        dsum = src[:, :, VD:VD + 1].rearrange("p h o -> p (h o)")
                        step(v.tensor_scalar(dn, dsum, -1.0, None, ALU.mult))
                        step(v.tensor_tensor(dn, dn, dsum, ALU.max))
                        step(v.tensor_tensor(dn, dn, em[:, t, 3 * i:3 * i + m], ALU.max))
                        step(v.reciprocal(dn, dn))
                        ins = v.tensor_tensor(HN[:, t, 3 * i:3 * i + m, :], src[:, :, 0:VD], bc(dn, VD), ALU.mult)
                        if i == 2:
                            ins.then_inc(hn_ready, 1)
                    dve.wait_ge(hsq_done, t + 1)
                    ins = v.tensor_reduce(hss[:, t, :], hsq[:, t, :, :], AX, ALU.add)
                    if t:
                        ins.then_inc(hss_ready, 1)
                dve.wait_ge(hstd_done, 1)
                step(v.reciprocal(hss, hss))
                dve.wait_ge(gam_in, 16 * (gain[0] + 1))
                gain[0] += 1
                flats = [HN[:, t, :, :].rearrange("p h v -> p (h v)") for t in range(NT)]
                for t in range(NT):
                    step(v.tensor_tensor(HN[:, t, :, :], HN[:, t, :, :], bc(hss[:, t, :], VD), ALU.mult))
                    step(v.tensor_tensor(flats[t], flats[t], gam[:, :], ALU.mult))
                for t in range(NT):
                    flat = flats[t]
                    dve.wait_ge(proj_act, 12 + t)
                    v.tensor_tensor(flat, flat, ogs[:, t, :], ALU.mult).then_inc(y_ready, 1)
                dve.wait_ge(y_ready, 2)
                v.memset(small[:, 0:1], 0.0).then_inc(gam_free, 1)
                rows(5)
                for t in range(NT):
                    dve.wait_ge(yb_done, 2 * t + 2)
                    v.tensor_copy(yT[:, 4:8, t * P:(t + 1) * P], bank[5 + 2 * t][:, :].rearrange("p (c q) -> p c q", c=4)).then_inc(yt_dve, 1)

            def first_max(val, onehot, scratch, top, n):
                step(v.tensor_reduce(top, val, AX, ALU.max))
                step(v.tensor_tensor(scratch, val, bc(top, n), ALU.is_equal))
                step(v.tensor_tensor(scratch, scratch, mid(idxm[:, 0:n], NT), ALU.mult))
                step(v.tensor_reduce(mnx, scratch, AX, ALU.min))
                step(v.tensor_tensor(onehot, mid(idxm[:, 0:n], NT), bc(mnx, n), ALU.is_equal))

            def ffn(l):
                v.memset(zero, 0.0).then_inc(zero_ready, 1)
                v.memset(Y[:, 512:1024], 0.0).then_inc(y_dve[l], 1)
                v.memset(SC, 0.0).then_inc(scat_ready[l], 1)
                if l == 1:
                    rows(6)
                dve.wait_ge(rlog_done, l + 1)
                dve.wait_ge(rparam_in, 64 * (l + 1))
                step(v.tensor_tensor(LG, bank[5][:, 0:72].rearrange("p (t n) -> p t n", t=NT), mid(rb, NT), ALU.add))
                v.memset(small[:, 0:1], 0.0).then_inc(rparam_free, 1)
                first_max(LG[:, :, 0:NG], R2[:, :, 0:NG], R1[:, :, 0:NG], gmx, NG)
                v.tensor_tensor(GE, LG[:, :, 0:NG], bc(gmx, NG), ALU.subtract).then_inc(gexp_in, 1)
                group = R2[:, :, 0:NG]
                O14 = O1.rearrange("p t (g e) -> p t g e", g=NG)
                for t in range(NT):
                    step(v.tensor_tensor(O14[:, t, :, :], LG[:, t, NG:].rearrange("p (g e) -> p g e", g=NG), bc(group[:, t, :], EG), ALU.mult))
                step(v.tensor_scalar(R2[:, :, 8:8 + NG], group, -MASKED, MASKED, ALU.mult, ALU.add))
                for t in range(NT):
                    step(v.tensor_tensor(OS.rearrange("p t (g e) -> p t g e", g=NG)[:, t, :, :], O14[:, t, :, :], bc(R2[:, t, 8:8 + NG], EG), ALU.add))
                first_max(OS, O1, R1, v1, NE)
                step(v.scalar_tensor_tensor(out=OS, in0=O1, scalar=2 * MASKED, in1=OS, op0=ALU.mult, op1=ALU.add))
                first_max(OS, O2, R1, v2, NE)
                v.tensor_tensor(OS, O1, O2, ALU.add).then_inc(onehot_ready, 1)
                v.tensor_tensor(ex, v2, v1, ALU.subtract).then_inc(wexp_in, 1)
                dve.wait_ge(gexp_done, l + 1)
                step(v.tensor_reduce(gsm, GE, AX, ALU.add))
                step(v.reciprocal(pg, gsm))
                vl = vals.rearrange("p (r t) -> p r t", t=NT)
                dve.wait_ge(rank_done, l + 1)
                rank = bank[7][:, 0:64].rearrange("p (t n) -> p t n", t=NT)
                step(v.tensor_scalar(POSG, rank, BLK - 0.5, 1.0e6, ALU.is_gt, ALU.mult))
                step(v.tensor_tensor(POSG, POSG, rank, ALU.add))
                step(v.scalar_tensor_tensor(out=POSG, in0=mid(idxm, NT), scalar=float(BLK), in1=POSG, op0=ALU.mult, op1=ALU.add))
                for r, o in enumerate((O1, O2)):
                    step(v.tensor_tensor(R1, o, POSG, ALU.mult))
                    step(v.tensor_reduce(PG[:, 2 * r:2 * r + 2], R1, AX, ALU.add))
                step(v.tensor_scalar(PG, PG, 99.0 * BLK, None, ALU.add))

                def select_group(g):
                    v.tensor_tensor(SELGQ, mid(iota_grp, 4), bc(PG, GRP), ALU.is_equal).then_inc(group_step[l], 1)
                    dve.wait_ge(group_step[l], 2 * g + 1)
                    v.tensor_tensor(SELG, SELGQ[:, 0:2, :], SELGQ[:, 2:4, :], ALU.add).then_inc(group_sel[l], 1)
                    v.tensor_scalar(PG, PG, -float(GRP), None, ALU.add).then_inc(group_step[l], 1)

                select_group(0)
                step(v.tensor_tensor(CMP, bc(bank[7][:, 64:96], 7), mid(cst[:, C_THR:C_THR + 7], NE), ALU.is_gt))
                step(v.tensor_reduce(NBL, CMP, AX, ALU.add))
                step(v.tensor_scalar(NBL, NBL, 1.0, None, ALU.add))
                step(v.memset(BBF[:, 0:1], 0.0))
                step(v.tensor_tensor_scan(out=BBF[:, 1:NE + 1], data0=ones[:, 0:NE], data1=NBL, initial=0.0, op0=ALU.mult, op1=ALU.add))
                v.tensor_tensor(tab[:, :], BBF, iota_grp[:, 0:NE + 1], ALU.subtract).then_inc(table_ready, 1)
                step(v.tensor_scalar(POSM, rank, BLK - 0.5, float(BLK), ALU.is_lt, ALU.mult))
                step(v.tensor_tensor(POSM, POSM, mid(NBL, NT), ALU.mult))
                step(v.tensor_tensor(POSM, POSM, rank, ALU.add))
                step(v.scalar_tensor_tensor(out=POSM, in0=mid(BBF[:, 0:NE], NT), scalar=float(BLK), in1=POSM, op0=ALU.mult, op1=ALU.add))
                for r, o in enumerate((O1, O2)):
                    step(v.tensor_tensor(R1, o, POSM, ALU.mult))
                    step(v.tensor_reduce(vl[:, r, :], R1, AX, ALU.add))
                dve.wait_ge(wexp_done, l + 1)
                step(v.tensor_scalar(s1, ex, 1.0, None, ALU.add))
                step(v.reciprocal(s1, s1))
                step(v.tensor_tensor(vl[:, 2, :], s1, pg, ALU.mult))
                step(v.tensor_tensor(vl[:, 3, :], vl[:, 2, :], ex, ALU.mult))
                step(v.tensor_scalar(vals[:, 0:4], vals[:, 0:4], -float(BLK), None, ALU.add))
                step(v.tensor_copy(PR, vals[:, 0:4]))
                step(v.tensor_copy(VP, cst[:, C_PMOD:C_PMOD + 1]))
                v.tensor_tensor(DG, mid(ident, 8), bc(vals, P), ALU.mult).then_inc(diag_ready, 1)
                dve.wait_ge(diag_ready, l + 1)

                if l == 0:
                    rows(3)
                step(v.tensor_tensor(SELQ, mid(iota32, 4), bc(PR, BLK), ALU.is_equal))
                v.tensor_tensor(SEL, SELQ[:, 0:2, :], SELQ[:, 2:4, :], ALU.add).then_inc(next_sel[l], 1)

                def expert_block(n, group=None):
                    own = STEPS * n
                    dve.wait_ge(up_done[l], n + 1)
                    v.tensor_copy(HU, bank[6][:, :]).then_inc(hu_ready[l], 1)
                    v.tensor_scalar(PR, PR, -float(BLK), None, ALU.add).then_inc(block_step[l], 1)
                    dve.wait_ge(block_step[l], own + 1)
                    v.tensor_tensor(SELQ, mid(iota32, 4), bc(PR, BLK), ALU.is_equal).then_inc(block_step[l], 1)
                    dve.wait_ge(block_step[l], own + 2)
                    v.tensor_tensor(SEL, SELQ[:, 0:2, :], SELQ[:, 2:4, :], ALU.add).then_inc(next_sel[l], 1)
                    dve.wait_ge(silu_ready[l], n + 1)
                    gate = bank[7][:, 0:P].rearrange("p (f s) -> p f s", f=FC)
                    up = bank[7][:, P:2 * P].rearrange("p (f s) -> p f s", f=FC)
                    v.tensor_scalar(SIL, SIL, 1.0, None, ALU.add).then_inc(block_step[l], 1)
                    dve.wait_ge(block_step[l], own + 3)
                    v.reciprocal(SIL, SIL).then_inc(block_step[l], 1)
                    dve.wait_ge(block_step[l], own + 4)
                    v.tensor_tensor(SIL, gate, SIL, ALU.mult).then_inc(block_step[l], 1)
                    dve.wait_ge(block_step[l], own + 5)
                    v.tensor_tensor(HID, up, SIL, ALU.mult).then_inc(hid_ready[l], 1)
                    dve.wait_ge(down_done[l], 2 * n + 1)
                    v.scalar_tensor_tensor(out=SC, in0=posrow[:, 0, :], scalar=VP, in1=wrow[:, 0, :], op0=ALU.is_equal, op1=ALU.mult).then_inc(block_step[l], 1)
                    v.scalar_tensor_tensor(out=SCT, in0=posrow[:, 1, :], scalar=VP, in1=wrow[:, 1, :], op0=ALU.is_equal, op1=ALU.mult).then_inc(block_step[l], 1)
                    dve.wait_ge(down_done[l], 2 * n + 2)
                    v.tensor_copy(Y[:, 512:1024], bank[6][:, :]).then_inc(y_dve[l], 1)
                    dve.wait_ge(block_step[l], own + 7)
                    v.tensor_tensor(SC, SC, SCT, ALU.add).then_inc(scat_ready[l], 1)
                    v.tensor_scalar(VP, VP, float(BLK), None, ALU.add).then_inc(block_step[l], 1)
                    if group is not None:
                        select_group(group)

                def expert(turn, u, more):
                    e = turn * UNROLL + u
                    x0 = dve.value_load(tab[0:1, bass.ds(e, 1)], min_val=0, max_val=EXTRA)
                    x1 = dve.value_load(tab[0:1, bass.ds(e + 1, 1)], min_val=0, max_val=EXTRA)
                    with dve.If(x0 < x1):
                        with dve.Fori(x0, x1) as x:
                            expert_block(x + e)
                    expert_block(x1 + e, turn + 1 if more and u == 0 else None)

                dve.wait_ge(rows_copied, l + 1)
                dve.wait_ge(table_ready, l + 1)
                with dve.Fori(0, NE // UNROLL) as turn:
                    for u in range(UNROLL):
                        expert(turn, u, True)
                for u in range(NE % UNROLL):
                    expert(NE // UNROLL, u, False)
                if l + 1 < DEPTH:
                    gain_scale(2 * l + 2)
                dve.wait_ge(gv_act, 2 * l + 2)
                for t in range(NT):
                    residual_tile(t, (2 * t, 2 * t + 1), gv[1], acc_done, 4 * l + 2 * t)
                if l + 1 < DEPTH:
                    for t in range(NT):
                        norm_tile(2 * l + 2, t)

            v.memset(eps, EPS).then_inc(fill_ready, 1)
            v.memset(cz[:, :], 0.0).then_inc(fill_ready, 1)
            dve.wait_ge(const_in, 16)
            rows(1)
            gain_scale(0)
            dve.wait_ge(x_in, 16 * NT)
            for t in range(NT):
                norm_tile(0, t)
            for l in range(DEPTH):
                copy_ht(2 * l)
                (hybrid, mlstm)[l]()
                mixer_end(l)
                copy_ht(2 * l + 1)
                ffn(l)



_INS = ['x', 'c', 'ada_w', 'ada_b', 'norm_mix', 'norm_ffn', 'hy_w_in', 'hy_q_norm', 'hy_k_norm', 'hy_conv_w', 'hy_w_out',
        'ml_w_in', 'ml_b_gates', 'ml_out_norm', 'ml_w_out', 'moe_w_group', 'moe_b_group', 'moe_w_expert', 'moe_b_expert',
        'moe_w_gate', 'moe_w_up', 'moe_w_down']


def kernel(**inputs):
    import numpy as _np
    import concourse.bacc as _bacc
    from concourse import mybir as _mybir
    from concourse.bass_utils import run_bass_kernel_spmd as _run

    nc = _bacc.Bacc("TRN2", target_bir_lowering=False, num_devices=1, dynamic_dma_scratch_size=2048)
    arrays, args = {}, []
    for name in _INS + ["consts"]:
        a = constant_table() if name == "consts" else _np.ascontiguousarray(inputs[name])
        arrays[f"in_{name}"] = a
        args.append(nc.dram_tensor(f"in_{name}", a.shape, _mybir.dt.from_np(a.dtype), kind="ExternalInput").ap())
    args.append(nc.dram_tensor("out_x", inputs["x"].shape, _mybir.dt.float32, kind="ExternalOutput").ap())
    decoder_kernel(nc, *args)
    r = _run(nc, [arrays], core_ids=[0])
    return r.results[0]["out_x"]
```
